# Optimizing a Trainium2 kernel written in Bass

```python
import jax, jax.numpy as jnp
from jax import lax
import numpy as np
import math

D_MODEL = 1024
BATCH = 1
SEQ = 256
DEPTH = 2

D_FF = 2816
EPS = 1e-6
NSA_HEADS = 8
NSA_KV_GROUPS = 2
HEAD_DIM = 64
NSA_WIDTH = NSA_HEADS * HEAD_DIM
KV_WIDTH = NSA_KV_GROUPS * HEAD_DIM
CMP_BLOCK = 32
CMP_STRIDE = 16
CMP_HIDDEN = 128
SLC_BLOCK = 64
RATIO = SLC_BLOCK // CMP_STRIDE
SLC_TOP_N = 16
WINDOW = 512
Q_BLOCK = 128
FORCE_BONUS = 1e4
CONV_WIDTH = 512
CONV_K = 3
IN_SIZES = (NSA_WIDTH, 3 * NSA_HEADS, KV_WIDTH, KV_WIDTH, KV_WIDTH, KV_WIDTH,
            KV_WIDTH, KV_WIDTH, CONV_WIDTH, CONV_WIDTH, CONV_WIDTH)
IN_COLS = sum(IN_SIZES)
IN_SPLITS = tuple(int(s) for s in np.cumsum(IN_SIZES)[:-1])
MIX_OUT = NSA_WIDTH + CONV_WIDTH
RWKV_HEAD = 64
RWKV_HEADS = D_MODEL // RWKV_HEAD
DECAY_LORA = 64
AAA_LORA = 64
GATE_LORA = 128
LNX_EPS = 64e-5


def rmsnorm(x, g):
    xf = x.astype(jnp.float32)
    y = xf * lax.rsqrt(jnp.mean(xf * xf, -1, keepdims=True) + EPS)
    return (y * g.astype(jnp.float32)).astype(x.dtype)

def macaron_half_ffn(x, pre_g, post_g, w_gate, w_up, w_down):
    h = rmsnorm(x, pre_g)
    h = (jax.nn.silu(h @ w_gate) * (h @ w_up)) @ w_down
    return x + 0.5 * rmsnorm(h, post_g)

def alibi_slopes(n):
    return 2.0 ** (-8.0 * jnp.arange(1, n + 1, dtype=jnp.float32) / n)

def masked_softmax(s, mask):
    s = jnp.where(mask, s.astype(jnp.float32), -jnp.inf)
    m = jnp.max(s, -1, keepdims=True)
    m = jnp.where(jnp.isfinite(m), m, 0.0)
    p = jnp.exp(s - m)
    return p / jnp.maximum(jnp.sum(p, -1, keepdims=True), 1e-30)

def compress_blocks(kv, pe, w1, w2):
    B, S, G, Dh = kv.shape
    halves = kv.reshape(B, S // CMP_STRIDE, CMP_STRIDE, G, Dh)
    blocks = jnp.concatenate([halves[:, :-1], halves[:, 1:]], axis=2)
    blocks = blocks + pe[None, None, :, None, :]
    nc = blocks.shape[1]
    flat = blocks.transpose(0, 1, 3, 2, 4).reshape(B, nc, G, CMP_BLOCK * Dh)
    return jax.nn.gelu(flat @ w1) @ w2

def nsa_attention(q, gates, kc, vc, k_slc, v_slc, k_win, v_win):
    B, S, H, Dh = q.shape
    G = kc.shape[2]
    R = H // G
    n_cmp = kc.shape[1]
    n_slc = S // SLC_BLOCK
    top_n = min(SLC_TOP_N, n_slc)
    slopes = alibi_slopes(H).reshape(G, R)
    cmp_end = jnp.arange(n_cmp) * CMP_STRIDE + (CMP_BLOCK - 1)
    qg = q.reshape(B, S, G, R, Dh) * (Dh ** -0.5)
    gg = gates.reshape(B, S, G, R, 3)
    kb = k_slc.reshape(B, n_slc, SLC_BLOCK, G, Dh).transpose(0, 3, 1, 2, 4)
    vb = v_slc.reshape(B, n_slc, SLC_BLOCK, G, Dh).transpose(0, 3, 1, 2, 4)
    gather = jax.vmap(jax.vmap(lambda blocks, ix: blocks[ix]))
    kw = jnp.pad(k_win, ((0, 0), (WINDOW, 0), (0, 0), (0, 0)))
    vw = jnp.pad(v_win, ((0, 0), (WINDOW, 0), (0, 0), (0, 0)))
    j = jnp.arange(n_slc)
    offs = jnp.arange(SLC_BLOCK)
    woffs = jnp.arange(Q_BLOCK + WINDOW) - WINDOW

    def query_block(qi):
        q0 = qi * Q_BLOCK
        t = q0 + jnp.arange(Q_BLOCK)
        qb = lax.dynamic_slice_in_dim(qg, q0, Q_BLOCK, axis=1)
        gb = lax.dynamic_slice_in_dim(gg, q0, Q_BLOCK, axis=1)
        d_cmp = t[:, None] - cmp_end[None, :]
        s = jnp.einsum("btgrd,bngd->bgrtn", qb, kc) - slopes[:, :, None, None] * d_cmp
        p_cmp = masked_softmax(s, d_cmp >= 0)
        o_cmp = jnp.einsum("bgrtn,bngd->btgrd", p_cmp.astype(vc.dtype), vc)
        imp = jnp.pad(p_cmp.sum(2), ((0, 0), (0, 0), (0, 0), (0, 1)))
        imp = imp.reshape(B, G, Q_BLOCK, n_slc, RATIO)
        last = imp[..., RATIO - 1]
        prev = jnp.pad(last, ((0, 0), (0, 0), (0, 0), (1, 0)))[..., :-1]
        imp = imp.sum(-1) - 0.5 * last + 0.5 * prev
        blk_t = (t // SLC_BLOCK)[:, None]
        forced = (j == 0) | (j == blk_t) | (j == blk_t - 1)
        imp = jnp.where(forced, imp + FORCE_BONUS, imp)
        imp = jnp.where(j <= blk_t, imp, -jnp.inf)
        _, idx = lax.top_k(imp, top_n)
        ks = gather(kb, idx)
        vs = gather(vb, idx)
        d_slc = t[:, None, None] - (idx[..., None] * SLC_BLOCK + offs)
        s = jnp.einsum("btgrd,bgtnld->bgrtnl", qb, ks) - slopes[:, :, None, None, None] * d_slc[:, :, None]
        mask = jnp.broadcast_to((d_slc >= 0)[:, :, None], s.shape)
        p = masked_softmax(s.reshape(B, G, R, Q_BLOCK, -1), mask.reshape(B, G, R, Q_BLOCK, -1))
        o_slc = jnp.einsum("bgrtm,bgtmd->btgrd", p.astype(vs.dtype),
                           vs.reshape(B, G, Q_BLOCK, top_n * SLC_BLOCK, Dh))
        kwb = lax.dynamic_slice_in_dim(kw, q0, Q_BLOCK + WINDOW, axis=1)
        vwb = lax.dynamic_slice_in_dim(vw, q0, Q_BLOCK + WINDOW, axis=1)
        kpos = q0 + woffs
        d_win = t[:, None] - kpos[None, :]
        mask = (d_win >= 0) & (d_win < WINDOW) & (kpos[None, :] >= 0)
        s = jnp.einsum("btgrd,bsgd->bgrts", qb, kwb) - slopes[:, :, None, None] * d_win
        p = masked_softmax(s, mask)
        o_win = jnp.einsum("bgrts,bsgd->btgrd", p.astype(vwb.dtype), vwb)
        return gb[..., 0:1] * o_cmp + gb[..., 1:2] * o_slc + gb[..., 2:3] * o_win

    out = lax.map(query_block, jnp.arange(S // Q_BLOCK))
    return out.transpose(1, 0, 2, 3, 4, 5).reshape(B, S, H * Dh)

def short_conv(b_gate, c_gate, u, conv_w, conv_b):
    z = c_gate * u
    y = lax.conv_general_dilated(z, conv_w[:, None, :].astype(z.dtype), window_strides=(1,),
                                 padding=[(CONV_K - 1, 0)],
                                 dimension_numbers=("NWC", "WIO", "NWC"),
                                 feature_group_count=z.shape[-1])
    return b_gate * (y + conv_b)

def nsa_shortconv_mixer(h, w_in, cmp_pe_k, cmp_w1_k, cmp_w2_k, cmp_pe_v, cmp_w1_v, cmp_w2_v,
                        conv_w, conv_b, w_out):
    B, S, _ = h.shape
    q, g, kc, vc, ks, vs, kw, vw, cb, cc, cu = jnp.split(h @ w_in, IN_SPLITS, axis=-1)
    kv = lambda t: t.reshape(B, S, NSA_KV_GROUPS, HEAD_DIM)
    kc = compress_blocks(kv(kc), cmp_pe_k, cmp_w1_k, cmp_w2_k)
    vc = compress_blocks(kv(vc), cmp_pe_v, cmp_w1_v, cmp_w2_v)
    o_nsa = nsa_attention(q.reshape(B, S, NSA_HEADS, HEAD_DIM),
                          jax.nn.sigmoid(g).reshape(B, S, NSA_HEADS, 3),
                          kc, vc, kv(ks), kv(vs), kv(kw), kv(vw))
    o_conv = short_conv(cb, cc, cu, conv_w, conv_b)
    return jnp.concatenate([o_nsa.astype(h.dtype), o_conv], axis=-1) @ w_out

def rwkv7_mixer(h, mu, w_r, w_k, w_v, w_o, w0, w_dec1, w_dec2, a0, w_a1, w_a2,
                w_g1, w_g2, k_k, k_a, r_k, lnx_g, lnx_b):
    B, S, D = h.shape
    H, N = RWKV_HEADS, RWKV_HEAD
    xx = jnp.pad(h, ((0, 0), (1, 0), (0, 0)))[:, :-1] - h
    xr, xw, xk, xv, xa, xg = [h + xx * mu[i] for i in range(6)]
    r = xr @ w_r
    k = xk @ w_k
    v = xv @ w_v
    w_log = -jax.nn.softplus(-(w0 + jnp.tanh(xw @ w_dec1) @ w_dec2)) - 0.5
    a = jax.nn.sigmoid(a0 + (xa @ w_a1) @ w_a2)
    g = jax.nn.sigmoid(xg @ w_g1) @ w_g2
    kk = (k * k_k).reshape(B, S, H, N).astype(jnp.float32)
    kk = kk * lax.rsqrt(jnp.maximum(jnp.sum(kk * kk, -1, keepdims=True), 1e-12))
    k = k * (1.0 + (a - 1.0) * k_a)
    decay = jnp.exp(-jnp.exp(w_log.astype(jnp.float32)))
    heads = lambda t: t.reshape(B, S, H, N).astype(jnp.float32).transpose(1, 0, 2, 3)
    xs = (heads(r), heads(decay), heads(k), heads(v), kk.transpose(1, 0, 2, 3), heads(a))

    def step(state, inp):
        r_t, w_t, k_t, v_t, kk_t, a_t = inp
        sa = jnp.einsum("bhij,bhj->bhi", state, -kk_t)
        state = (state * w_t[:, :, None, :] + sa[..., None] * (kk_t * a_t)[:, :, None, :]
                 + v_t[..., None] * k_t[:, :, None, :])
        return state, jnp.einsum("bhij,bhj->bhi", state, r_t)

    state0 = jnp.zeros((B, H, N, N), jnp.float32)
    _, y = lax.scan(step, state0, xs)
    y = y.transpose(1, 0, 2, 3)
    mean = jnp.mean(y, -1, keepdims=True)
    var = jnp.mean(jnp.square(y - mean), -1, keepdims=True)
    y = ((y - mean) * lax.rsqrt(var + LNX_EPS)).reshape(B, S, D) * lnx_g + lnx_b
    rh, kh, vh = (t.reshape(B, S, H, N).astype(jnp.float32) for t in (r, k, v))
    bonus = (jnp.sum(rh * kh * r_k, -1, keepdims=True) * vh).reshape(B, S, D)
    return ((y + bonus).astype(h.dtype) * g) @ w_o

def first_inputs(seed: int = 0) -> dict:
    key = jax.random.key(seed)
    keys = iter(jax.random.split(key, 80))

    def nrm(shape, scale):
        return jax.random.normal(next(keys), shape, jnp.float32) * scale

    def unif(shape, lo, hi):
        return jax.random.uniform(next(keys), shape, jnp.float32, lo, hi)

    def gain(n=D_MODEL):
        return 1.0 + nrm((n,), 0.05)

    inp = {"x": nrm((BATCH, SEQ, D_MODEL), 1.0)}

    def add_ffn(p):
        inp[p + "_pre_g"] = gain()
        inp[p + "_post_g"] = gain()
        inp[p + "_w_gate"] = nrm((D_MODEL, D_FF), D_MODEL ** -0.5)
        inp[p + "_w_up"] = nrm((D_MODEL, D_FF), D_MODEL ** -0.5)
        inp[p + "_w_down"] = nrm((D_FF, D_MODEL), D_FF ** -0.5)

    add_ffn("l0_ffn1")
    inp["l0_mix_pre_g"] = gain()
    inp["l0_mix_post_g"] = gain()
    inp["l0_w_in"] = nrm((D_MODEL, IN_COLS), D_MODEL ** -0.5)
    for kvn in ("k", "v"):
        inp["l0_cmp_pe_" + kvn] = nrm((CMP_BLOCK, HEAD_DIM), 0.1)
        inp["l0_cmp_w1_" + kvn] = nrm((CMP_BLOCK * HEAD_DIM, CMP_HIDDEN), (CMP_BLOCK * HEAD_DIM) ** -0.5)
        inp["l0_cmp_w2_" + kvn] = nrm((CMP_HIDDEN, HEAD_DIM), CMP_HIDDEN ** -0.5)
    inp["l0_conv_w"] = nrm((CONV_K, CONV_WIDTH), 0.5)
    inp["l0_conv_b"] = nrm((CONV_WIDTH,), 0.02)
    inp["l0_w_out"] = nrm((MIX_OUT, D_MODEL), MIX_OUT ** -0.5)
    add_ffn("l0_ffn2")
    add_ffn("l1_ffn1")
    inp["l1_mix_pre_g"] = gain()
    inp["l1_mix_post_g"] = gain()
    inp["l1_mu"] = unif((6, D_MODEL), 0.0, 1.0)
    inp["l1_w_r"] = nrm((D_MODEL, D_MODEL), D_MODEL ** -0.5)
    inp["l1_w_k"] = nrm((D_MODEL, D_MODEL), D_MODEL ** -0.5)
    inp["l1_w_v"] = nrm((D_MODEL, D_MODEL), D_MODEL ** -0.5)
    inp["l1_w_o"] = nrm((D_MODEL, D_MODEL), D_MODEL ** -0.5)
    inp["l1_w0"] = unif((D_MODEL,), -6.0, 1.0)
    inp["l1_w_dec1"] = nrm((D_MODEL, DECAY_LORA), D_MODEL ** -0.5)
    inp["l1_w_dec2"] = nrm((DECAY_LORA, D_MODEL), 0.1 * DECAY_LORA ** -0.5)
    inp["l1_a0"] = nrm((D_MODEL,), 0.5)
    inp["l1_w_a1"] = nrm((D_MODEL, AAA_LORA), D_MODEL ** -0.5)
    inp["l1_w_a2"] = nrm((AAA_LORA, D_MODEL), 0.5 * AAA_LORA ** -0.5)
    inp["l1_w_g1"] = nrm((D_MODEL, GATE_LORA), D_MODEL ** -0.5)
    inp["l1_w_g2"] = nrm((GATE_LORA, D_MODEL), GATE_LORA ** -0.5)
    inp["l1_k_k"] = 0.85 + nrm((D_MODEL,), 0.05)
    inp["l1_k_a"] = 1.0 + nrm((D_MODEL,), 0.05)
    inp["l1_r_k"] = nrm((RWKV_HEADS, RWKV_HEAD), 0.1)
    inp["l1_lnx_g"] = gain()
    inp["l1_lnx_b"] = nrm((D_MODEL,), 0.02)
    add_ffn("l1_ffn2")
    return inp

def first_block(x,
              l0_ffn1_pre_g, l0_ffn1_post_g, l0_ffn1_w_gate, l0_ffn1_w_up, l0_ffn1_w_down,
              l0_mix_pre_g, l0_mix_post_g, l0_w_in,
              l0_cmp_pe_k, l0_cmp_w1_k, l0_cmp_w2_k, l0_cmp_pe_v, l0_cmp_w1_v, l0_cmp_w2_v,
              l0_conv_w, l0_conv_b, l0_w_out,
              l0_ffn2_pre_g, l0_ffn2_post_g, l0_ffn2_w_gate, l0_ffn2_w_up, l0_ffn2_w_down,
              l1_ffn1_pre_g, l1_ffn1_post_g, l1_ffn1_w_gate, l1_ffn1_w_up, l1_ffn1_w_down,
              l1_mix_pre_g, l1_mix_post_g, l1_mu, l1_w_r, l1_w_k, l1_w_v, l1_w_o,
              l1_w0, l1_w_dec1, l1_w_dec2, l1_a0, l1_w_a1, l1_w_a2, l1_w_g1, l1_w_g2,
              l1_k_k, l1_k_a, l1_r_k, l1_lnx_g, l1_lnx_b,
              l1_ffn2_pre_g, l1_ffn2_post_g, l1_ffn2_w_gate, l1_ffn2_w_up, l1_ffn2_w_down):
    layers = [
        dict(ffn1=(l0_ffn1_pre_g, l0_ffn1_post_g, l0_ffn1_w_gate, l0_ffn1_w_up, l0_ffn1_w_down),
             norms=(l0_mix_pre_g, l0_mix_post_g),
             mixer=nsa_shortconv_mixer,
             mix=(l0_w_in, l0_cmp_pe_k, l0_cmp_w1_k, l0_cmp_w2_k, l0_cmp_pe_v, l0_cmp_w1_v,
                  l0_cmp_w2_v, l0_conv_w, l0_conv_b, l0_w_out),
             ffn2=(l0_ffn2_pre_g, l0_ffn2_post_g, l0_ffn2_w_gate, l0_ffn2_w_up, l0_ffn2_w_down)),
        dict(ffn1=(l1_ffn1_pre_g, l1_ffn1_post_g, l1_ffn1_w_gate, l1_ffn1_w_up, l1_ffn1_w_down),
             norms=(l1_mix_pre_g, l1_mix_post_g),
             mixer=rwkv7_mixer,
             mix=(l1_mu, l1_w_r, l1_w_k, l1_w_v, l1_w_o, l1_w0, l1_w_dec1, l1_w_dec2, l1_a0,
                  l1_w_a1, l1_w_a2, l1_w_g1, l1_w_g2, l1_k_k, l1_k_a, l1_r_k, l1_lnx_g, l1_lnx_b),
             ffn2=(l1_ffn2_pre_g, l1_ffn2_post_g, l1_ffn2_w_gate, l1_ffn2_w_up, l1_ffn2_w_down)),
    ]
    for i in range(DEPTH):
        p = layers[i]
        x = macaron_half_ffn(x, *p["ffn1"])
        pre_g, post_g = p["norms"]
        x = x + rmsnorm(p["mixer"](rmsnorm(x, pre_g), *p["mix"]), post_g)
        x = macaron_half_ffn(x, *p["ffn2"])
    return x


DEPTH_2 = 1

MEM_LEN = 256
SSD_HEADS = 16
SSD_HEAD_DIM = 64
SSD_INNER = SSD_HEADS * SSD_HEAD_DIM
SSD_GROUPS = 4
SSD_STATE = 128
SSD_CONV = 4
SSD_CHUNK = 128
SSD_XBC = SSD_INNER + 2 * SSD_GROUPS * SSD_STATE
ATT_HEADS = 16
ATT_HEAD_DIM = 64
ATT_WIDTH = ATT_HEADS * ATT_HEAD_DIM
KV_RANK = 256
IDX_HEADS = 16
IDX_DIM = 64
TOPK_MAX = 256
MEM_HEADS = 4
MEM_HEAD_DIM = D_MODEL // MEM_HEADS
ALPHA = (2.0 * DEPTH_2) ** 0.25
BETA = (8.0 * DEPTH_2) ** -0.25
LN_EPS = 1e-5
RMS_EPS = 1e-6
IN_SPLITS_2 = (D_MODEL, D_MODEL, SSD_INNER, SSD_XBC, SSD_HEADS,
             ATT_WIDTH, KV_RANK, IDX_HEADS * IDX_DIM, IDX_DIM, IDX_HEADS)
D_IN = 2 * D_MODEL + SSD_INNER + SSD_XBC + SSD_HEADS + ATT_WIDTH + KV_RANK + IDX_HEADS * IDX_DIM + IDX_DIM + IDX_HEADS


def layer_norm(x, g, b):
    xf = x.astype(jnp.float32)
    mu = jnp.mean(xf, -1, keepdims=True)
    var = jnp.mean(jnp.square(xf - mu), -1, keepdims=True)
    return ((xf - mu) * lax.rsqrt(var + LN_EPS) * g + b).astype(x.dtype)

def rms_norm(x, g):
    xf = x.astype(jnp.float32)
    y = xf * lax.rsqrt(jnp.mean(jnp.square(xf), -1, keepdims=True) + RMS_EPS)
    return (y * g).astype(x.dtype)

def swiglu_ffn(x, w_in, w_out):
    gate, up = jnp.split(x @ w_in, 2, axis=-1)
    return (jax.nn.silu(gate) * up) @ w_out

def split_cols(h, sizes):
    out, off = [], 0
    for s in sizes:
        out.append(h[..., off:off + s])
        off += s
    return out

def causal_dwconv(u, w, b):
    width, ch = w.shape
    out = lax.conv_general_dilated(u, w[:, None, :], window_strides=(1,),
                                   padding=[(width - 1, 0)],
                                   dimension_numbers=('NWC', 'WIO', 'NWC'),
                                   feature_group_count=ch)
    return out + b

def segsum(a):
    l = a.shape[-1]
    cs = jnp.cumsum(a, axis=-1)
    diff = cs[..., :, None] - cs[..., None, :]
    mask = jnp.tril(jnp.ones((l, l), dtype=bool))
    return jnp.where(mask, diff, -jnp.inf)

def ssd_chunked_scan(x, dt, a_head, bmat, cmat):
    bsz, seqlen, n_heads, p = x.shape
    g, n = bmat.shape[2], bmat.shape[3]
    r = n_heads // g
    l = SSD_CHUNK
    c = seqlen // l
    x = x.astype(jnp.float32).reshape(bsz, c, l, g, r, p)
    dt = dt.reshape(bsz, c, l, g, r)
    bmat = bmat.astype(jnp.float32).reshape(bsz, c, l, g, n)
    cmat = cmat.astype(jnp.float32).reshape(bsz, c, l, g, n)
    a = (dt * a_head.reshape(g, r)).transpose(0, 3, 4, 1, 2)
    a_cs = jnp.cumsum(a, axis=-1)
    xdt = x * dt[..., None]
    decay_in = jnp.exp(segsum(a))
    cb = jnp.einsum('bclgn,bcsgn->bcgls', cmat, bmat)
    y_diag = jnp.einsum('bcgls,bgrcls,bcsgrp->bclgrp', cb, decay_in, xdt)
    decay_to_end = jnp.exp(a_cs[..., -1:] - a_cs)
    chunk_states = jnp.einsum('bclgn,bgrcl,bclgrp->bcgrpn', bmat, decay_to_end, xdt)
    chunk_decay = jnp.exp(a_cs[..., -1])

    def step(h, inp):
        s_c, d_c = inp
        return d_c[..., None, None] * h + s_c, h

    h0 = jnp.zeros((bsz, g, r, p, n), jnp.float32)
    _, prev = lax.scan(step, h0, (jnp.moveaxis(chunk_states, 1, 0),
                                  jnp.moveaxis(chunk_decay, -1, 0)))
    prev = jnp.moveaxis(prev, 0, 1)
    y_off = jnp.einsum('bclgn,bcgrpn,bgrcl->bclgrp', cmat, prev, jnp.exp(a_cs))
    return (y_diag + y_off).reshape(bsz, seqlen, n_heads, p)

def ssd_branch(z, xbc, dt_raw, conv_w, conv_b, dt_bias, a_log, d_skip, norm_w):
    bsz, seqlen, _ = z.shape
    xbc = jax.nn.silu(causal_dwconv(xbc, conv_w, conv_b))
    gn = SSD_GROUPS * SSD_STATE
    xs, bm, cm = split_cols(xbc, (SSD_INNER, gn, gn))
    xh = xs.reshape(bsz, seqlen, SSD_HEADS, SSD_HEAD_DIM)
    dt = jax.nn.softplus(dt_raw.astype(jnp.float32) + dt_bias)
    a_head = -jnp.exp(a_log.astype(jnp.float32))
    y = ssd_chunked_scan(xh, dt, a_head,
                         bm.reshape(bsz, seqlen, SSD_GROUPS, SSD_STATE),
                         cm.reshape(bsz, seqlen, SSD_GROUPS, SSD_STATE))
    y = y + d_skip[None, None, :, None] * xh.astype(jnp.float32)
    y = y.reshape(bsz, seqlen, SSD_INNER) * jax.nn.silu(z.astype(jnp.float32))
    yg = y.reshape(bsz, seqlen, SSD_GROUPS, SSD_INNER // SSD_GROUPS)
    yg = yg * lax.rsqrt(jnp.mean(jnp.square(yg), -1, keepdims=True) + RMS_EPS)
    return (yg.reshape(bsz, seqlen, SSD_INNER) * norm_w).astype(z.dtype)

def dsa_branch(q, c_kv, q_idx, k_idx, w_idx, kv_norm_w, w_uk, w_uv):
    bsz, seqlen, _ = q.shape
    topk = min(TOPK_MAX, seqlen // 4)
    n_blocks = seqlen // Q_BLOCK
    q = q.reshape(bsz, seqlen, ATT_HEADS, ATT_HEAD_DIM)
    q_lat = jnp.einsum('bthd,hdr->bthr', q, w_uk) * (ATT_HEAD_DIM ** -0.5)
    c_kv = rms_norm(c_kv, kv_norm_w)
    q_idx = q_idx.reshape(bsz, seqlen, IDX_HEADS, IDX_DIM)
    w_idx = w_idx * (IDX_HEADS ** -0.5)
    slopes = 2.0 ** (-8.0 * jnp.arange(1, ATT_HEADS + 1, dtype=jnp.float32) / ATT_HEADS)
    key_pos = jnp.arange(seqlen, dtype=jnp.int32)

    def to_blocks(a):
        return a.reshape(bsz, n_blocks, Q_BLOCK, *a.shape[2:]).swapaxes(0, 1)

    t_blocks = key_pos.reshape(n_blocks, Q_BLOCK)

    def block(args):
        ql, qi, wi, t = args
        logits = jax.nn.relu(jnp.einsum('bqhd,bsd->bqhs', qi, k_idx))
        score = jnp.einsum('bqhs,bqh->bqs', logits, wi).astype(jnp.float32)
        causal = key_pos[None, :] <= t[:, None]
        score = jnp.where(causal[None], score, -jnp.inf)
        _, idx = lax.top_k(score, topk)
        sel = jax.vmap(lambda c, i: c[i])(c_kv, idx)
        s = jnp.einsum('bqhr,bqkr->bqhk', ql, sel).astype(jnp.float32)
        dist = (t[None, :, None] - idx).astype(jnp.float32)
        s = s - slopes[None, None, :, None] * dist[:, :, None, :]
        valid = idx <= t[None, :, None]
        s = jnp.where(valid[:, :, None, :], s, -jnp.inf)
        p = jax.nn.softmax(s, axis=-1).astype(sel.dtype)
        return jnp.einsum('bqhk,bqkr->bqhr', p, sel)

    o = lax.map(block, (to_blocks(q_lat), to_blocks(q_idx), to_blocks(w_idx), t_blocks))
    o = o.swapaxes(0, 1).reshape(bsz, seqlen, ATT_HEADS, KV_RANK)
    return jnp.einsum('bthr,hrd->bthd', o, w_uv).reshape(bsz, seqlen, ATT_WIDTH)

def memory_xattn(x, mem, w_mq, w_mkv, w_mo):
    bsz, seqlen, _ = x.shape
    q = (x @ w_mq).reshape(bsz, seqlen, MEM_HEADS, MEM_HEAD_DIM)
    k, v = jnp.split(mem @ w_mkv, 2, axis=-1)
    k = k.reshape(bsz, -1, MEM_HEADS, MEM_HEAD_DIM)
    v = v.reshape(bsz, -1, MEM_HEADS, MEM_HEAD_DIM)
    s = jnp.einsum('bthd,bmhd->bhtm', q, k).astype(jnp.float32) * (MEM_HEAD_DIM ** -0.5)
    p = jax.nn.softmax(s, axis=-1).astype(v.dtype)
    o = jnp.einsum('bhtm,bmhd->bthd', p, v).reshape(bsz, seqlen, D_MODEL)
    return o @ w_mo

def hybrid_layer(x, mem, ffn1_w_in, ffn1_w_out, ln1_g, ln1_b,
                 w_in, conv_w, conv_b, dt_bias, a_log, d_skip, ssd_norm_w,
                 kv_norm_w, w_uk, w_uv, w_proj_ssd, w_proj_att, w_out, ln2_g, ln2_b,
                 w_mq, w_mkv, w_mo, ln3_g, ln3_b,
                 ffn2_w_in, ffn2_w_out, ln4_g, ln4_b):
    x = layer_norm(ALPHA * x + 0.5 * swiglu_ffn(x, ffn1_w_in, ffn1_w_out), ln1_g, ln1_b)
    h = x @ w_in
    g_ssd, g_att, z, xbc, dt_raw, q, c_kv, q_idx, k_idx, w_idx = split_cols(h, IN_SPLITS_2)
    y_ssd = ssd_branch(z, xbc, dt_raw, conv_w, conv_b, dt_bias, a_log, d_skip, ssd_norm_w)
    y_att = dsa_branch(q, c_kv, q_idx, k_idx, w_idx, kv_norm_w, w_uk, w_uv)
    merged = jax.nn.sigmoid(g_ssd) * (y_ssd @ w_proj_ssd) + jax.nn.sigmoid(g_att) * (y_att @ w_proj_att)
    x = layer_norm(ALPHA * x + merged @ w_out, ln2_g, ln2_b)
    x = layer_norm(ALPHA * x + memory_xattn(x, mem, w_mq, w_mkv, w_mo), ln3_g, ln3_b)
    x = layer_norm(ALPHA * x + 0.5 * swiglu_ffn(x, ffn2_w_in, ffn2_w_out), ln4_g, ln4_b)
    return x

def second_inputs(seed: int = 0) -> dict:
    key = jax.random.key(seed)
    keys = iter(jax.random.split(key, 48))
    f32 = jnp.float32
    L = DEPTH_2

    def nrm(shape, scale):
        return jax.random.normal(next(keys), shape, f32) * scale

    def gain(shape):
        return 1.0 + nrm(shape, 0.02)

    x = nrm((BATCH, SEQ, D_MODEL), 1.0)
    mem = nrm((BATCH, MEM_LEN, D_MODEL), 1.0)
    ffn1_w_in = nrm((L, D_MODEL, 2 * D_FF), D_MODEL ** -0.5)
    ffn1_w_out = nrm((L, D_FF, D_MODEL), BETA * D_FF ** -0.5)
    ln1_g = gain((L, D_MODEL))
    ln1_b = nrm((L, D_MODEL), 0.02)
    w_in = nrm((L, D_MODEL, D_IN), D_MODEL ** -0.5)
    conv_w = nrm((L, SSD_CONV, SSD_XBC), SSD_CONV ** -0.5)
    conv_b = nrm((L, SSD_XBC), 0.02)
    dt0 = jnp.exp(jax.random.uniform(next(keys), (L, SSD_HEADS), f32,
                                     minval=math.log(1e-3), maxval=math.log(1e-1)))
    dt_bias = dt0 + jnp.log(-jnp.expm1(-dt0))
    a_log = jnp.log(jax.random.uniform(next(keys), (L, SSD_HEADS), f32, minval=1.0, maxval=16.0))
    d_skip = gain((L, SSD_HEADS))
    ssd_norm_w = gain((L, SSD_INNER))
    kv_norm_w = gain((L, KV_RANK))
    w_uk = nrm((L, ATT_HEADS, ATT_HEAD_DIM, KV_RANK), KV_RANK ** -0.5)
    w_uv = nrm((L, ATT_HEADS, KV_RANK, ATT_HEAD_DIM), KV_RANK ** -0.5)
    w_proj_ssd = nrm((L, SSD_INNER, D_MODEL), SSD_INNER ** -0.5)
    w_proj_att = nrm((L, ATT_WIDTH, D_MODEL), ATT_WIDTH ** -0.5)
    w_out = nrm((L, D_MODEL, D_MODEL), BETA * D_MODEL ** -0.5)
    ln2_g = gain((L, D_MODEL))
    ln2_b = nrm((L, D_MODEL), 0.02)
    w_mq = nrm((L, D_MODEL, D_MODEL), D_MODEL ** -0.5)
    w_mkv = nrm((L, D_MODEL, 2 * D_MODEL), D_MODEL ** -0.5)
    w_mo = nrm((L, D_MODEL, D_MODEL), BETA * D_MODEL ** -0.5)
    ln3_g = gain((L, D_MODEL))
    ln3_b = nrm((L, D_MODEL), 0.02)
    ffn2_w_in = nrm((L, D_MODEL, 2 * D_FF), D_MODEL ** -0.5)
    ffn2_w_out = nrm((L, D_FF, D_MODEL), BETA * D_FF ** -0.5)
    ln4_g = gain((L, D_MODEL))
    ln4_b = nrm((L, D_MODEL), 0.02)
    return {"x": x, "mem": mem,
            "ffn1_w_in": ffn1_w_in, "ffn1_w_out": ffn1_w_out, "ln1_g": ln1_g, "ln1_b": ln1_b,
            "w_in": w_in, "conv_w": conv_w, "conv_b": conv_b, "dt_bias": dt_bias,
            "a_log": a_log, "d_skip": d_skip, "ssd_norm_w": ssd_norm_w,
            "kv_norm_w": kv_norm_w, "w_uk": w_uk, "w_uv": w_uv,
            "w_proj_ssd": w_proj_ssd, "w_proj_att": w_proj_att, "w_out": w_out,
            "ln2_g": ln2_g, "ln2_b": ln2_b,
            "w_mq": w_mq, "w_mkv": w_mkv, "w_mo": w_mo, "ln3_g": ln3_g, "ln3_b": ln3_b,
            "ffn2_w_in": ffn2_w_in, "ffn2_w_out": ffn2_w_out, "ln4_g": ln4_g, "ln4_b": ln4_b}

def second_block(x, mem, ffn1_w_in, ffn1_w_out, ln1_g, ln1_b,
              w_in, conv_w, conv_b, dt_bias, a_log, d_skip, ssd_norm_w,
              kv_norm_w, w_uk, w_uv, w_proj_ssd, w_proj_att, w_out, ln2_g, ln2_b,
              w_mq, w_mkv, w_mo, ln3_g, ln3_b,
              ffn2_w_in, ffn2_w_out, ln4_g, ln4_b):
    for layer in range(DEPTH_2):
        x = hybrid_layer(x, mem,
                         ffn1_w_in[layer], ffn1_w_out[layer], ln1_g[layer], ln1_b[layer],
                         w_in[layer], conv_w[layer], conv_b[layer], dt_bias[layer],
                         a_log[layer], d_skip[layer], ssd_norm_w[layer],
                         kv_norm_w[layer], w_uk[layer], w_uv[layer],
                         w_proj_ssd[layer], w_proj_att[layer], w_out[layer],
                         ln2_g[layer], ln2_b[layer],
                         w_mq[layer], w_mkv[layer], w_mo[layer], ln3_g[layer], ln3_b[layer],
                         ffn2_w_in[layer], ffn2_w_out[layer], ln4_g[layer], ln4_b[layer])
    return x


_first_inputs = second_inputs


def second_inputs(seed=0):
    import zlib

    import numpy as np

    out = dict(_first_inputs(seed))
    spreads = {}
    factors = {'conv_b': 7.985,
     'd_skip': 8.0,
     'ssd_norm_w': 8.0,
     'kv_norm_w': 8.0,
     'ln2_g': 2.809,
     'ln2_b': 2.914,
     'ln3_g': 2.827,
     'ln3_b': 2.774,
     'ln4_g': 2.735,
     'ln4_b': 2.93}
    for name, (base, spread) in spreads.items():
        noise = np.random.default_rng([zlib.crc32(name.encode()), seed]).standard_normal(out[name].shape)
        drawn = base * np.exp(spread * noise) if base else spread * noise
        out[name] = __import__('jax').numpy.asarray(drawn.astype(out[name].dtype))
    for name, factor in factors.items():
        out[name] = (out[name] * factor).astype(out[name].dtype)
    return out


_narrow_inputs = second_inputs


def second_inputs(seed=0):

    out = dict(_narrow_inputs(seed))
    wider = {'d_skip': 3.75, 'ssd_norm_w': 4.05, 'ln4_g': 3.08, 'ln4_b': 3.08}
    for name, times in wider.items():
        mean = out[name].mean()
        out[name] = (mean + times * (out[name] - mean)).astype(out[name].dtype)
    return out


N_A_LAYERS = DEPTH // 2
N_B_LAYERS = DEPTH - N_A_LAYERS
N_META = 16
NEG_INF = -1e30


GLA_HEADS = 4
GLA_DK = D_MODEL // 2 // GLA_HEADS
GLA_DV = D_MODEL // GLA_HEADS
GLA_QK = GLA_HEADS * GLA_DK
GLA_V = GLA_HEADS * GLA_DV
GLA_RANK = 16
GLA_TAU = 16.0
GLA_IN = 2 * GLA_QK + 2 * GLA_V + GLA_RANK
CHUNK = 64

N_Q_HEADS = 16
N_KV_HEADS = 4
GROUP = N_Q_HEADS // N_KV_HEADS
WINDOW_3 = 128
ROT_DIM = HEAD_DIM // 4
ROPE_THETA = 500000.0


def rmsnorm_3(x, g):
    xf = x.astype(jnp.float32)
    y = xf * lax.rsqrt(jnp.mean(xf * xf, axis=-1, keepdims=True) + EPS)
    return (y * g.astype(jnp.float32)).astype(x.dtype)

def swiglu(x, w_in, w_out):
    gate, up = jnp.split(x @ w_in, 2, axis=-1)
    return (jax.nn.silu(gate) * up) @ w_out

def rope_tables(length):
    inv_freq = ROPE_THETA ** (-jnp.arange(0, ROT_DIM, 2, dtype=jnp.float32) / ROT_DIM)
    ang = jnp.arange(length, dtype=jnp.float32)[:, None] * inv_freq[None, :]
    return jnp.cos(ang), jnp.sin(ang)

def apply_partial_rope(x, cos, sin):
    half = ROT_DIM // 2
    shape = (cos.shape[0],) + (1,) * (x.ndim - 3) + (half,)
    c, s = cos.reshape(shape), sin.reshape(shape)
    x1 = x[..., :half].astype(jnp.float32)
    x2 = x[..., half:ROT_DIM].astype(jnp.float32)
    return jnp.concatenate([(x1 * c - x2 * s).astype(x.dtype), (x2 * c + x1 * s).astype(x.dtype),
                            x[..., ROT_DIM:]], axis=-1)

def gla_mixer(hn, w_in, w_gate, b_gate, g_head, w_out):
    B, L, _ = hn.shape
    q, k, v, r, lr = jnp.split(hn @ w_in, [GLA_QK, 2 * GLA_QK, 2 * GLA_QK + GLA_V, 2 * GLA_QK + 2 * GLA_V], axis=-1)
    gk = jax.nn.log_sigmoid((lr @ w_gate + b_gate).astype(jnp.float32)) / GLA_TAU
    pad = CHUNK - N_META
    padf = lambda t: jnp.pad(t, ((0, 0), (pad, 0), (0, 0)))
    Lp = L + pad
    nC = Lp // CHUNK
    def chunks(t, d):
        return t.reshape(B, nC, CHUNK, GLA_HEADS, d).transpose(0, 3, 1, 2, 4)
    qf = chunks(padf(q).astype(jnp.float32), GLA_DK) * (GLA_DK ** -0.5)
    kf = chunks(padf(k).astype(jnp.float32), GLA_DK)
    vf = chunks(padf(v).astype(jnp.float32), GLA_DV)
    bcum = jnp.cumsum(chunks(padf(gk), GLA_DK), axis=3)
    q_dec = qf * jnp.exp(bcum)
    k_dec = kf * jnp.exp(-bcum)
    causal = jnp.tril(jnp.ones((CHUNK, CHUNK), dtype=bool))
    att = jnp.where(causal, jnp.einsum('bhncd,bhnsd->bhncs', q_dec, k_dec), 0.0)
    o_intra = jnp.einsum('bhncs,bhnsv->bhncv', att, vf)
    b_last = bcum[:, :, :, -1:, :]
    chunk_kv = jnp.einsum('bhnsd,bhnsv->bhndv', kf * jnp.exp(b_last - bcum), vf)
    decay = jnp.exp(b_last[:, :, :, 0, :])

    def step(S, inp):
        kv_c, dec_c = inp
        return dec_c[..., None] * S + kv_c, S
    S0 = jnp.zeros((B, GLA_HEADS, GLA_DK, GLA_DV), jnp.float32)
    _, states = lax.scan(step, S0, (jnp.moveaxis(chunk_kv, 2, 0), jnp.moveaxis(decay, 2, 0)))
    states = jnp.moveaxis(states, 0, 2)
    o = o_intra + jnp.einsum('bhncd,bhndv->bhncv', q_dec, states)
    o = o.reshape(B, GLA_HEADS, Lp, GLA_DV)[:, :, pad:].transpose(0, 2, 1, 3)
    o = rmsnorm_3(o, g_head) * jax.nn.silu(r.astype(jnp.float32)).reshape(B, L, GLA_HEADS, GLA_DV)
    return o.reshape(B, L, GLA_V).astype(hn.dtype) @ w_out

def shared_kv(h, g_kv, w_kv, cos, sin):
    B, L, _ = h.shape
    k, v = jnp.split(rmsnorm_3(h, g_kv) @ w_kv, 2, axis=-1)
    k = apply_partial_rope(k.reshape(B, L, N_KV_HEADS, HEAD_DIM), cos, sin)
    v = v.reshape(B, L, N_KV_HEADS, HEAD_DIM)
    return k.transpose(0, 2, 1, 3), v.transpose(0, 2, 1, 3)

def sink_softmax(s, mask, sink):
    s = jnp.where(mask, s.astype(jnp.float32), NEG_INF)
    m = jnp.maximum(jnp.max(s, axis=-1, keepdims=True), sink)
    p = jnp.exp(s - m)
    return p / (jnp.sum(p, axis=-1, keepdims=True) + jnp.exp(sink - m))

def swa_mixer(hn, w_q, sinks, w_out, k, v, cos, sin):
    B, L, _ = hn.shape
    S = L - N_META
    nB = S // WINDOW_3
    q = (hn @ w_q).reshape(B, L, N_KV_HEADS, GROUP, HEAD_DIM)
    q = (apply_partial_rope(q, cos, sin) * (HEAD_DIM ** -0.5)).transpose(0, 2, 3, 1, 4)
    sink_b = sinks.reshape(N_KV_HEADS, GROUP).astype(jnp.float32)
    k_meta, v_meta = k[:, :, :N_META], v[:, :, :N_META]
    s_meta = jnp.einsum('bkgqd,bkmd->bkgqm', q[:, :, :, :N_META], k_meta)
    p_meta = sink_softmax(s_meta, jnp.tril(jnp.ones((N_META, N_META), dtype=bool)), sink_b[None, :, :, None, None])
    o_meta = jnp.einsum('bkgqm,bkmd->bkgqd', p_meta.astype(v.dtype), v_meta)
    q_blk = q[:, :, :, N_META:].reshape(B, N_KV_HEADS, GROUP, nB, WINDOW_3, HEAD_DIM)
    def band(t):
        t_meta = t[:, :, :N_META]
        t_blk = t[:, :, N_META:].reshape(B, N_KV_HEADS, nB, WINDOW_3, HEAD_DIM)
        prev = jnp.concatenate([jnp.zeros_like(t_blk[:, :, :1]), t_blk[:, :, :-1]], axis=2)
        meta = jnp.broadcast_to(t_meta[:, :, None], (B, N_KV_HEADS, nB, N_META, HEAD_DIM))
        return jnp.concatenate([meta, prev, t_blk], axis=3)
    k_band, v_band = band(k), band(v)
    s = jnp.einsum('bkgnqd,bknsd->bkgnqs', q_blk, k_band)
    i = jnp.arange(WINDOW_3)[:, None]
    j = jnp.arange(WINDOW_3)[None, :]
    blk = jnp.arange(nB)[:, None, None]
    mask = jnp.concatenate([
        jnp.ones((nB, WINDOW_3, N_META), dtype=bool),
        (j > i)[None] & (blk > 0),
        jnp.broadcast_to((j <= i)[None], (nB, WINDOW_3, WINDOW_3)),
    ], axis=-1)
    p = sink_softmax(s, mask, sink_b[None, :, :, None, None, None])
    o_real = jnp.einsum('bkgnqs,bknsd->bkgnqd', p.astype(v.dtype), v_band).reshape(B, N_KV_HEADS, GROUP, S, HEAD_DIM)
    o = jnp.concatenate([o_meta, o_real], axis=3).transpose(0, 3, 1, 2, 4).reshape(B, L, N_Q_HEADS * HEAD_DIM)
    return o @ w_out

def third_inputs(seed: int = 0) -> dict:
    key = jax.random.key(seed)
    ks = jax.random.split(key, 16)
    nrm = lambda k, shape, fan_in: jax.random.normal(k, shape, jnp.float32) * (fan_in ** -0.5)
    return {
        "x": jax.random.normal(ks[0], (BATCH, SEQ, D_MODEL), jnp.float32),
        "meta_tokens": jax.random.normal(ks[1], (N_META, D_MODEL), jnp.float32),
        "norm_gains": 1.0 + 0.02 * jax.random.normal(ks[2], (DEPTH, 6, D_MODEL), jnp.float32),
        "w_ffn_in": nrm(ks[3], (DEPTH, 2, D_MODEL, 2 * D_FF), D_MODEL),
        "w_ffn_out": nrm(ks[4], (DEPTH, 2, D_FF, D_MODEL), D_FF),
        "gla_w_in": nrm(ks[5], (N_A_LAYERS, D_MODEL, GLA_IN), D_MODEL),
        "gla_w_gate": nrm(ks[6], (N_A_LAYERS, GLA_RANK, GLA_QK), GLA_RANK),
        "gla_b_gate": 0.1 * jax.random.normal(ks[7], (N_A_LAYERS, GLA_QK), jnp.float32),
        "gla_norm": 1.0 + 0.02 * jax.random.normal(ks[8], (N_A_LAYERS, GLA_DV), jnp.float32),
        "gla_w_out": nrm(ks[9], (N_A_LAYERS, GLA_V, D_MODEL), GLA_V),
        "kv_norm": 1.0 + 0.02 * jax.random.normal(ks[10], (D_MODEL,), jnp.float32),
        "w_kv": nrm(ks[11], (D_MODEL, 2 * N_KV_HEADS * HEAD_DIM), D_MODEL),
        "swa_w_q": nrm(ks[12], (N_B_LAYERS, D_MODEL, N_Q_HEADS * HEAD_DIM), D_MODEL),
        "swa_sinks": 0.5 * jax.random.normal(ks[13], (N_B_LAYERS, N_Q_HEADS), jnp.float32),
        "swa_w_out": nrm(ks[14], (N_B_LAYERS, N_Q_HEADS * HEAD_DIM, D_MODEL), N_Q_HEADS * HEAD_DIM),
    }

def third_block(x, meta_tokens, norm_gains, w_ffn_in, w_ffn_out, gla_w_in, gla_w_gate, gla_b_gate, gla_norm,
              gla_w_out, kv_norm, w_kv, swa_w_q, swa_sinks, swa_w_out):
    B = x.shape[0]
    meta = jnp.broadcast_to(meta_tokens.astype(x.dtype)[None], (B, N_META, D_MODEL))
    h = jnp.concatenate([meta, x], axis=1)
    cos, sin = rope_tables(h.shape[1])
    k_sh, v_sh = None, None
    for layer in range(DEPTH):
        g = norm_gains[layer]
        h = h + 0.5 * rmsnorm_3(swiglu(rmsnorm_3(h, g[0]), w_ffn_in[layer, 0], w_ffn_out[layer, 0]), g[1])
        hn = rmsnorm_3(h, g[2])
        if layer < N_A_LAYERS:
            a = layer
            mix = gla_mixer(hn, gla_w_in[a], gla_w_gate[a], gla_b_gate[a], gla_norm[a], gla_w_out[a])
        else:
            b = layer - N_A_LAYERS
            mix = swa_mixer(hn, swa_w_q[b], swa_sinks[b], swa_w_out[b], k_sh, v_sh, cos, sin)
        h = h + rmsnorm_3(mix, g[3])
        h = h + 0.5 * rmsnorm_3(swiglu(rmsnorm_3(h, g[4]), w_ffn_in[layer, 1], w_ffn_out[layer, 1]), g[5])
        if layer == N_A_LAYERS - 1:
            k_sh, v_sh = shared_kv(h, kv_norm, w_kv, cos, sin)
    return h[:, N_META:]


def setup_inputs(seed=0):
    out = dict(first_inputs(seed))
    for name, value in second_inputs(seed + 1).items():
        if name != "x":
            out[name + "_2"] = value
    for name, value in third_inputs(seed + 2).items():
        if name != "x":
            out[name + "_3"] = value
    return out


def reference(
    x, l0_ffn1_pre_g, l0_ffn1_post_g, l0_ffn1_w_gate, l0_ffn1_w_up, l0_ffn1_w_down,
    l0_mix_pre_g, l0_mix_post_g, l0_w_in, l0_cmp_pe_k, l0_cmp_w1_k, l0_cmp_w2_k, l0_cmp_pe_v,
    l0_cmp_w1_v, l0_cmp_w2_v, l0_conv_w, l0_conv_b, l0_w_out, l0_ffn2_pre_g, l0_ffn2_post_g,
    l0_ffn2_w_gate, l0_ffn2_w_up, l0_ffn2_w_down, l1_ffn1_pre_g, l1_ffn1_post_g, l1_ffn1_w_gate,
    l1_ffn1_w_up, l1_ffn1_w_down, l1_mix_pre_g, l1_mix_post_g, l1_mu, l1_w_r, l1_w_k, l1_w_v,
    l1_w_o, l1_w0, l1_w_dec1, l1_w_dec2, l1_a0, l1_w_a1, l1_w_a2, l1_w_g1, l1_w_g2, l1_k_k,
    l1_k_a, l1_r_k, l1_lnx_g, l1_lnx_b, l1_ffn2_pre_g, l1_ffn2_post_g, l1_ffn2_w_gate,
    l1_ffn2_w_up, l1_ffn2_w_down, mem_2, ffn1_w_in_2, ffn1_w_out_2, ln1_g_2, ln1_b_2, w_in_2,
    conv_w_2, conv_b_2, dt_bias_2, a_log_2, d_skip_2, ssd_norm_w_2, kv_norm_w_2, w_uk_2, w_uv_2,
    w_proj_ssd_2, w_proj_att_2, w_out_2, ln2_g_2, ln2_b_2, w_mq_2, w_mkv_2, w_mo_2, ln3_g_2,
    ln3_b_2, ffn2_w_in_2, ffn2_w_out_2, ln4_g_2, ln4_b_2, meta_tokens_3, norm_gains_3,
    w_ffn_in_3, w_ffn_out_3, gla_w_in_3, gla_w_gate_3, gla_b_gate_3, gla_norm_3, gla_w_out_3,
    kv_norm_3, w_kv_3, swa_w_q_3, swa_sinks_3, swa_w_out_3,
):
    x = first_block(
        x, l0_ffn1_pre_g, l0_ffn1_post_g, l0_ffn1_w_gate, l0_ffn1_w_up, l0_ffn1_w_down,
        l0_mix_pre_g, l0_mix_post_g, l0_w_in, l0_cmp_pe_k, l0_cmp_w1_k, l0_cmp_w2_k,
        l0_cmp_pe_v, l0_cmp_w1_v, l0_cmp_w2_v, l0_conv_w, l0_conv_b, l0_w_out, l0_ffn2_pre_g,
        l0_ffn2_post_g, l0_ffn2_w_gate, l0_ffn2_w_up, l0_ffn2_w_down, l1_ffn1_pre_g,
        l1_ffn1_post_g, l1_ffn1_w_gate, l1_ffn1_w_up, l1_ffn1_w_down, l1_mix_pre_g,
        l1_mix_post_g, l1_mu, l1_w_r, l1_w_k, l1_w_v, l1_w_o, l1_w0, l1_w_dec1, l1_w_dec2,
        l1_a0, l1_w_a1, l1_w_a2, l1_w_g1, l1_w_g2, l1_k_k, l1_k_a, l1_r_k, l1_lnx_g, l1_lnx_b,
        l1_ffn2_pre_g, l1_ffn2_post_g, l1_ffn2_w_gate, l1_ffn2_w_up, l1_ffn2_w_down,
    )
    x = second_block(
        x, mem_2, ffn1_w_in_2, ffn1_w_out_2, ln1_g_2, ln1_b_2, w_in_2, conv_w_2, conv_b_2,
        dt_bias_2, a_log_2, d_skip_2, ssd_norm_w_2, kv_norm_w_2, w_uk_2, w_uv_2, w_proj_ssd_2,
        w_proj_att_2, w_out_2, ln2_g_2, ln2_b_2, w_mq_2, w_mkv_2, w_mo_2, ln3_g_2, ln3_b_2,
        ffn2_w_in_2, ffn2_w_out_2, ln4_g_2, ln4_b_2,
    )
    return third_block(
        x, meta_tokens_3, norm_gains_3, w_ffn_in_3, w_ffn_out_3, gla_w_in_3, gla_w_gate_3,
        gla_b_gate_3, gla_norm_3, gla_w_out_3, kv_norm_3, w_kv_3, swa_w_q_3, swa_sinks_3,
        swa_w_out_3,
    )


_drawn_inputs = setup_inputs


def setup_inputs(seed=0):
    import zlib

    import numpy as np

    out = dict(_drawn_inputs(seed))
    spreads = {}
    factors = {'gla_b_gate_3': 3.42, 'gla_norm_3': 35.028, 'kv_norm_3': 23.006, 'swa_sinks_3': 64.0}
    for name, (base, spread) in spreads.items():
        noise = np.random.default_rng([zlib.crc32(name.encode()), seed]).standard_normal(out[name].shape)
        drawn = base * np.exp(spread * noise) if base else spread * noise
        out[name] = __import__('jax').numpy.asarray(drawn.astype(out[name].dtype))
    for name, factor in factors.items():
        out[name] = (out[name] * factor).astype(out[name].dtype)
    return out
```

```python
from contextlib import ExitStack

import numpy as np

import concourse.bass as bass
from concourse import mybir

P = 128
D = 1024
FF = 2816
NF = FF // P
T1 = 256
T3 = 272
NSLOT = 8
SLOT = 2048
BIG = -1.0e30
ALPHA = 2.0 ** 0.25

ALU = mybir.AluOpType
ACT = mybir.ActivationFunctionType
F32 = mybir.dt.float32
AX_X = mybir.AxisListType.X

FFNS = ("l0_ffn1", "l0_ffn2", "l1_ffn1", "l1_ffn2")


def table(sizes):
    at, out = 0, {}
    for name, n in sizes:
        out[name] = (at, n)
        at += n
    return out, at


COLS, NCOL = table(
    [(f + s, 8) for f in FFNS for s in ("_pre_g", "_post_g")]
    + [(f"l{i}_mix_{s}_g", 8) for i in range(2) for s in ("pre", "post")]
    + [("l0_conv_w", 12), ("l0_conv_b", 4), ("l0_cmp_pe_k", 16), ("l0_cmp_pe_v", 16), ("l1_mu", 48)]
    + [(f"ln{i}_{s}_2", 8) for i in range(1, 5) for s in "gb"]
    + [("conv_w_2", 64), ("conv_b_2", 16), ("d_skip_2c", 8), ("ssd_norm_w_2", 8), ("kv_norm_w_2", 2)]
    + [("norm_gains_3", 96), ("kv_norm_3", 8), ("gla_b_gate_3", 4), ("gla_norm_3", 2)])

ROWS, NROW = table([("dt_bias_2", 16), ("a_log_2", 16), ("d_skip_2", 16), ("swa_sinks_3", 16)])

CSTS, NCST = table([
    ("ident", 128), ("ones", 128), ("alibi", 512), ("alibi_cmp", 32), ("m64", 256), ("suf64", 128),
    ("chunk", 2), ("level", 768), ("tri128", 128), ("suf128", 128), ("swa", 816), ("rope", 48),
    ("reset", 272)])


def constants():
    c = np.zeros((P, NCST), np.float32)

    def put(name, a):
        at, n = CSTS[name]
        a = np.asarray(a, np.float32)
        c[:a.shape[0], at:at + n] = a.reshape(a.shape[0], -1)

    i = np.arange(P)[:, None]
    j = np.arange(P)[None, :]
    put("ident", np.eye(P))
    put("ones", np.ones((P, P)))
    s = np.arange(T1)[None, :]
    put("alibi", np.concatenate([np.where(s <= i + P * m, s - (i + P * m), BIG) for m in range(2)], 1))
    n = np.arange(16)[None, :]
    e = 16 * n + 31
    put("alibi_cmp", np.concatenate([np.where((e <= i + P * m) & (n < 15), e - (i + P * m), BIG)
                                     for m in range(2)], 1))
    same = i // 64 == j // 64
    put("m64", np.concatenate([same & (i < j), same & (i <= j)], 1))
    put("suf64", same & (i > j))
    put("chunk", i // 64 == np.arange(2)[None, :])
    put("level", np.concatenate([(i // (2 * b) == j // (2 * b)) & (i % (2 * b) < b) & (j % (2 * b) >= b)
                                 for b in (1, 2, 4, 8, 16, 32)], 1))
    put("tri128", i <= j)
    put("suf128", i > j)
    keep = [np.concatenate([j <= i, np.zeros((P, P), bool), np.ones((P, 16), bool)], 1),
            np.concatenate([j > i, j <= i, np.ones((P, 16), bool)], 1),
            np.concatenate([np.zeros((P, T1), bool), np.arange(16)[None, :] <= i], 1)]
    put("swa", np.concatenate([np.where(k, 0.0, BIG) for k in keep], 1))
    freq = np.float32(500000.0) ** (-np.arange(0, 16, 2, dtype=np.float32) / np.float32(16))
    rope = []
    for base in (16, 16 + P, 0):
        ang = (np.arange(P, dtype=np.float32)[:, None] + np.float32(base)) * freq[None, :].astype(np.float32)
        rope += [np.cos(ang), np.sin(ang)]
    put("rope", np.concatenate(rope, 1))
    put("reset", np.broadcast_to((np.arange(T3) % 64 != 0)[None, :], (P, T3)))
    return c


class Prog:

    def __init__(self, nc, ctx):
        self.nc = nc
        self.ctx = ctx
        self.q = {e: [] for e in ("pe", "act", "dve", "pool", "sp")}
        self.h = {"pe": nc.tensor, "act": nc.scalar, "dve": nc.vector, "pool": nc.gpsimd, "sp": nc.sync}
        self.sem = {e: ctx.enter_context(nc.semaphore("s_" + e)) for e in ("pe", "act", "dve", "pool")}
        self.n = {e: 0 for e in self.sem}
        self.seen = {e: {} for e in self.q}
        for i in range(NSLOT):
            self.sem[f"slot{i}"] = ctx.enter_context(nc.semaphore(f"s_slot{i}"))
            self.n[f"slot{i}"] = 0
        self.slot_free = [None] * NSLOT
        self.units = 0
        self.ring = self.sb("ring", NSLOT * SLOT)
        self.ps = [ctx.enter_context(nc.psum_tensor(f"ps{i}", [P, 512], F32)) for i in range(8)]
        self.ps_free = [[] for _ in range(8)]
        self.nps = 0

    def sb(self, name, n):
        return self.ctx.enter_context(self.nc.sbuf_tensor(name, [P, n], F32))

    def wait(self, e, toks):
        for t in toks:
            if t is None:
                continue
            s, v = t
            if self.seen[e].get(s, 0) >= v:
                continue
            self.seen[e][s] = v
            self.q[e].append(lambda h=self.h[e], s=self.sem[s], v=v: h.wait_ge(s, v))

    def op(self, e, fn, *toks):
        if e != "pe" and self.n[e]:
            toks = toks + ((e, self.n[e]),)
        self.wait(e, toks)
        self.n[e] += 1
        self.q[e].append(lambda s=self.sem[e]: fn().then_inc(s, 1))
        return e, self.n[e]

    def last(self):
        return [(e, self.n[e]) for e in ("pe", "act", "dve", "pool") if self.n[e]]

    def fence(self):
        toks = self.last()
        for e in ("pe", "act", "dve", "pool"):
            self.wait(e, [t for t in toks if t[0] != e])
        for b in range(8):
            self.ps_free[b] = []

    def dma_group(self, name):
        self.sem[name] = self.ctx.enter_context(self.nc.semaphore("s_" + name))
        self.n[name] = 0

    def dma(self, e, group, out, in_, *toks):
        self.wait(e, toks)
        self.n[group] += 16
        self.q[e].append(lambda h=self.h[e], s=self.sem[group]: h.dma_start(out, in_).then_inc(s, 16))
        return group, self.n[group]

    def unit(self, *loads):
        i = self.units % NSLOT
        self.units += 1
        self.wait("sp", [self.slot_free[i]] if self.slot_free[i] else [])
        assert self.units <= NSLOT or self.slot_free[i], "slot reused before it was freed"
        self.slot_free[i] = None
        at = i * SLOT
        out = []
        for off, w, p0, p1, src in loads:
            dst = self.ring[p0:p1, at + off:at + off + w]
            tok = self.dma("sp", f"slot{i}", dst, src)
            out.append(dst)
        return i, out, tok

    def free_unit(self, i, tok):
        self.slot_free[i] = tok

    def bank(self):
        b = self.nps % 8
        self.nps += 1
        w, self.ps_free[b] = self.ps_free[b], None
        assert w is not None, f"bank {b} is still held"
        return b, self.ps[b], w

    def free(self, b, *toks):
        self.ps_free[b] = list(toks)

    def mm(self, out, pairs, *toks, first=True, final=True, inc=True):
        self.wait("pe", toks)
        n = len(pairs)
        for i, (a, b) in enumerate(pairs):
            def f(a=a, b=b, st=first and i == 0, sp=final and i == n - 1):
                return self.nc.tensor.matmul(out, a, b, start=st, stop=sp)
            if i == n - 1 and inc:
                self.n["pe"] += 1
                self.q["pe"].append(lambda f=f: f().then_inc(self.sem["pe"], 1))
            else:
                self.q["pe"].append(f)
        return ("pe", self.n["pe"]) if inc else None

    def tr(self, out, in_, ident, *toks, inc=True):
        self.wait("pe", toks)
        f = lambda: self.nc.tensor.transpose(out, in_, ident)
        if inc:
            self.n["pe"] += 1
            self.q["pe"].append(lambda: f().then_inc(self.sem["pe"], 1))
            return "pe", self.n["pe"]
        self.q["pe"].append(f)

    def act(self, out, in_, func, *toks, **kw):
        return self.op("act", lambda: self.nc.scalar.activation(out, in_, func, **kw), *toks)

    def tt(self, out, a, b, op, *toks, e="dve"):
        return self.op(e, lambda: self.h[e].tensor_tensor(out, a, b, op), *toks)

    def ts(self, out, a, s1, s2, op0, op1, *toks, e="dve"):
        if s2 is None:
            return self.op(e, lambda: self.h[e].tensor_scalar(out, a, s1, None, op0), *toks)
        return self.op(e, lambda: self.h[e].tensor_scalar(out, a, s1, s2, op0, op1), *toks)

    def stt(self, out, a, s, b, op0, op1, *toks, **kw):
        return self.op("dve", lambda: self.nc.vector.scalar_tensor_tensor(out, a, s, b, op0, op1, **kw), *toks)

    def cp(self, out, in_, *toks, e="dve"):
        if e == "act":
            return self.act(out, in_, ACT.Copy, *toks)
        return self.op(e, lambda: self.h[e].tensor_copy(out, in_), *toks)

    def red(self, out, in_, op, *toks):
        return self.op("dve", lambda: self.nc.vector.tensor_reduce(out, in_, AX_X, op), *toks)

    def recip(self, out, in_, *toks):
        return self.op("dve", lambda: self.nc.vector.reciprocal(out, in_), *toks)

    def run(self):
        block = self.ctx.enter_context(self.nc.Block())

        def play(name):
            def body(_):
                for f in self.q[name]:
                    f()
            return body

        block.sync(play("sp"))
        block.scalar(play("act"))
        block.vector(play("dve"))
        block.gpsimd(play("pool"))
        block.tensor(play("pe"))


def bc(ap, *shape):
    return ap.unsqueeze(len(ap.shape)).broadcast_to(list(ap.shape) + list(shape))


def bc_mid(ap, n):
    return ap.unsqueeze(1).broadcast_to([ap.shape[0], n] + list(ap.shape[1:]))


class Model:
    def __init__(self, nc, ctx, d, out, stages):
        self.d = d
        g = self.g = Prog(nc, ctx)
        self.stages = stages
        self.cst = g.sb("cst", NCST)
        self.cols = g.sb("cols", NCOL)
        self.rows = g.sb("rows", NROW)
        self.xT = g.sb("xT", 8 * T3)[:, :].rearrange("p (k t) -> p k t", k=8)
        self.hT = g.sb("hT", 8 * T3)[:, :].rearrange("p (k t) -> p k t", k=8)
        self.yT = g.sb("yT", 8 * T3)[:, :].rearrange("p (k t) -> p k t", k=8)
        self.sq_ = g.sb("sq", 8 * T3)
        self.sq = self.sq_[:, :].rearrange("p (k t) -> p k t", k=8)
        self.rstd = g.sb("rstd", 3 * T3)[:, :].rearrange("p (k t) -> p k t", k=3)
        self.tmp = g.sb("tmp", 4 * T3)[:, :].rearrange("p (k t) -> p k t", k=4)
        self.tmp_free = [None] * 4
        self.ntmp = 0
        self.small = g.sb("small", 512)
        self.A = g.sb("arena", 20800)
        self.hf = self.A[:, 0:NF * T3].rearrange("p (k t) -> p k t", k=NF)
        self.ident = self.c("ident")
        self.ones = self.c("ones")
        g.dma_group("cst")
        g.dma("sp", "cst", self.cst[:, :], d["cst"])
        g.dma("sp", "cst", self.cols[:, :], d["cols"])
        t = g.dma("sp", "cst", self.rows[:, :], d["rows"].broadcast_to([P, NROW]))
        for e in ("pe", "act", "dve", "pool"):
            g.wait(e, [t])
        self.T = T1
        self.xtok = [None] * 8
        self.load_x(d["x"], 0)
        plan = [
            lambda: self.ffn1("l0_ffn1"), self.nsa, lambda: self.ffn1("l0_ffn2"),
            lambda: self.ffn1("l1_ffn1"), self.rwkv, lambda: self.ffn1("l1_ffn2"),
            lambda: self.ffn2("ffn1", 1), self.hybrid, self.mem, lambda: self.ffn2("ffn2", 4),
            self.enter3, lambda: self.ffn3(0, 0), self.gla, lambda: self.ffn3(0, 1), self.shared, lambda: self.ffn3(1, 0),
            self.swa, lambda: self.ffn3(1, 1)]
        for i in stages:
            plan[i]()
        self.store(out)
        g.run()

    def c(self, name, j=None, w=128):
        at, n = CSTS[name]
        if j is None:
            return self.cst[:, at:at + n]
        return self.cst[:, at + j * w:at + (j + 1) * w]

    def col(self, name, j):
        at = COLS[name][0] + j
        return self.cols[:, at:at + 1]

    def load_x(self, x, at):
        g = self.g
        if at == 0:
            i, (stage,), t = g.unit((0, SLOT, 0, P, x))
            tiles = [(0, P, 0), (1, P, P)]
        else:
            i, (stage,), t = g.unit((0, D, 0, T3 - at, x))
            tiles = [(0, T3 - at, at)]
        stage = stage.rearrange("p (m c) -> p m c", c=D)
        for k in range(8):
            b, ps, w = g.bank()
            for m, p, c in tiles:
                tk = g.tr(ps[:, c - at:c - at + p], stage[0:p, m, k * P:(k + 1) * P], self.ident[0:p, 0:p], t, *w)
            wide = sum(p for _, p, _ in tiles)
            tk = g.cp(self.xT[:, k, at:at + wide], ps[:, 0:wide], tk)
            g.free(b, tk)
            self.xtok[k] = tk
        g.free_unit(i, ("pe", g.n["pe"]))
        g.fence()

    def store(self, out):
        g = self.g
        g.fence()
        g.dma_group("out")
        stage = self.A[:, 0:2048].rearrange("p (m c) -> p m c", m=2)
        for m in range(2):
            for h in range(2):
                b, ps, w = g.bank()
                for k in range(4):
                    tk = g.tr(ps[:, k * P:(k + 1) * P], self.xT[:, 4 * h + k, m * P:(m + 1) * P], self.ident, *w)
                tk = g.cp(stage[:, m, h * 512:(h + 1) * 512], ps[:, :], tk, e=("dve", "act")[h])
                g.free(b, tk)
                t = g.dma("sp", "out", out[m * P:(m + 1) * P, h * 512:(h + 1) * 512],
                          stage[:, m, h * 512:(h + 1) * 512], tk)
        g.wait("sp", [t])

    def sumsq(self, src, toks, T, mean=False):
        g = self.g
        b, ps, w = g.bank()
        for k in range(8):
            if mean:
                s, tk = src[:, k, 0:T], toks[k]
            else:
                s = self.sq[:, k, 0:T]
                if k % 2:
                    tk = g.tt(s, src[:, k, 0:T], src[:, k, 0:T], ALU.mult, toks[k], ("pe", g.n["pe"]))
                else:
                    tk = g.act(s, src[:, k, 0:T], ACT.Square, toks[k], ("pe", g.n["pe"]))
            tp = g.mm(ps[:, 0:T], [(self.ones, s)], tk, *w, first=k == 0, final=k == 7, inc=k == 7)
        return b, ps, tp

    def rsqrt(self, out, ps, tp, mult, add, T, b=None):
        g = self.g
        tk = g.ts(out, ps, mult, add, ALU.mult, ALU.add, tp)
        if b is not None:
            g.free(b, tk)
        tk = g.recip(out, out, tk)
        return g.act(out, out, ACT.Sqrt, tk)

    def prenorm(self, gain, j=0):
        g, T = self.g, self.T
        b, ps, tp = self.sumsq(self.xT, self.xtok, T)
        tr = self.rsqrt(self.rstd[:, 0, 0:T], ps[:, 0:T], tp, 1.0 / D, 1e-6, T, b)
        toks = []
        for k in range(8):
            toks.append(g.stt(self.hT[:, k, 0:T], self.xT[:, k, 0:T], self.col(gain, j * 8 + k), self.rstd[:, 0, 0:T],
                              ALU.mult, ALU.mult, tr))
        return toks

    def evac8(self, banks, T):
        g = self.g
        toks = []
        for k, (b, ps, tp) in enumerate(banks):
            tk = g.cp(self.yT[:, k, 0:T], ps[:, 0:T], tp, e=("dve", "act")[k % 2])
            g.free(b, tk)
            toks.append(tk)
        return toks

    def postnorm(self, banks, gain, j, half):
        g, T = self.g, self.T
        yt = self.evac8(banks, T)
        b, ps, tp = self.sumsq(self.yT, yt, T)
        f = 4.0 if half else 1.0
        tr = self.rsqrt(self.rstd[:, 0, 0:T], ps[:, 0:T], tp, f / D, f * 1e-6, T, b)
        for k in range(8):
            tk = g.stt(self.yT[:, k, 0:T], self.yT[:, k, 0:T], self.col(gain, j * 8 + k), self.rstd[:, 0, 0:T],
                       ALU.mult, ALU.mult, tr, tp)
            self.xtok[k] = g.tt(self.xT[:, k, 0:T], self.xT[:, k, 0:T], self.yT[:, k, 0:T], ALU.add, tk)
        g.fence()

    def layernorm(self, banks, n, half):
        g, T = self.g, self.T
        f = 2.0 if half else 1.0
        yt = []
        for k, (b, ps, tp) in enumerate(banks):
            tk = g.stt(self.yT[:, k, 0:T], self.xT[:, k, 0:T], ALPHA * f, ps[:, 0:T], ALU.mult, ALU.add, tp)
            g.free(b, tk)
            yt.append(tk)
        b, ps, tp = self.sumsq(self.yT, yt, T, mean=True)
        tm = g.ts(self.rstd[:, 1, 0:T], ps[:, 0:T], 1.0 / D, None, ALU.mult, None, tp)
        g.free(b, tm)
        yt = [g.tt(self.yT[:, k, 0:T], self.yT[:, k, 0:T], self.rstd[:, 1, 0:T], ALU.subtract, tm) for k in range(8)]
        b, ps, tp = self.sumsq(self.yT, yt, T)
        tr = self.rsqrt(self.rstd[:, 0, 0:T], ps[:, 0:T], tp, 1.0 / D, f * f * 1e-5, T, b)
        for k in range(8):
            tk = g.stt(self.yT[:, k, 0:T], self.yT[:, k, 0:T], self.col(f"ln{n}_g_2", k), self.rstd[:, 0, 0:T],
                       ALU.mult, ALU.mult, tr, tp)
            self.xtok[k] = g.act(self.xT[:, k, 0:T], self.yT[:, k, 0:T], ACT.Identity, tk,
                                 bias=self.col(f"ln{n}_b_2", k))
        g.fence()

    def colunit(self, name, j, k=8):
        i, (ap,), t = self.g.unit((0, k * 256, 0, P, self.d[name][j]))
        return i, ap.rearrange("p (k n) -> p k n", k=k), t

    def rowunit(self, name, j):
        i, (ap,), t = self.g.unit((0, SLOT, 0, P, self.d[name][j]))
        return i, ap.rearrange("p (k n) -> p k n", k=2), t

    def gettmp(self):
        i = self.ntmp % 4
        self.ntmp += 1
        return i, self.tmp[:, i, :], self.tmp_free[i]

    def down(self, name, src, toks, T, nk):
        g = self.g
        banks = [g.bank() for _ in range(8)]
        tp = None
        for u in range(nk // 2):
            i, w, t = self.rowunit(name, u)
            for kk in range(2):
                k = 2 * u + kk
                for n, (b, ps, wt) in enumerate(banks):
                    fin = k == nk - 1
                    tk = g.mm(ps[:, 0:T], [(w[:, kk, n * P:(n + 1) * P], src[:, k, 0:T])], t, toks[k], *wt,
                              first=k == 0, final=fin, inc=fin or (kk == 1 and n == 7))
                    if fin:
                        banks[n] = (b, ps, tk)
            g.free_unit(i, ("pe", g.n["pe"]))
        return banks

    def ffn(self, ht, wg, wu, wd, src=None):
        g, T = self.g, self.T
        src = self.hT if src is None else src
        hf = []
        for j in range(NF):
            if j % 2 == 0:
                ig, wgu, tg = self.colunit(wg, j // 2)
                iu, wuu, tu = self.colunit(wu, j // 2)
            c = (j % 2) * P
            bg, pg, w1 = g.bank()
            bu, pu, w2 = g.bank()
            for k in range(8):
                tp1 = g.mm(pg[:, 0:T], [(wgu[:, k, c:c + P], src[:, k, 0:T])], tg, ht[k], *w1,
                           first=k == 0, final=k == 7, inc=k == 7)
            tp2 = g.mm(pu[:, 0:T], [(wuu[:, k, c:c + P], src[:, k, 0:T]) for k in range(8)], tu, *w2)
            if j % 2:
                g.free_unit(ig, tp2)
                g.free_unit(iu, tp2)
            i, tmp, tf = self.gettmp()
            ta = g.act(tmp[:, 0:T], pg[:, 0:T], ACT.Silu, tp1, tf)
            g.free(bg, ta)
            td = g.tt(self.hf[:, j, 0:T], tmp[:, 0:T], pu[:, 0:T], ALU.mult, ta, tp2)
            g.free(bu, td)
            self.tmp_free[i] = td
            hf.append(td)
        return self.down(wd, self.hf, hf, T, NF)

    def ffn1(self, n):
        ht = self.prenorm(n + "_pre_g")
        banks = self.ffn(ht, n + "_w_gate", n + "_w_up", n + "_w_down")
        self.postnorm(banks, n + "_post_g", 0, True)

    def ffn2(self, n, ln):
        banks = self.ffn(self.xtok, n + "_w_gate_2", n + "_w_up_2", n + "_w_out_2", src=self.xT)
        self.layernorm(banks, ln, True)

    def ffn3(self, layer, i):
        ht = self.prenorm("norm_gains_3", layer * 6 + 4 * i)
        banks = self.ffn(ht, f"g3_{layer}{i}", f"u3_{layer}{i}", f"d3_{layer}{i}")
        self.postnorm(banks, "norm_gains_3", layer * 6 + 4 * i + 1, True)

    def enter3(self):
        self.g.fence()
        self.load_x(self.d["meta_tokens_3"], T1)
        self.T = T3


    def softmax(self, S, H, nk, rows, toks, sink=None, gate=None, floor=False, out=None):
        g = self.g
        n = self.nsm % 2
        self.nsm += 1
        sm = self.small[0:rows, 128 * n:128 * n + 128]
        mx, den, e = sm[:, 0:H], sm[:, 16:16 + H], sm[:, 32:32 + H]
        tk = g.red(mx, S, ALU.max, *toks)
        if sink is not None:
            tk = g.tt(mx, mx, sink, ALU.max, tk)
        if floor:
            tk = g.ts(mx, mx, -1e20, None, ALU.max, None, tk)
        tk = g.ts(mx, mx, -1.0, None, ALU.mult, None, tk)
        if sink is not None:
            ts = g.tt(e, sink, mx, ALU.add, tk)
            te = g.act(e, e, ACT.Exp, ts)
        for h in range(H):
            ta = g.act(S[:, h, :], S[:, h, :], ACT.Exp, tk, bias=mx[:, h:h + 1], accum_out=den[:, h:h + 1])
        if sink is not None:
            ta = g.tt(den, den, e, ALU.add, ta)
        if floor:
            ta = g.ts(den, den, 1e-30, None, ALU.max, None, ta)
        ta = g.recip(den, den, ta)
        if gate is not None:
            ta = g.tt(den, den, gate, ALU.mult, ta)
        for h in range(H):
            tk = g.ts(S[:, h, :], S[:, h, :], den[:, h:h + 1], None, ALU.mult, None, ta)
        return tk

    def turn(self, dst, src, rows, widths, toks, wfree=()):
        g = self.g
        b, ps, w = g.bank()
        out = []
        for i, (c, wd) in enumerate(widths):
            tp = g.tr(ps[0:wd, i * P:i * P + rows], src[:, c:c + wd], self.ident[0:rows, 0:rows], *toks, *w)
        e = ("dve", "act")[self.nturn % 2]
        self.nturn += 1
        full = [i for i, (c, wd) in enumerate(widths) if wd == P]
        if full:
            n = len(full)
            tk = g.cp(dst[:, 0:n, 0:rows], ps[:, 0:n * P].rearrange("p (n r) -> p n r", n=n)[:, :, 0:rows], tp,
                      *wfree, e=e)
            out.append(tk)
        for i, (c, wd) in enumerate(widths):
            if wd != P:
                tk = g.cp(dst[0:wd, i, 0:rows], ps[0:wd, i * P:i * P + rows], tp, *wfree, e=e)
                out.append(tk)
        g.free(b, *out)
        return out

    nsm = 0
    nturn = 0

    def linear(self, name, j0, n, src, toks, T, k=8):
        g = self.g
        for j in range(n):
            if j % 2 == 0:
                i, w, t = self.colunit(name, (j0 + j) // 2, k)
            c = (j % 2) * P
            b, ps, wt = g.bank()
            for kk in range(k):
                tp = g.mm(ps[:, 0:T], [(w[:, kk, c:c + P], src[:, kk, 0:T])], t, toks[kk], *wt,
                          first=kk == 0, final=kk == k - 1, inc=kk == k - 1)
            if j % 2 or j == n - 1:
                g.free_unit(i, tp)
            yield j, b, ps, tp

    def proj_out(self, name, src, toks):
        return self.down(name, src, toks, self.T, 8)

    def nsa(self):
        g, A = self.g, self.A
        at = [0]

        def buf(n, *shape):
            v = A[:, at[0]:at[0] + n]
            at[0] += n
            if shape:
                names = "abcd"[:len(shape)]
                v = v.rearrange("p (%s) -> p %s" % (" ".join(names), " ".join(names)), **dict(zip(names, shape)))
            return v

        qT = buf(4 * T1, 4, T1)
        kD = {s: buf(2 * T1, 2, T1) for s in ("ks", "kw")}
        kp = {s: buf(2 * T1, 2, T1) for s in ("kc", "vc")}
        V = buf(2 * T1, 2, T1)
        gate = buf(2 * 24, 2, 8, 3)
        z = buf(4 * 258, 4, 258)
        cb = buf(4 * T1, 4, T1)
        hid = buf(64, 2, 2, 16)
        kcT = buf(16 * 2, 2, 16)
        vc2 = buf(2 * 64, 2, 64)
        S1 = buf(8 * T1, 8, T1)
        S2 = buf(8 * T1, 8, T1)
        S3 = buf(8 * 16, 8, 16)
        PT = buf(2 * 5 * P, 2, 5, P)
        mix = self.sq
        ht = self.prenorm("l0_mix_pre_g")
        src = self.hT
        g.wait("act", [("pe", g.n["pe"])])
        g.wait("dve", [("pe", g.n["pe"])])

        tq = [None] * 4
        cu = {}
        for j, b, ps, tp in self.linear("nsa_in", 0, 20, src, ht, T1):
            if j < 4:
                tk = g.act(qT[:, j, :], ps[:, 0:T1], ACT.Copy, tp, scale=0.125)
                tq[j] = tk
            elif j < 6:
                s = ("kc", "vc")[j - 4]
                for i in range(2):
                    rows = ps[64 * i:64 * i + 64, :]
                    g.cp(kp[s][0:64, i, 0:T1], rows[:, 0:T1], tp)
                    tk = g.cp(kp[s][64:128, i, 0:T1 - 1], rows[:, 1:T1], tp)
                tkp = tk
            elif j < 8:
                s = ("ks", "kw")[j - 6]
                for i in range(2):
                    rows = ps[64 * i:64 * i + 64, 0:T1]
                    g.cp(kD[s][0:64, i, :], rows, tp, e="act")
                    tk = g.cp(kD[s][64:128, i, :], rows, tp, e="act")
                tkd = tk
            elif j < 12:
                tk = g.cp(cb[:, j - 8, :], ps[:, 0:T1], tp, e="act")
                cu[j - 8] = tk
            elif j < 16:
                if j == 12:
                    tz = g.op("dve", lambda: self.g.nc.vector.memset(z[:, :, 0:2], 0.0))
                tk = g.cp(z[:, j - 12, 2:258], ps[:, 0:T1], tp)
            else:
                c = j - 16
                tk = g.tt(z[:, c, 2:258], z[:, c, 2:258], ps[:, 0:T1], ALU.mult, tp, tz)
                g.free(b, tk)
                i, t, tf = self.gettmp()
                t = t[:, 0:T1]
                w = [self.col("l0_conv_w", r * 4 + c) for r in range(3)]
                tk = g.ts(t, z[:, c, 2:258], w[2], self.col("l0_conv_b", c), ALU.mult, ALU.add, tk, tf)
                tk = g.stt(t, z[:, c, 1:257], w[1], t, ALU.mult, ALU.add, tk)
                tk = g.stt(t, z[:, c, 0:256], w[0], t, ALU.mult, ALU.add, tk)
                tconv = g.tt(mix[:, 4 + c, 0:T1], t, cb[:, c, :], ALU.mult, tk, cu[c])
                self.tmp_free[i] = tconv
                continue
            g.free(b, tk)
        i, w, t = self.colunit("nsa_v", 0)
        for m in range(2):
            b, ps, wt = g.bank()
            tp = g.mm(ps[:, 0:256], [(src[:, k, m * P:(m + 1) * P], w[:, k, :]) for k in range(8)], t, *wt)
            tv = g.cp(V[:, m, :], ps[:, 0:256], tp)
            g.free(b, tv)
        g.free_unit(i, tp)
        i, (w, w2), t = g.unit((0, 192, 0, P, self.d["nsa_g"]), (256, 128, 0, P, self.d["cmp_w2"]))
        w = w.rearrange("p (k n) -> p k n", k=8)
        b, ps, wt = g.bank()
        for m in range(2):
            tp = g.mm(ps[:, m * 24:m * 24 + 24], [(src[:, k, m * P:(m + 1) * P], w[:, k, :]) for k in range(8)], t,
                      *wt)
        tg = g.act(gate.rearrange("p a b c -> p (a b c)"), ps[:, 0:48], ACT.Sigmoid, tp)
        g.free(b, tg)
        for s, name in enumerate(("kc", "vc")):
            i2, (w1,), t1 = g.unit((0, SLOT, 0, P, self.d["cmp_w1_" + "kv"[s]]))
            w1 = w1.rearrange("p (j n) -> p j n", j=16)
            b, ps, wt = g.bank()
            pe_at = COLS["l0_cmp_pe_" + "kv"[s]][0]
            tp = g.mm(ps[:, 64:65], [(w1[:, j, :], self.cols[:, pe_at + j:pe_at + j + 1]) for j in range(16)], t1, *wt)
            pb = self.small[:, 256 + s:257 + s]
            tb = g.cp(pb, ps[:, 64:65], tp)
            b2, ps2, wt = g.bank()
            for gr in range(2):
                tp = g.mm(ps2[:, gr * 16:gr * 16 + 15],
                          [(w1[:, j, :], kp[name][:, gr, 2 * j:2 * j + 16 * 14 + 1:16]) for j in range(16)], tkp, *wt)
            g.free(b, tb)
            g.free_unit(i2, tp)
            for gr in range(2):
                th = g.act(hid[:, s, gr, 0:15], ps2[:, gr * 16:gr * 16 + 15], ACT.Gelu_apprx_tanh, tp, tb, bias=pb)
            g.free(b2, th)
            b, ps, wt = g.bank()
            if s == 0:
                for gr in range(2):
                    tp = g.mm(ps[0:64, gr * 16:gr * 16 + 15], [(w2[:, 0:64], hid[:, s, gr, 0:15])], th, *wt)
                g.cp(kcT[0:64, :, 0:15], ps[0:64, 0:32].rearrange("p (a b) -> p a b", a=2)[:, :, 0:15], tp)
                tkc = g.cp(kcT[64:128, :, 0:15], ps[0:64, 0:32].rearrange("p (a b) -> p a b", a=2)[:, :, 0:15], tp)
            else:
                for gr in range(2):
                    tp = g.mm(ps[0:15, gr * 64:gr * 64 + 64], [(hid[:, s, gr, 0:15], w2[:, 64:128])], th, *wt)
                tkc = g.cp(vc2[0:15, :, :], ps[0:15, 0:128].rearrange("p (a b) -> p a b", a=2), tp)
            g.free(b, tkc)
        g.free_unit(i, tp)

        pt_free = [None, None]
        so = None
        for m in range(2):
            nk = P * (m + 1)
            last = []
            for h in range(8):
                o = 64 * (h % 2)
                q = qT[o:o + 64, h // 2, m * P:(m + 1) * P]
                b, ps, wt = g.bank()
                for x, s in enumerate(("ks", "kw")):
                    tp = g.mm(ps[:, x * 256:x * 256 + nk], [(q, kD[s][o:o + 64, h // 4, 0:nk])], tkd, tq[h // 2],
                              tkp, *wt)
                for x, S in enumerate((S1, S2)):
                    tk = g.stt(S[:, h, 0:nk], self.c("alibi")[:, m * 256:m * 256 + nk], 0.5 ** (h + 1),
                               ps[:, x * 256:x * 256 + nk], ALU.mult, ALU.add, tp, so)
                g.free(b, tk)
                b, ps, wt = g.bank()
                tp = g.mm(ps[:, 0:15], [(q, kcT[o:o + 64, h // 4, 0:15])], tkc, *wt)
                tk = g.stt(S3[:, h, 0:15], self.c("alibi_cmp")[:, m * 16:m * 16 + 15], 0.5 ** (h + 1),
                           ps[:, 0:15], ALU.mult, ALU.add, tp, so)
                g.free(b, tk)
            t1 = self.softmax(S1[:, :, 0:nk], 8, nk, P, [tk], gate=gate[:, m, :, 1])
            t2 = self.softmax(S2[:, :, 0:nk], 8, nk, P, [tk], gate=gate[:, m, :, 2])
            t3 = self.softmax(S3[:, :, 0:15], 8, 15, P, [tk], gate=gate[:, m, :, 0], floor=True)
            for h in range(8):
                gr = h // 4
                o = 64 * (h % 2)
                pt = PT[:, h % 2]
                wf = (pt_free[h % 2],)
                ta = self.turn(pt[:, 0:2], S1[:, h, :], P, [(c * P, P) for c in range(m + 1)], [t1, tg], wf)
                tb = self.turn(pt[:, 2:4], S2[:, h, :], P, [(c * P, P) for c in range(m + 1)], [t2], wf)
                tc = self.turn(pt[:, 4:5], S3[:, h, 0:15], P, [(0, 15)], [t3], wf)
                if h % 2 == 0:
                    bo, po, wt = g.bank()
                pairs = []
                for c in range(m + 1):
                    pairs.append((V[:, c, gr * 64:gr * 64 + 64], pt[:, c, :]))
                    pairs.append((V[:, c, P + gr * 64:P + gr * 64 + 64], pt[:, 2 + c, :]))
                pairs.append((vc2[0:15, gr, :], pt[0:15, 4, :]))
                so = g.mm(po[o:o + 64, 0:P], pairs, tv, tkc, *ta, *tb, *tc, *wt)
                pt_free[h % 2] = so
                if h % 2:
                    tk = g.cp(mix[:, h // 2, m * P:(m + 1) * P], po[:, 0:P], so, e="act")
                    g.free(bo, tk)
        banks = self.proj_out("nsa_out", mix, [tk] * 4 + [tconv] * 4)
        self.postnorm(banks, "l0_mix_post_g", 0, False)

    def tokmajor(self, name, src, toks, extra=None, n_units=4):
        g = self.g
        banks = [[g.bank() for _ in range(2)] for _ in range(2)]
        for u in range(n_units):
            i, w, t = self.rowunit(name, u)
            for kk in range(2):
                k = 2 * u + kk
                for m in range(2):
                    for h in range(2):
                        b, ps, wt = banks[m][h]
                        fin = k == 7
                        tk = g.mm(ps[:, :], [(src[:, k, m * P:(m + 1) * P], w[:, kk, h * 512:(h + 1) * 512])], t,
                                  toks[k], *wt, first=k == 0, final=fin, inc=fin or (kk == 1 and m == 1 and h == 1))
                        if fin:
                            banks[m][h] = (b, ps, tk)
            g.free_unit(i, ("pe", g.n["pe"]))
        return banks

    def rwkv(self):
        g, A, nc = self.g, self.A, self.g.nc
        C0 = float(np.exp(np.float64(-0.5)))
        v3 = lambda o: A[:, o:o + 2048].rearrange("p (m c) -> p m c", m=2)
        r, k, v, a, lw, gt = [v3(2048 * i) for i in range(6)]
        kk = self.hT.rearrange("p k t -> p (k t)")[:, 0:2048].rearrange("p (m c) -> p m c", m=2)
        W = 12288
        xx = A[:, W:W + 2048].rearrange("p (k t) -> p k t", k=8)
        xm = [self.yT, A[:, W + 2048:W + 4096].rearrange("p (k t) -> p k t", k=8)]
        ht = self.prenorm("l1_mix_pre_g")
        hT = self.hT
        g.ts(xx[:, :, 0:1], hT[:, :, 0:1], -1.0, None, ALU.mult, None, *ht)
        txx = g.tt(xx[:, :, 1:T1], hT[:, :, 0:T1 - 1], hT[:, :, 1:T1], ALU.subtract, *ht)
        xfree = [("pe", g.n["pe"]), None]
        count = [0]

        def mixed(i):
            n = count[0] % 2
            count[0] += 1
            toks = [g.stt(xm[n][:, q, 0:T1], xx[:, q, :], self.col("l1_mu", i * 8 + q), hT[:, q, 0:T1],
                          ALU.mult, ALU.add, txx, xfree[n]) for q in range(8)]
            return n, xm[n], toks

        il, (lora,), tl = g.unit((0, SLOT, 0, P, self.d["lora1"]))
        lora = lora.rearrange("p (k n) -> p k n", k=8)
        lT = A[:, W + 4096:W + 4096 + 768].rearrange("p (j t) -> p j t", j=3)
        tlo = []
        for j, (i, c0, w, f) in enumerate(((1, 0, 64, ACT.Tanh), (4, 64, 64, ACT.Copy), (5, 128, 128, ACT.Sigmoid))):
            n, x, toks = mixed(i)
            b, ps, wt = g.bank()
            for q in range(8):
                tp = g.mm(ps[0:w, 0:T1], [(lora[:, q, c0:c0 + w], x[:, q, 0:T1])], tl, toks[q], *wt,
                          first=q == 0, final=q == 7, inc=q == 7)
            xfree[n] = tp
            tk = g.act(lT[0:w, j, :], ps[0:w, 0:T1], f, tp)
            g.free(b, tk)
            tlo.append(tk)
        g.free_unit(il, tp)
        i2, (g2,), t2 = g.unit((0, 1024, 0, P, self.d["l1_w_g2"]))
        ib, (wa,), tb = g.unit((0, 2048, 0, 65, self.d["lora2"]))
        tone = g.op("dve", lambda: nc.vector.memset(lT[64:65, 0:2, :], 1.0))
        for j, dst in ((0, lw), (1, a), (2, gt)):
            for m in range(2):
                for h in range(2):
                    b, ps, wt = g.bank()
                    x = lT[:, j, m * P:(m + 1) * P]
                    hs = slice(h * 512, (h + 1) * 512)
                    if j == 2:
                        tp = g.mm(ps[:, :], [(x, g2[:, hs])], t2, tlo[j], *wt)
                        tk = g.cp(dst[:, m, hs], ps[:, :], tp)
                    else:
                        tp = g.mm(ps[:, :], [(x[0:65], wa[0:65, j * 1024 + h * 512:j * 1024 + h * 512 + 512])],
                                  tb, tlo[j], tone, *wt)
                        tk = g.act(dst[:, m, hs], ps[:, :], ACT.Sigmoid, tp)
                    g.free(b, tk)
        g.free_unit(i2, tp)
        g.free_unit(ib, tp)
        for i, name, dst in ((0, "l1_w_r", r), (2, "l1_w_k", k), (3, "l1_w_v", v)):
            n, x, toks = mixed(i)
            banks = self.tokmajor(name, x, toks)
            xfree[n] = ("pe", g.n["pe"])
            for m in range(2):
                for h in range(2):
                    b, ps, tp = banks[m][h]
                    tk = g.cp(dst[:, m, h * 512:(h + 1) * 512], ps[:, :], tp, e=("dve", "act")[h])
                    g.free(b, tk)
        g.fence()
        iv, (kkg, kag), tv = g.unit((0, 1024, 0, P, self.d["l1_k_k"].broadcast_to([P, 1024])),
                                    (1024, 1024, 0, P, self.d["l1_k_a"].broadcast_to([P, 1024])))
        iw, (rkg,), tw = g.unit((0, 1024, 0, P, self.d["l1_r_k"].broadcast_to([P, 1024])))
        s16 = self.small
        bonus = s16[:, 256:288].rearrange("p (m h) -> p m h", m=2)
        sc = self.yT.rearrange("p k t -> p (k t)")[:, 0:2048].rearrange("p (m c) -> p m c", m=2)
        h3 = lambda ap: ap.rearrange("p (h j) -> p h j", h=16)
        for m in range(2):
            t = g.tt(kk[:, m, :], k[:, m, :], kkg, ALU.mult, tv)
            t = g.act(sc[:, m, :], kk[:, m, :], ACT.Square, t)
            ss = s16[:, 16 * m:16 * m + 16]
            t = g.red(ss, h3(sc[:, m, :]), ALU.add, t)
            t = g.ts(ss, ss, 1e-12, None, ALU.max, None, t)
            t = g.recip(ss, ss, t)
            t = g.act(ss, ss, ACT.Sqrt, t)
            g.tt(h3(kk[:, m, :]), h3(kk[:, m, :]), bc(ss, 64), ALU.mult, t)
            t = g.stt(sc[:, m, :], a[:, m, :], -1.0, kag, ALU.add, ALU.mult)
            t = g.stt(k[:, m, :], sc[:, m, :], 1.0, k[:, m, :], ALU.add, ALU.mult, t)
            tk1 = g.tt(a[:, m, :], a[:, m, :], kk[:, m, :], ALU.mult)
            t = g.tt(sc[:, m, :], r[:, m, :], k[:, m, :], ALU.mult, t)
            t = g.tt(sc[:, m, :], sc[:, m, :], rkg, ALU.mult, t, tw)
            tbo = g.red(bonus[:, m, :], h3(sc[:, m, :]), ALU.add, t)
        g.free_unit(iv, tbo)
        g.free_unit(iw, tbo)
        g.fence()
        ig, (lng, lnb), tln = g.unit((0, 1024, 0, P, self.d["l1_lnx_g"].broadcast_to([P, 1024])),
                                     (1024, 1024, 0, P, self.d["l1_lnx_b"].broadcast_to([P, 1024])))
        pos = [W]

        def buf(n):
            x = A[:, pos[0]:pos[0] + n]
            pos[0] += n
            assert pos[0] <= 20800
            return x

        vec = buf(1536).rearrange("p (i c) -> p i c", i=6)
        ART = buf(1024).rearrange("p (h i t) -> p h i t", h=4, i=2)
        BK = buf(1024).rearrange("p (i h t) -> p i h t", i=2, h=4)
        M4 = buf(2048).rearrange("p (h c) -> p h c", h=4)
        Tm = buf(512).rearrange("p (h c) -> p h c", h=4)
        Tt = buf(512).rearrange("p (h c) -> p h c", h=4)
        Wm = buf(512).rearrange("p (h c) -> p h c", h=4)
        Mb = buf(512).rearrange("p (h c) -> p h c", h=4)
        fl = self.yT.rearrange("p k t -> p (k t)")
        ex = self.tmp.rearrange("p k t -> p (k t)")[:, 0:1024].rearrange("p (i c) -> p i c", i=4)
        pc = s16[0:64, 320:328].rearrange("p (h c) -> p h c", h=4)
        MV = fl[:, 0:256]
        TMV = fl[:, 256:512]
        U = fl[:, 512:768]
        Y1 = fl[:, 768:1024]
        TAT = fl[0:64, 1024:1536].rearrange("p (h t) -> p h t", h=4)
        ST = self.sq_[0:64, 0:1024].rearrange("p (h i) -> p h i", h=16)
        tst = g.op("dve", lambda: nc.vector.memset(ST, 0.0))
        m64 = self.c("m64")
        ty = None
        for m in range(2):
            for hg in range(4):
                cs = slice(hg * 256, hg * 256 + 256)
                hs = [slice(hg * 256 + 64 * h, hg * 256 + 64 * h + 64) for h in range(4)]
                l = lw[:, m, cs]
                pe0 = ("pe", g.n["pe"])
                b1, p1, w1 = g.bank()
                g.mm(p1[:, 0:256], [(m64[:, 0:128], l)], *w1, inc=False)
                t1 = g.mm(p1[:, 256:512], [(m64[:, 128:256], l)])
                b2, p2, w2 = g.bank()
                g.mm(p2[:, 0:256], [(self.c("suf64"), l)], *w2, inc=False)
                for h in range(4):
                    t2 = g.mm(p2[0:64, 256 + 2 * h:258 + 2 * h], [(lw[:, m, hs[h]], self.c("chunk"))])
                t = g.act(ex[:, 0:2, :], p1[:, :].rearrange("p (i c) -> p i c", i=2), ACT.Exp, t1, pe0, ty, scale=-C0)
                ta = g.act(ex[:, 2, :], p1[:, 256:512], ACT.Exp, t1, scale=C0)
                tb = g.act(ex[:, 3, :], p2[:, 0:256], ACT.Exp, t2, scale=-C0)
                tc = g.act(pc, p2[0:64, 256:264].rearrange("p (h c) -> p h c", h=4), ACT.Exp, t2, scale=-C0)
                g.free(b1, ta)
                g.free(b2, tc)
                tv_ = []
                for i, (x, e) in enumerate(((kk, 0), (r, 1), (a, 2), (k, 2), (a, 3), (k, 3))):
                    tv_.append(g.tt(vec[:, i, :], x[:, m, cs], ex[:, e, :], ALU.mult, t, ta, tb, pe0,
                                    e="pool" if i > 3 else "dve"))
                for i in range(4):
                    b, ps, w = g.bank()
                    for h in range(4):
                        tp = g.tr(ps[0:64, h * P:(h + 1) * P], vec[:, i, 64 * h:64 * h + 64], self.ident, tv_[i], *w)
                    dst = ART[0:64, :, i, :] if i < 2 else BK[0:64, i - 2, :, :]
                    tt_ = g.cp(dst, ps[0:64, :].rearrange("p (h t) -> p h t", h=4), tp, e=("dve", "act")[i % 2])
                    g.free(b, tt_)
                    if i == 2:
                        tA = tt_
                tm = []
                for h in range(4):
                    b, ps, w = g.bank()
                    rhs = ART[0:64, h].rearrange("p i t -> p (i t)")
                    g.mm(ps[:, 0:256], [(BK[0:64, 0, h, :], rhs)], tt_, tA, *w, inc=False)
                    tp = g.mm(ps[:, 256:512], [(BK[0:64, 1, h, :], rhs)])
                    tk = g.tt(M4[:, h, :].rearrange("p (i c) -> p i c", i=2),
                              ps[:, :].rearrange("p (i c) -> p i c", i=2), bc_mid(m64, 2), ALU.mult, tp)
                    g.free(b, tk)
                for lv in range(6):
                    mask = self.c("level", lv)
                    tmb = g.tt(Mb, M4[:, :, 0:128], bc_mid(mask, 4), ALU.mult, tk, ("pe", g.n["pe"]))
                    idb = bc_mid(self.ident, 4)
                    b, ps, w = g.bank()
                    for h in range(4):
                        rhs = self.ident if lv == 0 else Tm[:, h, :]
                        tp = g.mm(ps[:, h * P:(h + 1) * P], [(Mb[:, h, :], rhs)], tmb, *w, inc=h == 3)
                    p4 = lambda x: x[:, :].rearrange("p (h c) -> p h c", h=4)
                    if lv == 0:
                        g.tt(Tm, idb, p4(ps), ALU.subtract, tp)
                        tk = g.tt(Tt, idb, Mb, ALU.subtract, tmb)
                        g.free(b, tk)
                        continue
                    tw_ = g.cp(Wm, p4(ps), tp, e="act")
                    g.free(b, tw_)
                    if lv < 5:
                        b, ps, w = g.bank()
                        for h in range(4):
                            tp = g.mm(ps[:, h * P:(h + 1) * P], [(Tt[:, h, :], Wm[:, h, :])], tw_, tk, *w, inc=h == 3)
                        g.free(b, g.tt(Tm, Tm, p4(ps), ALU.subtract, tp))
                    b, ps, w = g.bank()
                    for h in range(4):
                        tp = g.mm(ps[:, h * P:(h + 1) * P], [(Wm[:, h, :], Tt[:, h, :])], tw_, tk, *w, inc=h == 3)
                    tk = g.tt(Tt, Tt, p4(ps), ALU.subtract, tp)
                    g.free(b, tk)
                b, ps, w = g.bank()
                for h in range(4):
                    tp = g.mm(ps[:, 64 * h:64 * h + 64], [(M4[:, h, 256:384], v[:, m, hs[h]])], *w)
                t = g.cp(MV, ps[:, 0:256], tp, e="act")
                g.free(b, t)
                b, ps, w = g.bank()
                for h in range(4):
                    tp = g.mm(ps[:, 64 * h:64 * h + 64], [(Tt[:, h, :], MV[:, 64 * h:64 * h + 64])], t, tk, *w)
                tmv = g.cp(TMV, ps[:, 0:256], tp, e="act")
                g.free(b, tmv)
                b, ps, w = g.bank()
                for h in range(4):
                    tp = g.mm(ps[0:64, h * P:(h + 1) * P], [(vec[:, 0, 64 * h:64 * h + 64], Tt[:, h, :])], *w)
                tat = g.cp(TAT, ps[0:64, :].rearrange("p (h t) -> p h t", h=4), tp)
                g.free(b, tat)
                by, py, wy = g.bank()
                for c in range(2):
                    o = 64 * c
                    b, ps, w = g.bank()
                    for h in range(4):
                        st = ST[:, hg * 4 + h, :]
                        tp = g.mm(ps[o:o + 64, 64 * h:64 * h + 64], [(TAT[:, h, o:o + 64], st)], tst, tat, *w)
                    for h in range(4):
                        st = ST[:, hg * 4 + h, :]
                        ty = g.mm(py[o:o + 64, 64 * h:64 * h + 64], [(ART[0:64, h, 1, o:o + 64], st)], *wy)
                    tu = g.stt(U[o:o + 64, :], ps[o:o + 64, 0:256], -1.0, TMV[o:o + 64, :], ALU.mult, ALU.subtract,
                               tp, tmv)
                    g.free(b, tu)
                    b, ps, w = g.bank()
                    for h in range(4):
                        hh = slice(64 * h, 64 * h + 64)
                        tp = g.mm(ps[0:64, hh], [(vec[o:o + 64, 4, hh], U[o:o + 64, hh]),
                                                 (vec[o:o + 64, 5, hh], v[o:o + 64, m, hs[h]])], tu, tv_[5], *w)
                    sg = ST[:, hg * 4:hg * 4 + 4, :]
                    t = g.tt(sg, sg, bc(pc[:, :, c], 64), ALU.mult, ty, tc)
                    tst = g.tt(sg, sg, ps[0:64, 0:256].rearrange("p (h i) -> p h i", h=4), ALU.add, t, tp)
                    g.free(b, tst)
                t = g.cp(Y1, py[:, 0:256], ty, e="act")
                g.free(by, t)
                b, ps, w = g.bank()
                for h in range(4):
                    hh = slice(64 * h, 64 * h + 64)
                    tp = g.mm(ps[:, hh], [(M4[:, h, 128:256], U[:, hh]), (M4[:, h, 384:512], v[:, m, hs[h]])], tu, *w)
                ty = g.tt(r[:, m, cs], Y1, ps[:, 0:256], ALU.add, tp, t)
                g.free(b, ty)
        g.fence()
        mu = s16[:, 0:32].rearrange("p (m h) -> p m h", m=2)
        var = s16[:, 32:64].rearrange("p (m h) -> p m h", m=2)
        ty = []
        for m in range(2):
            y, s = r[:, m, :], sc[:, m, :]
            t = g.red(mu[:, m, :], h3(y), ALU.add)
            t = g.ts(mu[:, m, :], mu[:, m, :], 1.0 / 64, None, ALU.mult, None, t)
            t = g.tt(h3(y), h3(y), bc(mu[:, m, :], 64), ALU.subtract, t)
            t = g.act(s, y, ACT.Square, t)
            t = g.red(var[:, m, :], h3(s), ALU.add, t)
            t = g.ts(var[:, m, :], var[:, m, :], 1.0 / 64, 64e-5, ALU.mult, ALU.add, t)
            t = g.recip(var[:, m, :], var[:, m, :], t)
            t = g.act(var[:, m, :], var[:, m, :], ACT.Sqrt, t)
            tp = g.tt(h3(v[:, m, :]), h3(v[:, m, :]), bc(bonus[:, m, :], 64), ALU.mult, e="pool")
            t = g.tt(h3(y), h3(y), bc(var[:, m, :], 64), ALU.mult, t)
            t = g.tt(y, y, lng, ALU.mult, t, tln)
            t = g.tt(y, y, lnb, ALU.add, t)
            t = g.tt(y, y, v[:, m, :], ALU.add, t, tp)
            ty.append(g.tt(y, y, gt[:, m, :], ALU.mult, t))
        g.free_unit(ig, ty[1])
        toks = self.turn_back(r, ty, self.hT)
        banks = self.proj_out("l1_w_o", self.hT, toks)
        self.postnorm(banks, "l1_mix_post_g", 0, False)

    def turn_back(self, y, ty, dst, scale=None):
        g = self.g
        toks = []
        for q in range(8):
            b, ps, w = g.bank()
            for m in range(2):
                tp = g.tr(ps[:, m * P:(m + 1) * P], y[:, m, q * P:(q + 1) * P], self.ident, ty[m], *w)
            if scale is not None:
                tk = g.act(dst[:, q, 0:T1], ps[:, 0:T1], ACT.Copy, tp, scale=self.col(scale, q))
            else:
                tk = g.cp(dst[:, q, 0:T1], ps[:, 0:T1], tp, e=("dve", "act")[q % 2])
            g.free(b, tk)
            toks.append(tk)
        return toks
    def carve(self, start, limit=20800):
        pos = [start]

        def buf(n, *shape):
            v = self.A[:, pos[0]:pos[0] + n]
            pos[0] += n
            assert pos[0] <= limit, pos[0]
            if shape:
                names = "abcd"[:len(shape)]
                v = v.rearrange("p (%s) -> p %s" % (" ".join(names), " ".join(names)), **dict(zip(names, shape)))
            return v

        return buf

    def softplus(self, x, t1, t2, *toks):
        g = self.g
        t = g.act(t1, x, ACT.Abs, *toks)
        t = g.act(t1, t1, ACT.Exp, t, scale=-1.0)
        t = g.act(t1, t1, ACT.Ln, t, bias=1.0)
        t = g.stt(x, x, 0.0, t1, ALU.max, ALU.add, t)
        return t

    def hybrid(self):
        g, nc = self.g, self.g.nc
        xT, xt = self.xT, self.xtok
        mem = self.carve(0)
        merged = mem(2048, 8, T1)
        fl = lambda v: v.rearrange("p k t -> p (k t)")
        buf = self.carve(2048)
        u = buf(4 * 260, 4, 260)
        xs = buf(2048, 8, T1)
        BC = buf(2048, 8, T1)
        xdt = buf(2048, 2, 1024)
        Bt = buf(512)
        xds = buf(1024)
        S0 = buf(1024)
        GL = buf(1024, 2, 4, P)
        CS = buf(1024, 2, 4, P)
        Gm = buf(256, 2, P)
        iw, (tw, kw), tt_ = g.unit((0, 256, 0, P, self.d["tokw"]), (256, 512, 0, P, self.d["kidx"]))
        tw = tw.rearrange("p (k n) -> p k n", k=8)
        kw = kw.rearrange("p (k n) -> p k n", k=8)
        s = self.small
        dt = s[:, 0:32].rearrange("p (m h) -> p m h", m=2)
        widx = s[:, 32:64].rearrange("p (m h) -> p m h", m=2)
        scr = s[:, 64:96].rearrange("p (m h) -> p m h", m=2)
        av = s[:, 96:128].rearrange("p (m h) -> p m h", m=2)
        acs = s[:, 128:160].rearrange("p (m h) -> p m h", m=2)
        dec = s[:, 160:176]
        ah = s[:, 176:192]
        rw = lambda n: self.rows[:, ROWS[n][0]:ROWS[n][0] + 16]
        ki = buf(T1)
        b, ps, w = g.bank()
        for m in range(2):
            tp = g.mm(ps[:, 32 * m:32 * m + 32], [(xT[:, k, m * P:(m + 1) * P], tw[:, k, :]) for k in range(8)], tt_,
                      *w, *xt)
        ps2 = ps[:, 0:64].rearrange("p (m n) -> p m n", m=2)
        t = g.tt(dt, ps2[:, :, 0:16], bc_mid(rw("dt_bias_2"), 2), ALU.add, tp)
        tw_ = g.ts(widx, ps2[:, :, 16:32], 0.25, None, ALU.mult, None, tp)
        g.free(b, tw_)
        b, ps, w = g.bank()
        tp = g.mm(ps[0:64, 0:T1], [(kw[:, k, :], xT[:, k, 0:T1]) for k in range(8)], *w)
        g.free_unit(iw, tp)
        g.cp(ki[0:64, :], ps[0:64, 0:T1], tp, e="act")
        tki = g.cp(ki[64:128, :], ps[0:64, 0:T1], tp, e="act")
        g.free(b, tki)
        t = self.softplus(dt, scr, None, t)
        ta = g.act(ah, rw("a_log_2"), ACT.Exp)
        ta = g.ts(ah, ah, -1.0, None, ALU.mult, None, ta)
        ta = g.tt(av, dt, bc_mid(ah, 2), ALU.mult, ta, t)
        b, ps, w = g.bank()
        for m in range(2):
            tp = g.mm(ps[:, 16 * m:16 * m + 16], [(self.c("tri128"), av[:, m, :])], ta, *w)
        tp = g.mm(ps[:, 32:48], [(self.c("suf128"), av[:, 0, :])])
        tacs = g.cp(acs, ps[:, 0:32].rearrange("p (m h) -> p m h", m=2), tp)
        tdec = g.act(dec, ps[:, 32:48], ACT.Exp, tp, tacs)
        g.free(b, tdec)
        tz = g.op("dve", lambda: nc.vector.memset(u[:, :, 0:3], 0.0))
        ufree = [None] * 4
        txb = [None] * 16
        for j, b, ps, tp in self.linear("xbc", 0, 16, xT, xt, T1):
            uu = u[:, j % 4, :]
            t = g.cp(uu[:, 3:259], ps[:, 0:T1], tp, ufree[j % 4], e="act")
            g.free(b, t)
            i, v, tf = self.gettmp()
            v = v[:, 0:T1]
            wc = [self.col("conv_w_2", r * 16 + j) for r in range(4)]
            t = g.ts(v, uu[:, 3:259], wc[3], self.col("conv_b_2", j), ALU.mult, ALU.add, t, tf)
            for r in (2, 1, 0):
                t = g.stt(v, uu[:, r:r + T1], wc[r], v, ALU.mult, ALU.add, t, tz)
            ufree[j % 4] = t
            dst = xs[:, j, :] if j < 8 else BC[:, j - 8, :]
            txb[j] = g.act(dst, v, ACT.Silu, t)
            self.tmp_free[i] = txb[j]
        BT, CT = BC[:, 0:4, :], BC[:, 4:8, :]
        for m in range(2):
            for hf in range(2):
                b, ps, w = g.bank()
                for q in range(4):
                    tp = g.tr(ps[:, q * P:(q + 1) * P], xs[:, 4 * hf + q, m * P:(m + 1) * P], self.ident,
                              txb[4 * hf + q], *w)
                txd = g.tt(xdt[:, m, hf * 512:(hf + 1) * 512].rearrange("p (h j) -> p h j", h=8),
                           ps[:, :].rearrange("p (h j) -> p h j", h=8), bc(dt[:, m, 8 * hf:8 * hf + 8], 64),
                           ALU.mult, tp)
                g.free(b, txd)
        b, ps, w = g.bank()
        for q in range(4):
            tp = g.tr(ps[:, q * P:(q + 1) * P], BT[:, q, 0:P], self.ident, txb[8 + q], *w)
        tbt = g.cp(Bt, ps[:, :], tp, e="act")
        g.free(b, tbt)
        txs = g.tt(xds.rearrange("p (h j) -> p h j", h=16), xdt[:, 0, :].rearrange("p (h j) -> p h j", h=16),
                   bc(dec, 64), ALU.mult, tdec, txd)
        for hf in range(2):
            b, ps, w = g.bank()
            for q in range(2):
                gr = 2 * hf + q
                tp = g.mm(ps[:, q * 256:(q + 1) * 256], [(Bt[:, gr * P:(gr + 1) * P], xds[:, gr * 256:(gr + 1) * 256])],
                          tbt, txs, *w)
            ts0 = g.cp(S0[:, hf * 512:(hf + 1) * 512], ps[:, :], tp, e="act")
            g.free(b, ts0)
        gfree = [None, None]
        yss = self.hT
        ty = [None] * 8
        n = 0
        for m in range(2):
            tc = slice(m * P, (m + 1) * P)
            for gr in range(4):
                i = n % 2
                n += 1
                b, ps, w = g.bank()
                tp = g.mm(ps[:, 0:P], [(BT[:, gr, tc], CT[:, gr, tc])], txb[8 + gr], txb[12 + gr], *w)
                tg = g.tt(Gm[:, i, :], ps[:, 0:P], self.c("tri128"), ALU.mult, tp, gfree[i])
                g.free(b, tg)
                b, ps, w = g.bank()
                for r in range(4):
                    h = 4 * gr + r
                    tp = g.mm(ps[:, r * P:(r + 1) * P], [(av[:, m, h:h + 1].broadcast_to([P, P]), self.c("tri128"))],
                              *w)
                for r in range(4):
                    h = 4 * gr + r
                    t = g.ts(GL[:, i, r, :], ps[:, r * P:(r + 1) * P], acs[:, m, h:h + 1], 0.0, ALU.subtract, ALU.min,
                             tp, tacs, gfree[i])
                if m:
                    tcs = g.act(CS[:, i], ps[:, :].rearrange("p (r t) -> p r t", r=4), ACT.Exp, tp, t, gfree[i])
                    tcs = g.tt(CS[:, i], CS[:, i], bc_mid(CT[:, gr, tc], 4), ALU.mult, tcs)
                    g.free(b, tcs)
                else:
                    tcs = None
                    g.free(b, t)
                t = g.act(GL[:, i], GL[:, i], ACT.Exp, t)
                tgl = g.tt(GL[:, i], GL[:, i], bc_mid(Gm[:, i, :], 4), ALU.mult, t, tg)
                for r in range(0, 4, 2):
                    b, ps, w = g.bank()
                    for h in (4 * gr + r, 4 * gr + r + 1):
                        o = 64 * (h % 2)
                        pairs = [(xdt[:, m, h * 64:h * 64 + 64], GL[:, i, h % 4, :])]
                        if m:
                            pairs.append((S0[:, h * 64:h * 64 + 64], CS[:, i, h % 4, :]))
                        tp = g.mm(ps[o:o + 64, 0:P], pairs, tgl, tcs, ts0, txd, *w)
                    q = 2 * gr + r // 2
                    ty[q] = g.stt(yss[:, q, tc], xs[:, q, tc], self.col("d_skip_2c", q), ps[:, 0:P], ALU.mult,
                                  ALU.add, tp)
                    g.free(b, ty[q])
                gfree[i] = tp
        for j, b, ps, tp in self.linear("z_2", 0, 8, xT, xt, T1):
            i, v, tf = self.gettmp()
            t = g.act(v[:, 0:T1], ps[:, 0:T1], ACT.Silu, tp, tf)
            g.free(b, t)
            ty[j] = g.tt(yss[:, j, 0:T1], yss[:, j, 0:T1], v[:, 0:T1], ALU.mult, t, ty[j])
            self.tmp_free[i] = ty[j]
            ts_ = g.act(self.sq[:, j, 0:T1], yss[:, j, 0:T1], ACT.Square, ty[j])
            if j % 2:
                b, ps, w = g.bank()
                tp = g.mm(ps[:, 0:T1], [(self.ones, self.sq[:, q, 0:T1]) for q in (j - 1, j)], ts_, *w)
                r_ = self.rstd[:, (j // 2) % 2, 0:T1]
                t = self.rsqrt(r_, ps[:, 0:T1], tp, 1.0 / 256, 1e-6, T1, b)
                for q in (j - 1, j):
                    ty[q] = g.stt(yss[:, q, 0:T1], yss[:, q, 0:T1], self.col("ssd_norm_w_2", q), r_, ALU.mult,
                                  ALU.mult, t)
        yt = self.evac8(self.down("w_proj_ssd_2", yss, ty, T1, 8), T1)
        tm = [None] * 8
        for j, b, ps, tp in self.linear("g_ssd", 0, 8, xT, xt, T1):
            t = g.act(merged[:, j, :], ps[:, 0:T1], ACT.Sigmoid, tp)
            g.free(b, t)
            tm[j] = g.tt(merged[:, j, :], merged[:, j, :], self.yT[:, j, 0:T1], ALU.mult, t, yt[j])
        g.fence()
        buf = self.carve(2048)
        qT = buf(2048, 8, T1)
        kT = buf(2048, 8, T1)
        V = buf(2048, 2, 1024)
        qi = buf(2048, 8, T1)
        S = buf(2048, 2, 4, T1)
        PT = buf(512, 2, 2, P)
        sc = buf(512, 2, T1)
        wk = buf(1024, 2, 2, T1)
        sel = buf(512, 2, T1)
        cT = buf(512, 2, T1)
        assert buf(1) is not None
        m8 = s[:, 448:464].rearrange("p (m h) -> p m h", m=2)
        tck = [None] * 2
        for j, b, ps, tp in self.linear("ckv", 0, 2, xT, xt, T1):
            tck[j] = g.cp(cT[:, j, :], ps[:, 0:T1], tp)
            g.free(b, tck[j])
        for j in range(2):
            t = g.act(self.sq[:, j, 0:T1], cT[:, j, :], ACT.Square, tck[j])
        b, ps, w = g.bank()
        tp = g.mm(ps[:, 0:T1], [(self.ones, self.sq[:, q, 0:T1]) for q in range(2)], t, *w)
        r_ = self.rstd[:, 0, 0:T1]
        t = self.rsqrt(r_, ps[:, 0:T1], tp, 1.0 / 256, 1e-6, T1, b)
        for q in range(2):
            tck[q] = g.stt(cT[:, q, :], cT[:, q, :], self.col("kv_norm_w_2", q), r_, ALU.mult, ALU.mult, t)
        tq = []
        for j, b, ps, tp in self.linear("qidx", 0, 8, xT, xt, T1):
            tq.append(g.cp(qi[:, j, :], ps[:, 0:T1], tp, e="act"))
            g.free(b, tq[j])
        for m in range(2):
            nk = P * (m + 1)
            for h in range(16):
                o = 64 * (h % 2)
                b, ps, w = g.bank()
                tp = g.mm(ps[:, 0:nk], [(qi[o:o + 64, h // 2, m * P:(m + 1) * P], ki[o:o + 64, 0:nk])], tq[h // 2],
                          tki, *w)
                i, v, tf = self.gettmp()
                t = g.act(v[:, 0:nk], ps[:, 0:nk], ACT.Relu, tp, tf)
                g.free(b, t)
                if h == 0:
                    ta = g.ts(sc[:, m, 0:nk], v[:, 0:nk], widx[:, m, h:h + 1], None, ALU.mult, None, t)
                else:
                    ta = g.stt(sc[:, m, 0:nk], v[:, 0:nk], widx[:, m, h:h + 1], sc[:, m, 0:nk], ALU.mult, ALU.add, t)
                self.tmp_free[i] = ta
        tqq, tkk = [], []
        for j, b, ps, tp in self.linear("q_2", 0, 8, xT, xt, T1):
            tqq.append(g.act(qT[:, j, :], ps[:, 0:T1], ACT.Copy, tp, scale=0.125))
            g.free(b, tqq[j])
        for n in range(1):
            i, (wk_,), t = g.unit((0, SLOT, 0, P, self.d["w_uk"]))
            wk_ = wk_.rearrange("p (r n) -> p r n", r=2)
            for j in range(8):
                b, ps, w = g.bank()
                tp = g.mm(ps[:, 0:T1], [(wk_[:, r, j * P:(j + 1) * P], cT[:, r, :]) for r in range(2)], t, *tck, *w)
                tkk.append(g.cp(kT[:, j, :], ps[:, 0:T1], tp, e="act"))
                g.free(b, tkk[j])
            g.free_unit(i, tp)
            i, (wv_,), t = g.unit((0, SLOT, 0, P, self.d["w_uv"]))
            wv_ = wv_.rearrange("p (r n) -> p r n", r=2)
            for m in range(2):
                for h in range(2):
                    b, ps, w = g.bank()
                    tp = g.mm(ps[:, :], [(cT[:, r, m * P:(m + 1) * P], wv_[:, r, h * 512:(h + 1) * 512])
                                         for r in range(2)], t, *w)
                    tvv = g.cp(V[:, m, h * 512:(h + 1) * 512], ps[:, :], tp, e="act")
                    g.free(b, tvv)
            g.free_unit(i, tp)
        for m in range(2):
            nk = P * (m + 1)
            al = self.c("alibi")[:, m * 256:m * 256 + nk]
            t = g.ts(sel[:, m, 0:nk], al, -1e29, BIG, ALU.is_lt, ALU.mult)
            cur = sc[:, m, 0:nk]
            t = g.tt(cur, cur, sel[:, m, 0:nk], ALU.add, t)
            for r in range(8):
                nx = wk[:, m, r % 2, 0:nk]
                t = g.op("dve", lambda o=m8[:, m, :], c=cur: nc.vector.max(o, c), t)
                t = g.op("dve", lambda o=nx, v=m8[:, m, :], c=cur: nc.vector.match_replace(o, v, c, -3e38), t)
                cur = nx
            t = g.ts(sel[:, m, 0:nk], cur, -2e38, BIG, ALU.is_gt, ALU.mult, t)
            tsel = g.tt(sel[:, m, 0:nk], sel[:, m, 0:nk], al, ALU.add, t)
        oT = self.hT
        ptf, sfree = [None, None], [None, None]
        n = 0
        to = [None] * 8
        for m in range(2):
            nk = P * (m + 1)
            for h0 in range(0, 16, 4):
                SS = S[:, n % 2]
                for r in range(4):
                    h = h0 + r
                    o = 64 * (h % 2)
                    b, ps, w = g.bank()
                    tp = g.mm(ps[:, 0:nk], [(qT[o:o + 64, h // 2, m * P:(m + 1) * P], kT[o:o + 64, h // 2, 0:nk])],
                              tqq[h // 2], tkk[h // 2], *w)
                    t = g.stt(SS[:, r, 0:nk], sel[:, m, 0:nk], float(np.float32(2.0) ** np.float32(-0.5 * (h + 1))),
                              ps[:, 0:nk], ALU.mult, ALU.add, tp, tsel, sfree[n % 2])
                    g.free(b, t)
                t = self.softmax(SS[:, :, 0:nk], 4, nk, P, [t])
                for r in range(4):
                    h = h0 + r
                    o = 64 * (h % 2)
                    pt = PT[:, h % 2]
                    tx = self.turn(pt, SS[:, r, :], P, [(c * P, P) for c in range(m + 1)], [t], (ptf[h % 2],))
                    sfree[n % 2] = ("pe", g.n["pe"])
                    if h % 2 == 0:
                        bo, po, wo = g.bank()
                    ptf[h % 2] = g.mm(po[o:o + 64, 0:P], [(V[:, c, h * 64:h * 64 + 64], pt[:, c, :])
                                                          for c in range(m + 1)], tvv, *tx, *wo)
                    if h % 2:
                        to[h // 2] = g.cp(oT[:, h // 2, m * P:(m + 1) * P], po[:, 0:P], ptf[h % 2], e="act")
                        g.free(bo, to[h // 2])
                n += 1
        yt = self.evac8(self.down("w_proj_att_2", oT, to, T1, 8), T1)
        for j, b, ps, tp in self.linear("g_att", 0, 8, xT, xt, T1):
            i, v, tf = self.gettmp()
            t = g.act(v[:, 0:T1], ps[:, 0:T1], ACT.Sigmoid, tp, tf)
            g.free(b, t)
            t = g.tt(v[:, 0:T1], v[:, 0:T1], self.yT[:, j, 0:T1], ALU.mult, t, yt[j])
            tm[j] = g.tt(merged[:, j, :], merged[:, j, :], v[:, 0:T1], ALU.add, t)
            self.tmp_free[i] = tm[j]
        self.layernorm(self.down("w_out_2", merged, tm, T1, 8), 2, False)

    def mem(self):
        g = self.g
        buf = self.carve(0)
        mT = buf(2048, 8, T1)
        qT = buf(2048, 8, T1)
        kT = buf(2048, 8, T1)
        V = buf(2048, 2, 1024)
        S = buf(1024, 4, T1)
        PT = buf(512, 2, 2, P)
        i, (mm,), t = g.unit((0, SLOT, 0, P, self.d["mem_2"]))
        tm = self.turn_back(mm.rearrange("p (m c) -> p m c", m=2), [t, t], mT)
        g.free_unit(i, ("pe", g.n["pe"]))
        tk, tq = [], []
        for j, b, ps, tp in self.linear("mk", 0, 8, mT, tm, T1):
            tk.append(g.cp(kT[:, j, :], ps[:, 0:T1], tp, e="act"))
            g.free(b, tk[j])
        banks = self.tokmajor("mv", mT, tm)
        for m in range(2):
            for h in range(2):
                b, ps, tp = banks[m][h]
                tv = g.cp(V[:, m, h * 512:(h + 1) * 512], ps[:, :], tp)
                g.free(b, tv)
        for j, b, ps, tp in self.linear("mq", 0, 8, self.xT, self.xtok, T1):
            tq.append(g.act(qT[:, j, :], ps[:, 0:T1], ACT.Copy, tp, scale=1.0 / 16))
            g.free(b, tq[j])
        oT = self.hT
        ptf, sf = [None, None], None
        to = [None] * 8
        for m in range(2):
            for h in range(4):
                b, ps, w = g.bank()
                tp = g.mm(ps[:, 0:T1], [(qT[:, 2 * h + i, m * P:(m + 1) * P], kT[:, 2 * h + i, :]) for i in range(2)],
                          *tk, *tq, *w)
                t = g.cp(S[:, h, :], ps[:, 0:T1], tp, sf)
                g.free(b, t)
            t = self.softmax(S, 4, T1, P, [t])
            for h in range(4):
                pt = PT[:, h % 2]
                tx = self.turn(pt, S[:, h, :], P, [(0, P), (P, P)], [t], (ptf[h % 2],))
                sf = ("pe", g.n["pe"])
                b, ps, w = g.bank()
                for i in range(2):
                    tp = g.mm(ps[:, i * P:(i + 1) * P], [(V[:, c, (2 * h + i) * P:(2 * h + i + 1) * P], pt[:, c, :])
                                                         for c in range(2)], tv, *tx, *w)
                ptf[h % 2] = tp
                t2 = g.cp(oT[:, 2 * h:2 * h + 2, m * P:(m + 1) * P], ps[:, 0:256].rearrange("p (i t) -> p i t", i=2),
                          tp, e="act")
                g.free(b, t2)
                to[2 * h] = to[2 * h + 1] = t2
        self.layernorm(self.down("w_mo", oT, to, T1, 8), 3, False)

    TILES = ((0, 0, P), (1, P, P), (2, T1, 16))

    def tokmajor3(self, name, src, toks):
        g = self.g
        banks = {(m, h): g.bank() for m in range(3) for h in range(2)}
        out = []
        for u in range(4):
            i, w, t = self.rowunit(name, u)
            for kk in range(2):
                k = 2 * u + kk
                for m, c, n in self.TILES:
                    for h in range(2):
                        b, ps, wt = banks[m, h]
                        fin = k == 7
                        tk = g.mm(ps[0:n, :], [(src[:, k, c:c + n], w[:, kk, h * 512:(h + 1) * 512])], t, toks[k],
                                  *wt, first=k == 0, final=fin, inc=fin or (kk == 1 and m == 2 and h == 1))
                        if fin:
                            out.append((m, h, n, b, ps, tk))
            g.free_unit(i, ("pe", g.n["pe"]))
        return out

    def gla(self):
        g, nc, T = self.g, self.g.nc, T3
        buf = self.carve(0)
        q, k, gk, eb, en = [buf(4 * T, 4, T) for _ in range(5)]
        v = buf(3072, 3, 1024)
        sr = buf(8 * T, 8, T)
        ke = buf(1536, 3, 512)
        S = buf(1024, 4, 256)
        att = buf(512, 4, P)
        ot = buf(1024, 4, 256)
        lr = buf(T)
        ht = self.prenorm("norm_gains_3", 2)
        src = self.hT
        il, (wl, wg), tl = g.unit((0, 128, 0, P, self.d["gla_lr"]), (128, 512, 0, 16, self.d["gla_gate"]))
        wl = wl.rearrange("p (k n) -> p k n", k=8)
        b, ps, w = g.bank()
        tp = g.mm(ps[0:16, 0:T], [(wl[:, kk, :], src[:, kk, 0:T]) for kk in range(8)], tl, *ht, *w)
        t = g.cp(lr[0:16, :], ps[0:16, 0:T], tp)
        g.free(b, t)
        for j in range(4):
            b, ps, w = g.bank()
            tp = g.mm(ps[:, 0:T], [(wg[0:16, j * P:(j + 1) * P], lr[0:16, :])], t, *w)
            tg = g.ts(gk[:, j, :], ps[:, 0:T], self.col("gla_b_gate_3", j), None, ALU.add, None, tp)
            g.free(b, tg)
        g.free_unit(il, tp)
        t = g.act(eb, gk, ACT.Abs, tg)
        t = g.act(eb, eb, ACT.Exp, t, scale=-1.0)
        t = g.act(eb, eb, ACT.Ln, t, bias=1.0)
        t = g.stt(gk, gk, 0.0, eb, ALU.min, ALU.subtract, t)
        t = g.ts(gk, gk, 1.0 / 16, None, ALU.mult, None, t)
        for j in range(4):
            tb = g.op("dve", lambda j=j: nc.vector.tensor_tensor_scan(en[:, j, :], self.c("reset"), gk[:, j, :], 0.0,
                                                                      ALU.mult, ALU.add), t)
        tbe = g.act(eb, en, ACT.Exp, tb)
        bl = en[:, :, 0:T1].rearrange("p j (c t) -> p j c t", c=4)
        for j in range(4):
            g.tt(gk[:, j, 0:T1].rearrange("p (c t) -> p c t", c=4), bc(bl[:, j, :, 63], 64), bl[:, j], ALU.subtract, tb)
        t = g.tt(gk[:, :, T1:T], bc(en[:, :, T - 1], 16), en[:, :, T1:T], ALU.subtract)
        tge = g.act(gk, gk, ACT.Exp, t)
        ten = g.act(en, en, ACT.Exp, tge, t, scale=-1.0)
        tq = []
        for j, b, ps, tp in self.linear("gla_qk", 0, 8, src, ht, T):
            if j < 4:
                tq.append(g.stt(q[:, j, :], ps[:, 0:T], float(P ** -0.5), eb[:, j, :], ALU.mult, ALU.mult, tp, tbe))
            else:
                c = j - 4
                g.tt(k[:, c, :], ps[:, 0:T], en[:, c, :], ALU.mult, tp, ten)
                tq.append(g.tt(gk[:, c, :], gk[:, c, :], ps[:, 0:T], ALU.mult, tp, tge))
            g.free(b, tq[j])
        tv = [None] * 3
        for m, h, n, b, ps, tp in self.tokmajor3("gla_v", src, ht):
            tv[m] = g.cp(v[0:n, m, h * 512:(h + 1) * 512], ps[0:n, :], tp, e="act")
            g.free(b, tv[m])
        tr_ = []
        for j, b, ps, tp in self.linear("gla_r", 0, 8, src, ht, T):
            tr_.append(g.act(sr[:, j, :], ps[:, 0:T], ACT.Silu, tp))
            g.free(b, tr_[j])
        tke = []
        for m, c, n in self.TILES:
            b, ps, w = g.bank()
            for j in range(4):
                tp = g.tr(ps[0:n, j * P:(j + 1) * P], gk[:, j, c:c + n], self.ident, *tq, *w)
            tke.append(g.cp(ke[0:n, m, :], ps[0:n, :], tp))
            g.free(b, tke[m])
        mi = self.c("m64")[:, 128:256].bitcast(mybir.dt.uint32)
        t0 = g.op("dve", lambda: nc.vector.memset(att, 0.0))
        t0 = g.op("dve", lambda: nc.vector.memset(S, 0.0))
        mix = self.sq
        g.wait("dve", [("pe", g.n["pe"])])
        tS = [t0] * 4
        of = [None] * 4
        s = self.small
        toks = [None] * 8
        for m, c, n in (self.TILES[2], self.TILES[0], self.TILES[1]):
            for h in range(4):
                hv = slice(h * 256, (h + 1) * 256)
                b, ps, w = g.bank()
                tp = g.mm(ps[0:n, 0:n], [(k[:, h, c:c + n], q[:, h, c:c + n])], *tq, *w)
                ta = g.op("dve", lambda o=att[0:n, h, 0:n], mk=mi[0:n, 0:n], dt=ps[0:n, 0:n]:
                          nc.vector.copy_predicated(o, mk, dt), tp, t0, of[h])
                g.free(b, ta)
                bo, po, wo = g.bank()
                to = g.mm(po[0:n, 0:256], [(att[0:n, h, 0:n], v[0:n, m, hv])], ta, tv[m], *wo, final=m == 2)
                for cc in range(1 if m == 2 else 2):
                    o = 64 * cc
                    w_ = min(n, 64)
                    if m < 2:
                        to = g.mm(po[o:o + 64, 0:256], [(q[:, h, c + o:c + o + 64], S[:, h, :])], tS[h],
                                  first=False)
                    if m == 1 and cc == 1:
                        break
                    b, ps, w = g.bank()
                    tp = g.mm(ps[:, 0:256], [(ke[o:o + w_, m, h * P:(h + 1) * P], v[o:o + w_, m, hv])], tke[m], *w)
                    tS[h] = g.stt(S[:, h, :], S[:, h, :], eb[:, h, c + o + w_ - 1:c + o + w_], ps[:, 0:256], ALU.mult,
                                  ALU.add, tp, to)
                    g.free(b, tS[h])
                ss = s[0:n, 16 * m + h:16 * m + h + 1]
                t = g.act(ot[0:n, h, :], po[0:n, 0:256], ACT.Square, to, of[h], accum_out=ss)
                t = g.ts(ss, ss, 1.0 / 256, 1e-6, ALU.mult, ALU.add, t)
                t = g.recip(ss, ss, t)
                t = g.act(ss, ss, ACT.Sqrt, t)
                t = g.ts(ot[0:n, h, :], po[0:n, 0:256], ss, None, ALU.mult, None, t)
                g.free(bo, t)
                b, ps, w = g.bank()
                for i in range(2):
                    tp = g.tr(ps[:, i * P:i * P + n], ot[0:n, h, i * P:(i + 1) * P], self.ident[0:n, 0:n], t, *w)
                of[h] = tp
                for i in range(2):
                    toks[2 * h + i] = g.stt(mix[:, 2 * h + i, c:c + n], ps[:, i * P:i * P + n],
                                            self.col("gla_norm_3", i), sr[:, 2 * h + i, c:c + n], ALU.mult, ALU.mult,
                                            tp, tr_[2 * h + i])
                g.free(b, toks[2 * h + 1])
        self.postnorm(self.down("gla_out", mix, toks, T, 8), "norm_gains_3", 3, False)

    def rope(self, x, H, m, n, tok):
        g = self.g
        x3 = x.rearrange("p (h j) -> p h j", h=H)
        at = CSTS["rope"][0] + 16 * m
        c = bc_mid(self.cst[0:n, at:at + 8], H)
        s = bc_mid(self.cst[0:n, at + 8:at + 16], H)
        r = self.rstd.rearrange("p k t -> p (k t)")
        a, b2, d, e = [r[0:n, i * 128:i * 128 + 8 * H].rearrange("p (h j) -> p h j", h=H) for i in range(4)]
        x1, x2 = x3[:, :, 0:8], x3[:, :, 8:16]
        g.tt(a, x1, c, ALU.mult, tok)
        g.tt(b2, x2, s, ALU.mult)
        g.tt(d, x2, c, ALU.mult)
        g.tt(e, x1, s, ALU.mult)
        g.tt(x1, a, b2, ALU.subtract)
        return g.tt(x2, d, e, ALU.add)

    def shared(self):
        g, T = self.g, T3
        buf = self.carve(18900)
        kD, V = self.kD3, self.V3 = buf(4 * T, 4, T), buf(768, 3, 256)
        kt = self.A[:, 0:768].rearrange("p (m c) -> p m c", m=3)
        ht = self.prenorm("kv_norm_3")
        src = self.hT
        for u in range(2):
            i, w, t = self.colunit("w_kv", u)
            for m, c, n in self.TILES:
                b, ps, wt = g.bank()
                tp = g.mm(ps[0:n, 0:256], [(src[:, k, c:c + n], w[:, k, :]) for k in range(8)], t, *ht, *wt)
                tk = g.cp((kt, V)[u][0:n, m, :], ps[0:n, 0:256], tp)
                g.free(b, tk)
                if u == 0:
                    tk = self.rope(kt[0:n, m, :], 4, m, n, tk)
                    b, ps, wt = g.bank()
                    for h in range(4):
                        tp2 = g.tr(ps[0:64, h * P:h * P + n], kt[0:n, m, h * 64:h * 64 + 64], self.ident[0:n, 0:n],
                                   tk, *wt)
                    p4 = ps[0:64, :].rearrange("p (h t) -> p h t", h=4)[:, :, 0:n]
                    g.cp(kD[0:64, :, c:c + n], p4, tp2)
                    tk = g.cp(kD[64:128, :, c:c + n], p4, tp2)
                    g.free(b, tk)
            g.free_unit(i, tp)
        self.tkv = tk
        g.fence()

    def swa(self):
        g, T = self.g, T3
        buf = self.carve(0, 18900)
        qt = buf(3072, 3, 1024)
        qT = buf(8 * T, 8, T)
        S = buf(8 * T, 2, 4, T)
        PT = buf(768, 2, 3, P)
        kD, V = self.kD3, self.V3
        ht = self.prenorm("norm_gains_3", 8)
        tm = [None] * 3
        for m, h, n, b, ps, tp in self.tokmajor3("swa_q", self.hT, ht):
            tm[m] = g.act(qt[0:n, m, h * 512:(h + 1) * 512], ps[0:n, :], ACT.Copy, tp, scale=0.125)
            g.free(b, tm[m])
        tq = []
        for m, c, n in self.TILES:
            t = self.rope(qt[0:n, m, :], 16, m, n, tm[m])
            for hf in range(2):
                b, ps, w = g.bank()
                for i in range(4):
                    tp = g.tr(ps[:, i * P:i * P + n], qt[0:n, m, (4 * hf + i) * P:(4 * hf + i + 1) * P],
                              self.ident[0:n, 0:n], t, *w)
                tx = g.cp(qT[:, 4 * hf:4 * hf + 4, c:c + n],
                          ps[:, :].rearrange("p (h t) -> p h t", h=4)[:, :, 0:n], tp)
                g.free(b, tx)
            tq.append(tx)
        mix = self.sq
        g.wait("act", [("pe", g.n["pe"])])
        ptf, sfree = [None, None], [None, None]
        to = [None] * 8
        x = 0
        sinks = self.rows[:, ROWS["swa_sinks_3"][0]:ROWS["swa_sinks_3"][0] + 16]
        for m, c, n in self.TILES:
            keys = ((0, 2), (0, 1, 2), (2,))[m]
            for kv in range(4):
                SS = S[0:n, x % 2]
                for r in range(4):
                    h = 4 * kv + r
                    o = 64 * (h % 2)
                    b, ps, w = g.bank()
                    tp = g.mm(ps[0:n, 0:T], [(qT[o:o + 64, h // 2, c:c + n], kD[o:o + 64, kv, :])], tq[m], self.tkv,
                              *w)
                    at = CSTS["swa"][0] + m * T
                    t = g.tt(SS[:, r, :], ps[0:n, 0:T], self.cst[0:n, at:at + T], ALU.add, tp, sfree[x % 2])
                    g.free(b, t)
                t = self.softmax(SS, 4, T, n, [t], sink=sinks[0:n, 4 * kv:4 * kv + 4])
                for r in range(4):
                    h = 4 * kv + r
                    o = 64 * (h % 2)
                    pt = PT[:, h % 2]
                    tx = self.turn(pt, SS[:, r, :], n, [(kk * P, (P, P, 16)[kk]) for kk in keys], [t], (ptf[h % 2],))
                    sfree[x % 2] = ("pe", g.n["pe"])
                    if h % 2 == 0:
                        bo, po, wo = g.bank()
                    pairs = [(V[0:(P, P, 16)[kk], kk, kv * 64:kv * 64 + 64], pt[0:(P, P, 16)[kk], i, 0:n])
                             for i, kk in enumerate(keys)]
                    ptf[h % 2] = g.mm(po[o:o + 64, 0:n], pairs, *tx, *wo)
                    if h % 2:
                        to[h // 2] = g.cp(mix[:, h // 2, c:c + n], po[:, 0:n], ptf[h % 2], e="act")
                        g.free(bo, to[h // 2])
                x += 1
        self.postnorm(self.down("swa_out", mix, to, T, 8), "norm_gains_3", 9, False)


def colunits(w):
    k, n = w.shape
    return w.reshape(k // P, P, n // 256, 256).transpose(2, 1, 0, 3).reshape(n // 256, P, k // P * 256)


def rowunits(w):
    k, n = w.shape
    return w.reshape(k // 256, 2, P, n).transpose(0, 2, 1, 3).reshape(k // 256, P, 2 * n)


def layout(v):
    d = {"x": v["x"][0].reshape(2, P, D).transpose(1, 0, 2).reshape(P, SLOT), "cst": constants(), "meta_tokens_3": v["meta_tokens_3"]}
    cols = np.zeros((P, NCOL), np.float32)
    for name, (at, n) in COLS.items():
        a = np.repeat(v["d_skip_2"].reshape(-1), 64) if name == "d_skip_2c" else v[name]
        cols[:, at:at + n] = np.asarray(a).reshape(n, P).T
    d["cols"] = cols
    d["rows"] = np.concatenate([np.asarray(v[n]).reshape(1, 16) for n in ROWS], 1)
    for f in FFNS:
        d[f + "_w_gate"] = colunits(v[f + "_w_gate"])
        d[f + "_w_up"] = colunits(v[f + "_w_up"])
        d[f + "_w_down"] = rowunits(v[f + "_w_down"])
    for f in ("ffn1", "ffn2"):
        w = v[f + "_w_in_2"][0]
        d[f + "_w_gate_2"] = colunits(w[:, :FF])
        d[f + "_w_up_2"] = colunits(w[:, FF:])
        d[f + "_w_out_2"] = rowunits(v[f + "_w_out_2"][0])
    for a in range(2):
        for b in range(2):
            w = v["w_ffn_in_3"][a, b]
            d[f"g3_{a}{b}"] = colunits(w[:, :FF])
            d[f"u3_{a}{b}"] = colunits(w[:, FF:])
            d[f"d3_{a}{b}"] = rowunits(v["w_ffn_out_3"][a, b])
    w = v["l0_w_in"]
    c = np.cumsum([0, 512, 24, 128, 128, 128, 128, 128, 128, 512, 512, 512])
    part = lambda i: w[:, c[i]:c[i + 1]]
    d["nsa_in"] = colunits(np.concatenate([part(i) for i in (0, 2, 3, 4, 6, 8, 9, 10)], 1))
    d["nsa_v"] = colunits(np.concatenate([part(5), part(7)], 1))
    d["nsa_g"] = part(1).reshape(8, P, 24).transpose(1, 0, 2).reshape(P, 192)
    d["cmp_w2"] = np.concatenate([v["l0_cmp_w2_k"], v["l0_cmp_w2_v"]], 1)
    for s in "kv":
        d["cmp_w1_" + s] = v["l0_cmp_w1_" + s].reshape(16, P, P).transpose(1, 0, 2).reshape(P, SLOT)
    d["nsa_out"] = rowunits(v["l0_w_out"])
    d["lora1"] = np.concatenate([v["l1_w_dec1"], v["l1_w_a1"], v["l1_w_g1"]], 1).reshape(8, P, 256).transpose(
        1, 0, 2).reshape(P, SLOT)
    d["lora2"] = np.concatenate([np.concatenate([v["l1_w_dec2"], v["l1_w_a2"]], 1),
                                 np.concatenate([v["l1_w0"], v["l1_a0"]])[None]], 0)
    d["l1_w_g2"] = v["l1_w_g2"]
    for n in ("l1_w_r", "l1_w_k", "l1_w_v", "l1_w_o"):
        d[n] = rowunits(v[n])
    for n in ("l1_k_k", "l1_k_a", "l1_r_k", "l1_lnx_g", "l1_lnx_b"):
        d[n] = v[n].reshape(1, D)
    w = v["w_in_2"][0]
    c = np.cumsum([0, 1024, 1024, 1024, 2048, 16, 1024, 256, 1024, 64, 16])
    part = lambda i: w[:, c[i]:c[i + 1]]
    for i, n in ((0, "g_ssd"), (1, "g_att"), (2, "z_2"), (3, "xbc"), (5, "q_2"), (6, "ckv"), (7, "qidx")):
        d[n] = colunits(part(i))
    d["tokw"] = np.concatenate([part(4), part(9)], 1).reshape(8, P, 32).transpose(1, 0, 2).reshape(P, 256)
    d["kidx"] = part(8).reshape(8, P, 64).transpose(1, 0, 2).reshape(P, 512)
    d["w_uk"] = v["w_uk_2"][0].transpose(2, 0, 1).reshape(2, P, D).transpose(1, 0, 2).reshape(P, SLOT)
    d["w_uv"] = v["w_uv_2"][0].transpose(1, 0, 2).reshape(2, P, D).transpose(1, 0, 2).reshape(P, SLOT)
    for n in ("w_proj_ssd_2", "w_proj_att_2", "w_out_2"):
        d[n] = rowunits(v[n][0])
    d["mem_2"] = v["mem_2"][0].reshape(2, P, D).transpose(1, 0, 2).reshape(P, SLOT)
    d["mq"] = colunits(v["w_mq_2"][0])
    d["mk"] = colunits(v["w_mkv_2"][0][:, :D])
    d["mv"] = rowunits(v["w_mkv_2"][0][:, D:])
    d["w_mo"] = rowunits(v["w_mo_2"][0])
    w = v["gla_w_in_3"][0]
    d["gla_qk"] = colunits(w[:, :1024])
    d["gla_v"] = rowunits(w[:, 1024:2048])
    d["gla_r"] = colunits(w[:, 2048:3072])
    d["gla_lr"] = w[:, 3072:].reshape(8, P, 16).transpose(1, 0, 2).reshape(P, 128)
    d["gla_gate"] = v["gla_w_gate_3"][0]
    d["gla_out"] = rowunits(v["gla_w_out_3"][0])
    d["w_kv"] = colunits(v["w_kv_3"])
    d["swa_q"] = rowunits(v["swa_w_q_3"][0])
    d["swa_out"] = rowunits(v["swa_w_out_3"][0])
    return {n: np.ascontiguousarray(a) for n, a in d.items()}


def program(nc, arrays, stages):
    d = {n: nc.dram_tensor("in_" + n, a.shape, F32, kind="ExternalInput").ap() for n, a in arrays.items()}
    out = nc.dram_tensor("out_0", (T1, D), F32, kind="ExternalOutput").ap()
    with ExitStack() as ctx:
        Model(nc, ctx, d, out, stages)


def kernel(**inputs):
    import concourse.bacc as _bacc
    from concourse.bass_utils import run_bass_kernel_spmd as _run

    arrays = layout({n: np.asarray(a) for n, a in inputs.items()})
    nc = _bacc.Bacc("TRN2", target_bir_lowering=False, num_devices=1)
    program(nc, arrays, range(18))
    r = _run(nc, [{"in_" + n: a for n, a in arrays.items()}], core_ids=[0])
    return r.results[0]["out_0"].reshape(1, T1, D)
```

```python
from contextlib import ExitStack

import numpy as np

import concourse.bass as bass
from concourse import mybir

P = 128
D = 1024
FF = 2816
NF = FF // P
T1 = 256
T3 = 272
NPAR = 2
SLOT = 2048
NRAW = 8
NHI = 5
UNIT = 1024
BIG = -1.0e30
ALPHA = 2.0 ** 0.25

ALU = mybir.AluOpType
ACT = mybir.ActivationFunctionType
F32 = mybir.dt.float32
F32R = mybir.dt.float32r
AX_X = mybir.AxisListType.X

FFNS = ("l0_ffn1", "l0_ffn2", "l1_ffn1", "l1_ffn2")


def table(sizes):
    at, out = 0, {}
    for name, n in sizes:
        out[name] = (at, n)
        at += n
    return out, at


COLS, NCOL = table(
    [(f + s, 8) for f in FFNS for s in ("_pre_g", "_post_g")]
    + [(f"l{i}_mix_{s}_g", 8) for i in range(2) for s in ("pre", "post")]
    + [("l0_conv_w", 12), ("l0_conv_b", 4), ("l0_cmp_pe_k", 16), ("l0_cmp_pe_v", 16), ("l1_mu", 48)]
    + [(f"ln{i}_{s}_2", 8) for i in range(1, 5) for s in "gb"]
    + [("conv_w_2", 64), ("conv_b_2", 16), ("d_skip_2c", 8), ("ssd_norm_w_2", 8), ("kv_norm_w_2", 2)]
    + [("norm_gains_3", 96), ("kv_norm_3", 8), ("gla_b_gate_3", 4), ("gla_norm_3", 2)])

ROWS, NROW = table([("dt_bias_2", 16), ("a_log_2", 16), ("d_skip_2", 16), ("swa_sinks_3", 16)])

CSTS, NCST = table([
    ("ident", 128), ("ones", 128), ("half", 1), ("alibi", 512), ("alibi_cmp", 32), ("m64", 256), ("suf64", 128),
    ("chunk", 2), ("level", 768), ("tri128", 128), ("suf128", 128), ("swa", 816), ("rope", 48),
    ("reset", 272)])


def constants():
    c = np.zeros((P, NCST), np.float32)

    def put(name, a):
        at, n = CSTS[name]
        a = np.asarray(a, np.float32)
        c[:a.shape[0], at:at + n] = a.reshape(a.shape[0], -1)

    i = np.arange(P)[:, None]
    j = np.arange(P)[None, :]
    put("ident", np.eye(P))
    put("ones", np.ones((P, P)))
    s = np.arange(T1)[None, :]
    put("alibi", np.concatenate([np.where(s <= i + P * m, s - (i + P * m), BIG) for m in range(2)], 1))
    n = np.arange(16)[None, :]
    e = 16 * n + 31
    put("alibi_cmp", np.concatenate([np.where((e <= i + P * m) & (n < 15), e - (i + P * m), BIG)
                                     for m in range(2)], 1))
    same = i // 64 == j // 64
    put("m64", np.concatenate([same & (i < j), same & (i <= j)], 1))
    put("suf64", same & (i > j))
    put("chunk", i // 64 == np.arange(2)[None, :])
    put("level", np.concatenate([(i // (2 * b) == j // (2 * b)) & (i % (2 * b) < b) & (j % (2 * b) >= b)
                                 for b in (1, 2, 4, 8, 16, 32)], 1))
    put("tri128", i <= j)
    put("suf128", i > j)
    put("half", np.full((P, 1), -0.5))
    keep = [np.concatenate([j <= i, np.zeros((P, P), bool), np.ones((P, 16), bool)], 1),
            np.concatenate([j > i, j <= i, np.ones((P, 16), bool)], 1),
            np.concatenate([np.zeros((P, T1), bool), np.arange(16)[None, :] <= i], 1)]
    put("swa", np.concatenate([np.where(k, 0.0, BIG) for k in keep], 1))
    freq = np.float32(500000.0) ** (-np.arange(0, 16, 2, dtype=np.float32) / np.float32(16))
    rope = []
    for base in (16, 16 + P, 0):
        ang = (np.arange(P, dtype=np.float32)[:, None] + np.float32(base)) * freq[None, :].astype(np.float32)
        rope += [np.cos(ang), np.sin(ang)]
    put("rope", np.concatenate(rope, 1))
    put("reset", np.broadcast_to((np.arange(T3) % 64 != 0)[None, :], (P, T3)))
    return c


class Prog:

    def __init__(self, nc, ctx):
        self.nc = nc
        self.ctx = ctx
        self.q = {e: [] for e in ("pe", "act", "dve", "pool", "sp")}
        self.h = {"pe": nc.tensor, "act": nc.scalar, "dve": nc.vector, "pool": nc.gpsimd, "sp": nc.sync}
        self.sem = {e: ctx.enter_context(nc.semaphore("s_" + e)) for e in ("pe", "act", "dve", "pool")}
        self.n = {e: 0 for e in self.sem}
        self.seen = {e: {} for e in self.q}
        self.at = (nc.sbuf_base + 63) // 64 * 64
        self.raw, self.raw_at = self.place("raw", NRAW * UNIT)
        self.lo = self.alias("lo", self.raw_at, NRAW * UNIT)
        self.hi, _ = self.place("hi", NHI * UNIT, F32R)
        self.par, _ = self.place("par", NPAR * SLOT)
        for i in range(NPAR):
            self.new_sem(f"par{i}")
        for i in range(NRAW):
            self.new_sem(f"raw{i}")
        self.new_sem("cvh")
        self.new_sem("cvl")
        self.new_sem("cvp")
        self.par_free = [None] * NPAR
        self.npar = 0
        self.weights = []
        self.w_free = []
        self.ps = [ctx.enter_context(nc.psum_tensor(f"ps{i}", [P, 512], F32)) for i in range(8)]
        self.ps_free = [[] for _ in range(8)]
        self.nps = 0
        for w in range(NHI):
            self.split_later(w)

    def new_sem(self, name):
        self.sem[name] = self.ctx.enter_context(self.nc.semaphore("s_" + name))
        self.n[name] = 0

    def place(self, name, n, dt=F32):
        at = self.at
        self.at += (4 * n + 63) // 64 * 64
        return self.nc.alloc_sbuf_tensor_at(name, [P, n], dt, offset=at), at

    def alias(self, name, at, n, dt=F32R):
        return self.nc.alloc_sbuf_tensor_at(name, [P, n], dt, offset=at)

    def sb(self, name, n):
        return self.place(name, n)[0]

    def wait(self, e, toks):
        for t in toks:
            if t is None:
                continue
            s, v = t
            if self.seen[e].get(s, 0) >= v:
                continue
            self.seen[e][s] = v
            self.q[e].append(lambda h=self.h[e], s=self.sem[s], v=v: h.wait_ge(s, v))

    def op(self, e, fn, *toks):
        if e != "pe" and self.n[e]:
            toks = toks + ((e, self.n[e]),)
        self.wait(e, toks)
        self.n[e] += 1
        self.q[e].append(lambda s=self.sem[e]: fn().then_inc(s, 1))
        return e, self.n[e]

    def last(self):
        return [(e, self.n[e]) for e in ("pe", "act", "dve", "pool") if self.n[e]]

    def fence(self):
        toks = self.last()
        for e in ("pe", "act", "dve", "pool"):
            self.wait(e, [t for t in toks if t[0] != e])
        for b in range(8):
            self.ps_free[b] = []

    def dma_group(self, name):
        self.new_sem(name)

    def dma(self, e, group, out, in_, *toks):
        self.wait(e, toks)
        self.n[group] += 16
        self.q[e].append(lambda h=self.h[e], s=self.sem[group]: h.dma_start(out, in_).then_inc(s, 16))
        return group, self.n[group]

    def unit(self, *loads):
        i = self.npar % NPAR
        self.npar += 1
        assert self.npar <= NPAR or self.par_free[i], "slot reused before it was freed"
        self.wait("pool", [self.par_free[i]])
        self.par_free[i] = None
        at = i * SLOT
        out = []
        for off, w, p0, p1, src in loads:
            dst = self.par[p0:p1, at + off:at + off + w]
            tok = self.dma("pool", f"par{i}", dst, src)
            out.append(dst)
        return i, out, tok

    def free_unit(self, i, tok):
        self.par_free[i] = tok

    def weight(self, src):
        w = len(self.weights)
        if w >= NRAW:
            self.wait("sp", [self.w_free[w - NRAW]])
        tok = self.dma("sp", f"raw{w % NRAW}", self.raw[:, w % NRAW * UNIT:(w % NRAW + 1) * UNIT], src)
        self.weights.append(tok)
        self.w_free.append(None)
        hi = self.hi[:, w % NHI * UNIT:(w % NHI + 1) * UNIT]
        lo = self.lo[:, w % NRAW * UNIT:(w % NRAW + 1) * UNIT]
        return w, hi, lo, self.parted(w)

    def parted(self, w):
        return ("cvp", w // 3 + 1) if w % 3 == 2 else ("cvl", w - w // 3 + 1 - (w % 3 == 2))

    def free_weight(self, w, tok):
        self.w_free[w] = tok
        self.split_later(w + NHI)

    def split_later(self, w):
        nc = self.nc
        raw = self.raw[:, w % NRAW * UNIT:(w % NRAW + 1) * UNIT]
        lo = self.lo[:, w % NRAW * UNIT:(w % NRAW + 1) * UNIT]
        hi = self.hi[:, w % NHI * UNIT:(w % NHI + 1) * UNIT]

        def first():
            if w >= len(self.weights):
                return
            s, v = self.weights[w]
            nc.scalar.wait_ge(self.sem[s], v)
            if w >= NHI:
                s, v = self.w_free[w - NHI]
                nc.scalar.wait_ge(self.sem[s], v)
            nc.scalar.activation(hi, raw, ACT.Copy).then_inc(self.sem["cvh"], 1)

        def second():
            if w >= len(self.weights):
                return
            h.wait_ge(self.sem["cvh"], w + 1)
            h.tensor_tensor(lo, raw, hi.bitcast(F32), ALU.subtract).then_inc(self.sem[self.parted(w)[0]], 1)

        e = "pool" if w % 3 == 2 else "dve"
        h = self.h[e]
        self.q["act"].append(first)
        self.q[e].append(second)

    def bank(self):
        while self.ps_free[self.nps % 8] is None:
            assert any(w is not None for w in self.ps_free), "every bank is held"
            self.nps += 1
        b = self.nps % 8
        self.nps += 1
        w, self.ps_free[b] = self.ps_free[b], None
        return b, self.ps[b], w

    def free(self, b, *toks):
        self.ps_free[b] = list(toks)

    def mm(self, out, pairs, *toks, first=True, final=True, inc=True, loose=False):
        self.wait("pe", toks)
        n = len(pairs)
        for i, (a, b) in enumerate(pairs):
            def f(a=a, b=b, st=first and i == 0, sp=final and i == n - 1):
                return self.nc.tensor.matmul(out, a, b, start=st, stop=sp, skip_group_check=loose)
            if i == n - 1 and inc:
                self.n["pe"] += 1
                self.q["pe"].append(lambda f=f: f().then_inc(self.sem["pe"], 1))
            else:
                self.q["pe"].append(f)
        return ("pe", self.n["pe"]) if inc else None

    def mm3(self, out, a, b, *toks, **kw):
        return self.mm(out, [(a[0], b[0]), (a[0], b[1]), (a[1], b[0])], *toks, **kw)

    def split(self, hi, lo, src, *toks):
        t = self.act(hi, src, ACT.Copy, *toks)
        return self.op("dve", lambda: self.nc.vector.tensor_tensor(lo, src, hi.bitcast(F32), ALU.subtract), t, *toks)

    def tr(self, out, in_, ident, *toks, inc=True):
        self.wait("pe", toks)
        f = lambda: self.nc.tensor.transpose(out, in_, ident)
        if inc:
            self.n["pe"] += 1
            self.q["pe"].append(lambda: f().then_inc(self.sem["pe"], 1))
            return "pe", self.n["pe"]
        self.q["pe"].append(f)

    def act(self, out, in_, func, *toks, **kw):
        return self.op("act", lambda: self.nc.scalar.activation(out, in_, func, **kw), *toks)

    def tt(self, out, a, b, op, *toks, e="dve"):
        return self.op(e, lambda: self.h[e].tensor_tensor(out, a, b, op), *toks)

    def ts(self, out, a, s1, s2, op0, op1, *toks, e="dve"):
        if s2 is None:
            return self.op(e, lambda: self.h[e].tensor_scalar(out, a, s1, None, op0), *toks)
        return self.op(e, lambda: self.h[e].tensor_scalar(out, a, s1, s2, op0, op1), *toks)

    def stt(self, out, a, s, b, op0, op1, *toks, **kw):
        return self.op("dve", lambda: self.nc.vector.scalar_tensor_tensor(out, a, s, b, op0, op1, **kw), *toks)

    def cp(self, out, in_, *toks, e="dve"):
        if e == "act":
            return self.act(out, in_, ACT.Copy, *toks)
        return self.op(e, lambda: self.h[e].tensor_copy(out, in_), *toks)

    def red(self, out, in_, op, *toks):
        return self.op("dve", lambda: self.nc.vector.tensor_reduce(out, in_, AX_X, op), *toks)

    def recip(self, out, in_, *toks):
        return self.op("dve", lambda: self.nc.vector.reciprocal(out, in_), *toks)

    def run(self):
        block = self.ctx.enter_context(self.nc.Block())

        def play(name):
            def body(_):
                for f in self.q[name]:
                    f()
            return body

        block.sync(play("sp"))
        block.scalar(play("act"))
        block.vector(play("dve"))
        block.gpsimd(play("pool"))
        block.tensor(play("pe"))


def bc(ap, *shape):
    return ap.unsqueeze(len(ap.shape)).broadcast_to(list(ap.shape) + list(shape))


def bc_mid(ap, n):
    return ap.unsqueeze(1).broadcast_to([ap.shape[0], n] + list(ap.shape[1:]))


class Model:
    def __init__(self, nc, ctx, d, out, stages):
        self.d = d
        g = self.g = Prog(nc, ctx)
        self.stages = stages
        self.cst = g.sb("cst", NCST)
        self.cols = g.sb("cols", NCOL + P)
        self.rows = g.sb("rows", NROW)
        self.xT = g.sb("xT", 8 * T3)[:, :].rearrange("p (k t) -> p k t", k=8)
        _, at = g.place("hT_hi", 8 * T3, F32R)
        self.H = self.view("hh", at, 8)
        self.Hf = self.view("hf32", at, 8, F32)
        _, at = g.place("hT_lo", 8 * T3, F32R)
        self.L = self.view("hl", at, 8)
        self.Lf = self.view("lf32", at, 8, F32)
        self.hp = (self.H, self.L)
        self.yT = g.sb("yT", 8 * T3)[:, :].rearrange("p (k t) -> p k t", k=8)
        self.sq_, at = g.place("sq", 8 * T3)
        self.sqR = self.view("sqr", at, 8)
        self.sq = self.sq_[:, :].rearrange("p (k t) -> p k t", k=8)
        self.rstd = g.sb("rstd", 3 * T3)[:, :].rearrange("p (k t) -> p k t", k=3)
        self.tmp = g.sb("tmp", 4 * T3)[:, :].rearrange("p (k t) -> p k t", k=4)
        self.tmp_free = [None] * 4
        self.ntmp = 0
        self.small = g.sb("small", 512)
        self.NA = (nc.sbuf_usable_end - g.at) // 4 // 16 * 16
        self.A, self.Aat = g.place("arena", self.NA)
        self.hf = (self.over("hfh", 0, NF, T3), self.over("hfl", NF * T3, NF, T3))
        self.ident = self.c("ident")
        self.ones = self.c("ones")
        g.dma_group("cst")
        g.dma("sp", "cst", self.cst[:, 0:257], d["cst"][:, 0:257])
        t = g.dma("sp", "cst", self.cols[:, :], d["cols"])
        for e in ("pe", "act", "dve", "pool"):
            g.wait(e, [t])
        self.T = T1
        self.xtok = [None] * 8
        self.load_x(d["x"], 0)
        g.dma_group("cst2")
        g.dma("pool", "cst2", self.cst[:, 257:NCST], d["cst"][:, 257:NCST])
        self.cst2 = g.dma("pool", "cst2", self.rows[:, :], d["rows"].broadcast_to([P, NROW]))
        plan = [
            lambda: self.ffn1("l0_ffn1"), self.nsa, lambda: self.ffn1("l0_ffn2"),
            lambda: self.ffn1("l1_ffn1"), self.rwkv, lambda: self.ffn1("l1_ffn2"),
            lambda: self.ffn2("ffn1", 1), self.hybrid, self.mem, lambda: self.ffn2("ffn2", 4),
            self.enter3, lambda: self.ffn3(0, 0), self.gla, lambda: self.ffn3(0, 1), self.shared, lambda: self.ffn3(1, 0),
            self.swa, lambda: self.ffn3(1, 1)]
        for i in stages:
            if plan[i] in (self.nsa, self.rwkv, self.hybrid, self.mem, self.gla, self.shared, self.swa):
                g.fence()
                for e in ("pe", "act", "dve", "pool"):
                    g.wait(e, [self.cst2])
            plan[i]()
        self.store(out)
        g.run()

    def view(self, name, at, k, dt=F32R, T=T3):
        return self.g.alias(name, at, k * T, dt)[:, :].rearrange("p (k t) -> p k t", k=k)

    def over(self, name, start, k, T):
        return self.view(name, self.Aat + 4 * start, k, F32R, T)

    def c(self, name, j=None, w=128):
        at, n = CSTS[name]
        if j is None:
            return self.cst[:, at:at + n]
        return self.cst[:, at + j * w:at + (j + 1) * w]

    def col(self, name, j):
        at = COLS[name][0] + j
        return self.cols[:, at:at + 1]

    def load_x(self, x, at):
        g = self.g
        if at == 0:
            i, (stage,), t = g.unit((0, SLOT, 0, P, x))
            tiles = [(0, P, 0), (1, P, P)]
        else:
            i, (stage,), t = g.unit((0, D, 0, T3 - at, x))
            tiles = [(0, T3 - at, at)]
        stage = stage.rearrange("p (m c) -> p m c", c=D)
        for k in range(8):
            b, ps, w = g.bank()
            for m, p, c in tiles:
                tk = g.tr(ps[:, c - at:c - at + p], stage[0:p, m, k * P:(k + 1) * P], self.ident[0:p, 0:p], t, *w)
            wide = sum(p for _, p, _ in tiles)
            tk = g.cp(self.xT[:, k, at:at + wide], ps[:, 0:wide], tk)
            g.free(b, tk)
            self.xtok[k] = tk
        g.free_unit(i, ("pe", g.n["pe"]))
        g.fence()

    def store(self, out):
        g = self.g
        g.fence()
        g.dma_group("out")
        stage = self.A[:, 0:2048].rearrange("p (m c) -> p m c", m=2)
        for m in range(2):
            for h in range(2):
                b, ps, w = g.bank()
                for k in range(4):
                    tk = g.tr(ps[:, k * P:(k + 1) * P], self.xT[:, 4 * h + k, m * P:(m + 1) * P], self.ident, *w)
                tk = g.cp(stage[:, m, h * 512:(h + 1) * 512], ps[:, :], tk, e=("dve", "act")[h])
                g.free(b, tk)
                t = g.dma("sp", "out", out[m * P:(m + 1) * P, h * 512:(h + 1) * 512],
                          stage[:, m, h * 512:(h + 1) * 512], tk)
        g.wait("sp", [t])

    def tiles(self):
        return ((0, 0, P), (1, P, P)) + (((2, T1, T3 - T1),) if self.T == T3 else ())

    def squares(self, src, toks, k, e):
        s = self.sq[:, k, 0:self.T]
        x = src[:, k, 0:self.T]
        if e == "act":
            return self.g.act(s, x, ACT.Square, toks[k], self.sqtok)
        return self.g.tt(s, x, x, ALU.mult, toks[k], self.sqtok, e=e)

    def rms(self, src, toks, mult, add, made=None):
        g, T = self.g, self.T
        b, ps, w = g.bank()
        self.sqtok = self.sqtok or ("pe", g.n["pe"])
        for k in range(8):
            tk = made[k] if made else self.squares(src, toks, k, ("act", "dve")[k % 2])
            for m, c, n in self.tiles():
                fin = m == self.tiles()[-1][0]
                tp = g.mm(ps[0:n, m:m + 1], [(self.sq[:, k, c:c + n], self.ones[:, 0:1])], tk, *w,
                          first=k == 0 and m == 0, final=k == 7, inc=k == 7 and fin, loose=True)
        self.sqtok = None
        r = self.small[:, 300:303]
        parts = [(P, 0, 2)] + ([(16, 2, 3)] if T == T3 else [])
        for n, x, y in parts:
            tk = g.ts(r[0:n, x:y], ps[0:n, x:y], mult, add, ALU.mult, ALU.add, tp)
        g.free(b, tk)
        half = self.c("half")
        for n, x, y in parts:
            tk = g.tt(r[0:n, x:y], r[0:n, x:y], half[0:n, :].broadcast_to([n, y - x]), ALU.pow, tk, e="pool")
        b, ps, w = g.bank()
        for m, c, n in self.tiles():
            tp = g.mm(ps[:, c:c + n], [(r[0:n, m:m + 1].broadcast_to([n, P]), self.ident[0:n, 0:n])], tk, *w)
        return b, ps, tp

    def rsqrt(self, out, ps, tp, mult, add, T, b=None):
        g = self.g
        tk = g.ts(out, ps, mult, add, ALU.mult, ALU.add, tp)
        if b is not None:
            g.free(b, tk)
        tk = g.recip(out, out, tk)
        return g.act(out, out, ACT.Sqrt, tk)

    def prenorm(self, gain, j=0):
        g, T = self.g, self.T
        b, ps, tp = self.rms(self.xT, self.xtok, 1.0 / D, 1e-6)
        toks = []
        for k in range(8):
            t = g.stt(self.sq[:, k, 0:T], self.xT[:, k, 0:T], self.col(gain, j * 8 + k), ps[:, 0:T],
                      ALU.mult, ALU.mult, tp)
            toks.append(g.split(self.H[:, k, 0:T], self.L[:, k, 0:T], self.sq[:, k, 0:T], t))
        g.free(b, t)
        return toks

    def lazynorm(self, gain, j=0):
        g, T = self.g, self.T
        toks = []
        for k in range(8):
            c = self.col(gain, j * 8 + k)
            t = g.act(self.H[:, k, 0:T], self.xT[:, k, 0:T], ACT.Copy, self.xtok[k], scale=c)
            toks.append(g.stt(self.L[:, k, 0:T], self.xT[:, k, 0:T], c, self.H[:, k, 0:T].bitcast(F32),
                              ALU.mult, ALU.subtract, t))

        self.sqtok = ("pe", g.n["pe"])
        sq = [self.squares(self.xT, self.xtok, k, "pool") for k in range(8)]

        def later():
            b, ps, tp = self.rms(self.xT, self.xtok, 1.0 / D, 1e-6, made=sq)
            t = g.cp(self.rstd[:, 2, 0:T], ps[:, 0:T], tp, e="act")
            g.free(b, t)
            return t

        return toks, later

    def evac8(self, banks, T, scaled=False):
        g = self.g
        toks = []
        for k, (b, ps, tp) in enumerate(banks):
            if scaled:
                tk = g.tt(self.yT[:, k, 0:T], ps[:, 0:T], self.rstd[:, 2, 0:T], ALU.mult, tp)
            else:
                tk = g.cp(self.yT[:, k, 0:T], ps[:, 0:T], tp, e=("dve", "act")[k % 2])
            g.free(b, tk)
            toks.append(tk)
        return toks

    def postnorm(self, banks, gain, j, half, scaled=False):
        g, T = self.g, self.T
        yt = self.evac8(banks, T, scaled)
        f = 4.0 if half else 1.0
        b, ps, tp = self.rms(self.yT, yt, f / D, f * 1e-6)
        for k in range(8):
            tk = g.stt(self.yT[:, k, 0:T], self.yT[:, k, 0:T], self.col(gain, j * 8 + k), ps[:, 0:T],
                       ALU.mult, ALU.mult, tp)
            self.xtok[k] = g.tt(self.xT[:, k, 0:T], self.xT[:, k, 0:T], self.yT[:, k, 0:T], ALU.add, tk,
                                e=("dve", "pool")[k % 2])
        g.free(b, tk)

    def layernorm(self, banks, n, half):
        g, T = self.g, self.T
        f = 2.0 if half else 1.0
        yt = []
        for k, (b, ps, tp) in enumerate(banks):
            tk = g.stt(self.yT[:, k, 0:T], self.xT[:, k, 0:T], ALPHA * f, ps[:, 0:T], ALU.mult, ALU.add, tp)
            g.free(b, tk)
            yt.append(tk)
        b, ps, w = g.bank()
        for k in range(8):
            tp = g.mm(ps[:, 0:T], [(self.ones, self.yT[:, k, 0:T])], yt[k], *w, first=k == 0, final=k == 7,
                      inc=k == 7)
        yt = [g.stt(self.yT[:, k, 0:T], ps[:, 0:T], -1.0 / D, self.yT[:, k, 0:T], ALU.mult, ALU.add, tp)
              for k in range(8)]
        g.free(b, yt[7])
        b, ps, tp = self.rms(self.yT, yt, 1.0 / D, f * f * 1e-5)
        for k in range(8):
            tk = g.stt(self.yT[:, k, 0:T], self.yT[:, k, 0:T], self.col(f"ln{n}_g_2", k), ps[:, 0:T],
                       ALU.mult, ALU.mult, tp)
            self.xtok[k] = g.act(self.xT[:, k, 0:T], self.yT[:, k, 0:T], ACT.Identity, tk,
                                 bias=self.col(f"ln{n}_b_2", k))
        g.free(b, tk)

    def splitx(self):
        T = self.T
        return [self.g.split(self.H[:, k, 0:T], self.L[:, k, 0:T], self.xT[:, k, 0:T], self.xtok[k])
                for k in range(8)]

    def colunit(self, name, j):
        w, hi, lo, t = self.g.weight(self.d[name][j])
        return w, [x.rearrange("p (k n) -> p k n", k=8) for x in (hi, lo)], t

    def rowunit(self, name, j):
        w, hi, lo, t = self.g.weight(self.d[name][j])
        return w, (hi, lo), t

    def gettmp(self):
        i = self.ntmp % 4
        self.ntmp += 1
        return i, self.tmp[:, i, :], self.tmp_free[i]

    def down(self, name, src, toks, T, nk):
        g = self.g
        banks = [g.bank() for _ in range(8)]
        ends = nk > 8
        groups = [range(3)] * ends + [(k,) for k in range(3 * ends, nk - 3 * ends)] + [range(nk - 3, nk)] * ends
        for ks in groups:
            us = [self.rowunit(name, k) for k in ks]
            fin = ks[-1] == nk - 1
            for n, (b, ps, wt) in enumerate(banks):
                c = slice(n * P, (n + 1) * P)
                for k, (i, w, t) in zip(ks, us):
                    end = k == nk - 1
                    tk = g.mm3(ps[:, 0:T], [x[:, c] for x in w], [x[:, k, 0:T] for x in src], t, toks[k], *wt,
                               first=k == 0, final=end, inc=end or n == 7)
                if fin:
                    banks[n] = (b, ps, tk)
            for n, (i, w, t) in enumerate(us):
                g.free_weight(i, ("pe", g.n["pe"] - len(us) + 1 + n))
        return banks

    def ffn(self, ht, wg, wu, wd, later=None):
        g, T = self.g, self.T
        src = self.hp
        hf = []
        tr = None
        held = []
        for js in ((0, 1),) + tuple((j,) for j in range(2, NF)):
            us = [[self.colunit(name, j), g.bank()] for j in js for name in (wg, wu)]
            for k in range(8):
                for (i, w, t), (b, ps, wt) in us:
                    if len(js) > 1:
                        g.mm3(ps[:, 0:T], [x[:, k, :] for x in w], [x[:, k, 0:T] for x in src], t, ht[k], *wt,
                              first=k == 0, final=k == 7, inc=k == 7)
            if len(js) == 1:
                for (i, w, t), (b, ps, wt) in us:
                    for k in range(8):
                        g.mm3(ps[:, 0:T], [x[:, k, :] for x in w], [x[:, k, 0:T] for x in src], t, ht[k], *wt,
                              first=k == 0, final=k == 7, inc=k == 7)
            tps = [("pe", g.n["pe"] - len(us) + 1 + n) for n in range(len(us))]
            for n, ((i, w, t), _) in enumerate(us):
                g.free_weight(i, tps[n])
            held += [(j, us[2 * n][1], us[2 * n + 1][1], tps[2 * n], tps[2 * n + 1]) for n, j in enumerate(js)]
            if later and js[0] == 0:
                continue
            if later and js[0] == 2:
                tr = later()
            r = self.rstd[:, 2, 0:T]
            for j, (bg, pg, _), (bu, pu, _), tg, tu in held:
                i, tmp, tf = self.gettmp()
                tmp = tmp[:, 0:T]
                if later:
                    t = g.tt(tmp, pg[:, 0:T], r, ALU.mult, tg, tr, tf)
                    g.free(bg, t)
                    t = g.act(tmp, tmp, ACT.Silu, t)
                else:
                    t = g.act(tmp, pg[:, 0:T], ACT.Silu, tg, tf)
                    g.free(bg, t)
                t = g.tt(tmp, tmp, pu[:, 0:T], ALU.mult, t, tu)
                g.free(bu, t)
                t = g.split(self.hf[0][:, j, 0:T], self.hf[1][:, j, 0:T], tmp, t)
                self.tmp_free[i] = t
                hf.append(t)
            held = []
        self.sqtok = ("pe", g.n["pe"])
        return self.down(wd, self.hf, hf, T, NF)

    def ffn1(self, n):
        ht, later = self.lazynorm(n + "_pre_g")
        banks = self.ffn(ht, n + "_w_gate", n + "_w_up", n + "_w_down", later)
        self.postnorm(banks, n + "_post_g", 0, True, scaled=True)

    def ffn2(self, n, ln):
        banks = self.ffn(self.splitx(), n + "_w_gate_2", n + "_w_up_2", n + "_w_out_2")
        self.layernorm(banks, ln, True)

    def ffn3(self, layer, i):
        ht, later = self.lazynorm("norm_gains_3", layer * 6 + 4 * i)
        banks = self.ffn(ht, f"g3_{layer}{i}", f"u3_{layer}{i}", f"d3_{layer}{i}", later)
        self.postnorm(banks, "norm_gains_3", layer * 6 + 4 * i + 1, True, scaled=True)

    def enter3(self):
        self.g.fence()
        self.load_x(self.d["meta_tokens_3"], T1)
        self.T = T3


    def together(self, *work, lead=1):
        for i, w in enumerate(work):
            for _ in range(lead * (len(work) - 1 - i)):
                next(w)
        work = list(work)
        while work:
            work = [w for w in work if next(w, self) is not self]

    def softmax(self, S, H, nk, rows, toks, n, sink=None, gate=None, floor=False):
        g = self.g
        sm = self.small[0:rows, 64 * n:64 * n + 64]
        mx, den, e = sm[:, 0:H], sm[:, 16:16 + H], sm[:, 32:32 + H]
        tk = g.red(mx, S, ALU.max, *toks)
        if sink is not None:
            tk = g.tt(mx, mx, sink, ALU.max, tk)
        if floor:
            tk = g.ts(mx, mx, -1e20, None, ALU.max, None, tk)
        tk = g.ts(mx, mx, -1.0, None, ALU.mult, None, tk)
        if sink is not None:
            ts = g.tt(e, sink, mx, ALU.add, tk)
            te = g.act(e, e, ACT.Exp, ts)
        for h in range(H):
            ta = g.act(S[:, h, :], S[:, h, :], ACT.Exp, tk, bias=mx[:, h:h + 1], accum_out=den[:, h:h + 1])
        if sink is not None:
            ta = g.tt(den, den, e, ALU.add, ta)
        yield
        if floor:
            ta = g.ts(den, den, 1e-30, None, ALU.max, None, ta)
        ta = g.recip(den, den, ta)
        if gate is not None:
            ta = g.tt(den, den, gate, ALU.mult, ta)
        for h in range(H):
            tk = g.ts(S[:, h, :], S[:, h, :], den[:, h:h + 1], None, ALU.mult, None, ta)
        return tk

    def turn(self, dst, src, rows, widths, toks, wfree=()):
        g = self.g
        b, ps, w = g.bank()
        out = []
        for i, (c, wd) in enumerate(widths):
            tp = g.tr(ps[0:wd, i * P:i * P + rows], src[:, c:c + wd], self.ident[0:rows, 0:rows], *toks, *w)
        e = ("dve", "act")[self.nturn % 2]
        self.nturn += 1
        full = [i for i, (c, wd) in enumerate(widths) if wd == P]
        if full:
            n = len(full)
            tk = g.cp(dst[:, 0:n, 0:rows], ps[:, 0:n * P].rearrange("p (n r) -> p n r", n=n)[:, :, 0:rows], tp,
                      *wfree, e=e)
            out.append(tk)
        for i, (c, wd) in enumerate(widths):
            if wd != P:
                tk = g.cp(dst[0:wd, i, 0:rows], ps[0:wd, i * P:i * P + rows], tp, *wfree, e=e)
                out.append(tk)
        g.free(b, *out)
        return out

    sqtok = None
    nturn = 0

    def linear(self, name, n, src, toks, T):
        g = self.g
        for j in range(n):
            i, w, t = self.colunit(name, j)
            b, ps, wt = g.bank()
            for kk in range(8):
                tp = g.mm3(ps[:, 0:T], [x[:, kk, :] for x in w], [x[:, kk, 0:T] for x in src], t, toks[kk], *wt,
                           first=kk == 0, final=kk == 7, inc=kk == 7)
            g.free_weight(i, tp)
            yield j, b, ps, tp

    def nsa(self):
        g, A = self.g, self.A
        at = [0]

        def buf(n, *shape):
            v = A[:, at[0]:at[0] + n]
            at[0] += n
            if shape:
                names = "abcd"[:len(shape)]
                v = v.rearrange("p (%s) -> p %s" % (" ".join(names), " ".join(names)), **dict(zip(names, shape)))
            return v

        qT = buf(4 * T1, 4, T1)
        kD = {s: buf(2 * T1, 2, T1) for s in ("ks", "kw")}
        kp = {s: buf(2 * T1, 2, T1) for s in ("kc", "vc")}
        V = buf(2 * T1, 2, T1)
        gate = buf(2 * 24, 2, 8, 3)
        z = buf(4 * 258, 4, 258)
        cb = buf(4 * T1, 4, T1)
        hid = buf(64, 2, 2, 16)
        kcT = buf(16 * 2, 2, 16)
        vc2 = buf(2 * 64, 2, 64)
        S1 = buf(8 * T1, 8, T1)
        S2 = buf(8 * T1, 8, T1)
        S3 = buf(8 * 16, 8, 16)
        PT = buf(4 * 5 * P, 4, 5, P)
        buf(2048)
        mix = (self.sqR, self.over("nsal", at[0] - 2048, 8, T1))
        ht = self.prenorm("l0_mix_pre_g")
        src = self.hp
        g.wait("act", [("pe", g.n["pe"])])
        g.wait("dve", [("pe", g.n["pe"])])

        i, (w,), t = g.unit((0, 192, 0, P, self.d["nsa_g"]))
        w = w.rearrange("p (k n) -> p k n", k=8)
        w1s = []

        def cmp_load(s):
            i2, (w1,), t1 = g.unit((0, SLOT, 0, P, self.d["cmp_w1_" + s]))
            w1s.append((i2, w1, t1))

        cmp_load("k")
        b, ps, wt = g.bank()
        for m in range(2):
            tp = g.mm(ps[:, m * 24:m * 24 + 24], [(self.sq[:, k, m * P:(m + 1) * P], w[:, k, :]) for k in range(8)], t,
                      *ht, *wt)
        tg = g.act(gate.rearrange("p a b c -> p (a b c)"), ps[:, 0:48], ACT.Sigmoid, tp)
        g.free(b, tg)
        g.free_unit(i, tp)
        cmp_load("v")
        w2 = self.cols[:, NCOL:NCOL + P]
        tkc = [None, None]

        def compressed():
            for s, name in enumerate(("kc", "vc")):
                i2, w1, t1 = w1s[s]
                w1 = w1.rearrange("p (j n) -> p j n", j=16)
                b, ps, wt = g.bank()
                pe_at = COLS["l0_cmp_pe_" + "kv"[s]][0]
                tp = g.mm(ps[:, 64:65], [(w1[:, j, :], self.cols[:, pe_at + j:pe_at + j + 1]) for j in range(16)], t1,
                          *wt)
                pb = self.small[:, 256 + s:257 + s]
                tb = g.cp(pb, ps[:, 64:65], tp)
                g.free(b, tb)
                b2, ps2, wt = g.bank()
                for gr in range(2):
                    tp = g.mm(ps2[:, gr * 16:gr * 16 + 15],
                              [(w1[:, j, :], kp[name][:, gr, 2 * j:2 * j + 16 * 14 + 1:16]) for j in range(16)], tkp,
                              *wt)
                g.free_unit(i2, tp)
                for gr in range(2):
                    th = g.act(hid[:, s, gr, 0:15], ps2[:, gr * 16:gr * 16 + 15], ACT.Gelu_apprx_tanh, tp, tb, bias=pb)
                g.free(b2, th)
                yield
                b, ps, wt = g.bank()
                if s == 0:
                    for gr in range(2):
                        tp = g.mm(ps[0:64, gr * 16:gr * 16 + 15], [(w2[:, 0:64], hid[:, s, gr, 0:15])], th, *wt)
                    p3 = ps[0:64, 0:32].rearrange("p (a b) -> p a b", a=2)[:, :, 0:15]
                    g.cp(kcT[0:64, :, 0:15], p3, tp)
                    tkc[s] = g.cp(kcT[64:128, :, 0:15], p3, tp)
                else:
                    for gr in range(2):
                        tp = g.mm(ps[0:15, gr * 64:gr * 64 + 64], [(hid[:, s, gr, 0:15], w2[:, 64:128])], th, *wt)
                    tkc[s] = g.cp(vc2[0:15, :, :], ps[0:15, 0:128].rearrange("p (a b) -> p a b", a=2), tp)
                g.free(b, tkc[s])
                yield

        cmp_ = compressed()
        tq = [None] * 4
        cu = {}
        for j, b, ps, tp in self.linear("nsa_in", 20, src, ht, T1):
            if j < 4:
                tk = g.act(qT[:, j, :], ps[:, 0:T1], ACT.Copy, tp, scale=0.125)
                tq[j] = tk
            elif j < 6:
                s = ("kc", "vc")[j - 4]
                for i in range(2):
                    rows = ps[64 * i:64 * i + 64, :]
                    g.cp(kp[s][0:64, i, 0:T1], rows[:, 0:T1], tp)
                    tk = g.cp(kp[s][64:128, i, 0:T1 - 1], rows[:, 1:T1], tp)
                tkp = tk
            elif j < 8:
                s = ("ks", "kw")[j - 6]
                for i in range(2):
                    rows = ps[64 * i:64 * i + 64, 0:T1]
                    g.cp(kD[s][0:64, i, :], rows, tp, e="act")
                    tk = g.cp(kD[s][64:128, i, :], rows, tp, e="act")
                tkd = tk
            elif j < 12:
                if j > 8:
                    next(cmp_, None)
                tk = g.cp(cb[:, j - 8, :], ps[:, 0:T1], tp, e="act")
                cu[j - 8] = tk
            elif j < 16:
                if j == 12:
                    tz = g.op("dve", lambda: self.g.nc.vector.memset(z[:, :, 0:2], 0.0))
                tk = g.cp(z[:, j - 12, 2:258], ps[:, 0:T1], tp)
            else:
                c = j - 16
                next(cmp_, None)
                tk = g.tt(z[:, c, 2:258], z[:, c, 2:258], ps[:, 0:T1], ALU.mult, tp, tz)
                g.free(b, tk)
                i, t, tf = self.gettmp()
                t = t[:, 0:T1]
                w = [self.col("l0_conv_w", r * 4 + c) for r in range(3)]
                tk = g.ts(t, z[:, c, 2:258], w[2], self.col("l0_conv_b", c), ALU.mult, ALU.add, tk, tf)
                tk = g.stt(t, z[:, c, 1:257], w[1], t, ALU.mult, ALU.add, tk)
                tk = g.stt(t, z[:, c, 0:256], w[0], t, ALU.mult, ALU.add, tk)
                tk = g.tt(t, t, cb[:, c, :], ALU.mult, tk, cu[c])
                tconv = g.split(mix[0][:, 4 + c, 0:T1], mix[1][:, 4 + c, 0:T1], t, tk)
                self.tmp_free[i] = tconv
                continue
            g.free(b, tk)
        for x in range(2):
            i, w, t = self.colunit("nsa_v", x)
            b, ps, wt = g.bank()
            for m in range(2):
                for k in range(8):
                    tp = g.mm3(ps[:, m * P:(m + 1) * P], [y[:, k, m * P:(m + 1) * P] for y in src],
                               [y[:, k, :] for y in w], t, *wt, first=k == 0, final=k == 7, inc=k == 7)
            tv = g.cp(V[:, :, x * P:(x + 1) * P], ps[:, 0:256].rearrange("p (m c) -> p m c", m=2), tp)
            g.free(b, tv)
            g.free_weight(i, tp)
        def heads(u):
            ptf = [None, None]
            so = None
            sl = slice(4 * u, 4 * u + 4)
            for m in range(2):
                nk = P * (m + 1)
                for h in range(4 * u, 4 * u + 4):
                    o = 64 * (h % 2)
                    q = qT[o:o + 64, h // 2, m * P:(m + 1) * P]
                    b, ps, wt = g.bank()
                    for x, s in enumerate(("ks", "kw")):
                        tp = g.mm(ps[:, x * 256:x * 256 + nk], [(q, kD[s][o:o + 64, u, 0:nk])], tkd, tq[h // 2], *wt)
                    for x, S in enumerate((S1, S2)):
                        tk = g.stt(S[:, h, 0:nk], self.c("alibi")[:, m * 256:m * 256 + nk], 0.5 ** (h + 1),
                                   ps[:, x * 256:x * 256 + nk], ALU.mult, ALU.add, tp, so)
                    g.free(b, tk)
                    b, ps, wt = g.bank()
                    tp = g.mm(ps[:, 0:15], [(q, kcT[o:o + 64, u, 0:15])], tkc[0], *wt)
                    tk = g.stt(S3[:, h, 0:15], self.c("alibi_cmp")[:, m * 16:m * 16 + 15], 0.5 ** (h + 1),
                               ps[:, 0:15], ALU.mult, ALU.add, tp, so)
                    g.free(b, tk)
                    if h % 2:
                        yield
                t1 = yield from self.softmax(S1[:, sl, 0:nk], 4, nk, P, [tk], 2 * u, gate=gate[:, m, sl, 1])
                t2 = yield from self.softmax(S2[:, sl, 0:nk], 4, nk, P, [tk], 2 * u + 1, gate=gate[:, m, sl, 2])
                t3 = yield from self.softmax(S3[:, sl, 0:15], 4, 15, P, [tk], 2 * u, gate=gate[:, m, sl, 0], floor=True)
                for h in range(4 * u, 4 * u + 4):
                    o = 64 * (h % 2)
                    pt = PT[:, 2 * u + h % 2]
                    wf = (ptf[h % 2],)
                    ta = self.turn(pt[:, 0:2], S1[:, h, :], P, [(c * P, P) for c in range(m + 1)], [t1, tg], wf)
                    tb = self.turn(pt[:, 2:4], S2[:, h, :], P, [(c * P, P) for c in range(m + 1)], [t2], wf)
                    tc = self.turn(pt[:, 4:5], S3[:, h, 0:15], P, [(0, 15)], [t3], wf)
                    yield
                    if h % 2 == 0:
                        bo, po, wt = g.bank()
                    pairs = []
                    for c in range(m + 1):
                        pairs.append((V[:, c, u * 64:u * 64 + 64], pt[:, c, :]))
                        pairs.append((V[:, c, P + u * 64:P + u * 64 + 64], pt[:, 2 + c, :]))
                    pairs.append((vc2[0:15, u, :], pt[0:15, 4, :]))
                    so = g.mm(po[o:o + 64, 0:P], pairs, tv, tkc[1], *ta, *tb, *tc, *wt)
                    ptf[h % 2] = so
                    if h % 2:
                        ty[h // 2] = g.split(mix[0][:, h // 2, m * P:(m + 1) * P], mix[1][:, h // 2, m * P:(m + 1) * P],
                                             po[:, 0:P], so)
                        g.free(bo, ty[h // 2])

        ty = [None] * 4
        self.together(heads(0), heads(1), lead=3)
        banks = self.down("nsa_out", mix, ty + [tconv] * 4, T1, 8)
        self.postnorm(banks, "l0_mix_post_g", 0, False)

    def tokmajor(self, name, src, toks):
        g = self.g
        banks = [[g.bank() for _ in range(2)] for _ in range(2)]
        for k in range(8):
            i, w, t = self.rowunit(name, k)
            for m in range(2):
                for h in range(2):
                    b, ps, wt = banks[m][h]
                    tk = g.mm3(ps[:, :], [x[:, k, m * P:(m + 1) * P] for x in src],
                               [x[:, h * 512:(h + 1) * 512] for x in w], t, toks[k], *wt,
                               first=k == 0, final=k == 7, inc=k == 7 or (m == 1 and h == 1))
                    if k == 7:
                        banks[m][h] = (b, ps, tk)
            g.free_weight(i, ("pe", g.n["pe"]))
        return banks

    def rwkv(self):
        g, A, nc = self.g, self.A, self.g.nc
        C0 = float(np.exp(np.float64(-0.5)))
        v3 = lambda o: A[:, o:o + 2048].rearrange("p (m c) -> p m c", m=2)
        r, k, v, a, lw, kk = [v3(2048 * i) for i in range(6)]
        W = 12288
        xx = self.yT
        xf = [A[:, W + 2048 * i:W + 2048 * i + 2048].rearrange("p (k t) -> p k t", k=8) for i in range(2)]
        xm = [self.hp, [self.over(f"xm{i}", W + 2048 * i, 8, T1) for i in range(2)]]
        ht = self.prenorm("l1_mix_pre_g")
        hT = self.sq
        g.ts(xx[:, :, 0:1], hT[:, :, 0:1], -1.0, None, ALU.mult, None, *ht)
        txx = g.tt(xx[:, :, 1:T1], hT[:, :, 0:T1 - 1], hT[:, :, 1:T1], ALU.subtract, *ht)
        xfree = [("pe", g.n["pe"]), None]
        count = [0]
        lf = self.Lf.rearrange("p k t -> p (k t)")

        def mixed(i, split=False):
            n = count[0] % 2
            count[0] += 1
            if not split:
                return n, xf[n], [g.stt(xf[n][:, q, 0:T1], xx[:, q, 0:T1], self.col("l1_mu", i * 8 + q),
                                        hT[:, q, 0:T1], ALU.mult, ALU.add, txx, xfree[n]) for q in range(8)]
            toks = []
            for q in range(8):
                x, v, tf = self.gettmp()
                t = g.stt(v[:, 0:T1], xx[:, q, 0:T1], self.col("l1_mu", i * 8 + q), hT[:, q, 0:T1],
                          ALU.mult, ALU.add, txx, tf)
                self.tmp_free[x] = g.split(xm[n][0][:, q, 0:T1], xm[n][1][:, q, 0:T1], v[:, 0:T1], t, xfree[n])
                toks.append(self.tmp_free[x])
            return n, xm[n], toks

        il, (lora,), tl = g.unit((0, SLOT, 0, P, self.d["lora1"]))
        lora = lora.rearrange("p (k n) -> p k n", k=8)
        lT = self.rstd.rearrange("p k t -> p (k t)")[:, 0:768].rearrange("p (j t) -> p j t", j=3)
        tlo = []
        for j, (i, c0, w, f) in enumerate(((1, 0, 64, ACT.Tanh), (4, 64, 64, ACT.Copy), (5, 128, 128, ACT.Sigmoid))):
            n, x, toks = mixed(i)
            b, ps, wt = g.bank()
            for q in range(8):
                tp = g.mm(ps[0:w, 0:T1], [(lora[:, q, c0:c0 + w], x[:, q, 0:T1])], tl, toks[q], *wt,
                          first=q == 0, final=q == 7, inc=q == 7)
            xfree[n] = tp
            tk = g.act(lT[0:w, j, :], ps[0:w, 0:T1], f, tp)
            g.free(b, tk)
            tlo.append(tk)
        g.free_unit(il, tp)
        ib, (wa,), tb = g.unit((0, 2048, 0, 65, self.d["lora2"]))
        tone = g.op("dve", lambda: nc.vector.memset(lT[64:65, 0:2, :], 1.0))
        for j, dst in ((0, lw), (1, a)):
            for m in range(2):
                for h in range(2):
                    b, ps, wt = g.bank()
                    x = lT[:, j, m * P:(m + 1) * P]
                    hs = slice(h * 512, (h + 1) * 512)
                    tp = g.mm(ps[:, :], [(x[0:65], wa[0:65, j * 1024 + h * 512:j * 1024 + h * 512 + 512])],
                              tb, tlo[j], tone, *wt)
                    tk = g.act(dst[:, m, hs], ps[:, :], ACT.Sigmoid, tp)
                    g.free(b, tk)
        ta_ = tk
        g.free_unit(ib, tp)
        xfree = [xfree[0], ("pe", g.n["pe"])]
        iv, (kkg, kag), tv = g.unit((0, 1024, 0, P, self.d["l1_k_k"].broadcast_to([P, 1024])),
                                    (1024, 1024, 0, P, self.d["l1_k_a"].broadcast_to([P, 1024])))
        iw, (rkg,), tw = g.unit((0, 1024, 0, P, self.d["l1_r_k"].broadcast_to([P, 1024])))
        s16 = self.small
        bonus = s16[:, 256:288].rearrange("p (m h) -> p m h", m=2)
        sc = A[:, W + 4096:W + 6144].rearrange("p (m c) -> p m c", m=2)
        h3 = lambda ap: ap.rearrange("p (h j) -> p h j", j=64)
        got = {}

        def keys(m):
            t = g.tt(kk[:, m, :], k[:, m, :], kkg, ALU.mult, tv, *got["l1_w_k"])
            t = g.act(sc[:, m, :], kk[:, m, :], ACT.Square, t)
            ss = s16[:, 16 * m:16 * m + 16]
            t = g.red(ss, h3(sc[:, m, :]), ALU.add, t)
            t = g.ts(ss, ss, 1e-12, None, ALU.max, None, t)
            t = g.recip(ss, ss, t)
            t = g.act(ss, ss, ACT.Sqrt, t)
            g.tt(h3(kk[:, m, :]), h3(kk[:, m, :]), bc(ss, 64), ALU.mult, t)
            t = g.stt(sc[:, m, :], a[:, m, :], -1.0, kag, ALU.add, ALU.mult, ta_)
            t = g.stt(k[:, m, :], sc[:, m, :], 1.0, k[:, m, :], ALU.add, ALU.mult, t)
            return g.tt(a[:, m, :], a[:, m, :], kk[:, m, :], ALU.mult)

        def extra(m):
            t = g.tt(sc[:, m, :], r[:, m, :], k[:, m, :], ALU.mult, *got["l1_w_r"])
            t = g.tt(sc[:, m, :], sc[:, m, :], rkg, ALU.mult, t, tw)
            return g.red(bonus[:, m, :], h3(sc[:, m, :]), ALU.add, t)

        for i, name, dst in ((2, "l1_w_k", k), (0, "l1_w_r", r), (3, "l1_w_v", v)):
            n, x, toks = mixed(i, True)
            if i == 0:
                keys(0)
            if i == 3:
                g.free_unit(iv, keys(1))
                extra(0)
            banks = self.tokmajor(name, x, toks)
            xfree[n] = ("pe", g.n["pe"])
            got[name] = []
            for m in range(2):
                for h in range(2):
                    b, ps, tp = banks[m][h]
                    tk = g.cp(dst[:, m, h * 512:(h + 1) * 512], ps[:, :], tp, e=("dve", "act")[h])
                    g.free(b, tk)
                    got[name].append(tk)
        g.free_unit(iw, extra(1))
        g.fence()
        ig, (lng, lnb), tln = g.unit((0, 1024, 0, P, self.d["l1_lnx_g"].broadcast_to([P, 1024])),
                                     (1024, 1024, 0, P, self.d["l1_lnx_b"].broadcast_to([P, 1024])))
        i2, (g2,), tg2 = g.unit((0, 1024, 0, P, self.d["l1_w_g2"]))
        fl = self.yT.rearrange("p k t -> p (k t)")
        ST = self.sq_[0:64, 0:1024].rearrange("p (h i) -> p h i", h=16)
        t0 = g.op("dve", lambda: nc.vector.memset(ST, 0.0))
        m64 = self.c("m64")
        p4 = lambda x: x[:, :].rearrange("p (h c) -> p h c", h=4)

        def heads(n, hgs):
            o = W + 4096 * n
            ART = A[:, o:o + 1024].rearrange("p (h i t) -> p h i t", h=4, i=2)
            bk = A[:, o + 1024:o + 2048]
            BK = bk.rearrange("p (i h t) -> p i h t", i=2, h=4)
            Tm, Tt = p4(bk[:, 0:512]), p4(bk[:, 512:1024])
            M4 = p4((A[:, W + 2048:W + 4096], self.Hf.rearrange("p k t -> p (k t)")[:, 0:2048])[n])
            vec = (lf, fl)[n][:, 0:1536].rearrange("p (i c) -> p i c", i=6)
            exf = (self.tmp.rearrange("p k t -> p (k t)")[:, 0:1024], self.sq_[:, 1024:2048])[n]
            ex = exf.rearrange("p (i c) -> p i c", i=4)
            Mb, Wm = p4(exf[:, 0:512]), p4(exf[:, 512:1024])
            MV, TMV, U = vec[:, 1, :], vec[:, 2, :], vec[:, 3, :]
            Y1 = exf[:, 0:256]
            TAT = p4(exf[0:64, 256:768])
            mu, var = s16[:, 64 * n:64 * n + 4], s16[:, 64 * n + 16:64 * n + 20]
            sqs = exf[:, 768:1024]
            half = self.c("half").broadcast_to([P, 4])
            pc = s16[0:64, 320 + 8 * n:328 + 8 * n].rearrange("p (h c) -> p h c", h=4)
            ty = None
            for hg in hgs:
                tst = t0
                for m in range(2):
                    cs = slice(hg * 256, hg * 256 + 256)
                    hs = [slice(hg * 256 + 64 * h, hg * 256 + 64 * h + 64) for h in range(4)]
                    l = lw[:, m, cs]
                    b1, p1, w1 = g.bank()
                    g.mm(p1[:, 0:256], [(m64[:, 0:128], l)], *w1, inc=False)
                    t1 = g.mm(p1[:, 256:512], [(m64[:, 128:256], l)])
                    b2, p2, w2 = g.bank()
                    g.mm(p2[:, 0:256], [(self.c("suf64"), l)], *w2, inc=False)
                    for h in range(4):
                        t2 = g.mm(p2[0:64, 256 + 2 * h:258 + 2 * h], [(lw[:, m, hs[h]], self.c("chunk"))])
                    yield
                    t = g.act(ex[:, 0:2, :], p1[:, :].rearrange("p (i c) -> p i c", i=2), ACT.Exp, t1, ty, scale=-C0)
                    ta = g.act(ex[:, 2, :], p1[:, 256:512], ACT.Exp, t1, scale=C0)
                    tb = g.act(ex[:, 3, :], p2[:, 0:256], ACT.Exp, t2, scale=-C0)
                    tc = g.act(pc, p2[0:64, 256:264].rearrange("p (h c) -> p h c", h=4), ACT.Exp, t2, scale=-C0)
                    g.free(b1, ta)
                    g.free(b2, tc)
                    tv_ = []
                    for i, (x, e, w) in enumerate(((kk, 0, t), (r, 1, t), (a, 2, ta), (k, 2, ta), (a, 3, tb), (k, 3, tb))):
                        tv_.append(g.tt(vec[:, i, :], x[:, m, cs], ex[:, e, :], ALU.mult, w, ty,
                                        e="pool" if i > 3 else "dve"))
                    for i in range(4):
                        b, ps, w = g.bank()
                        for h in range(4):
                            tp = g.tr(ps[0:64, h * P:(h + 1) * P], vec[:, i, 64 * h:64 * h + 64], self.ident, tv_[i],
                                      *w)
                        dst = ART[0:64, :, i, :] if i < 2 else BK[0:64, i - 2, :, :]
                        tt_ = g.cp(dst, p4(ps[0:64, :]), tp, e=("dve", "act")[i % 2])
                        g.free(b, tt_)
                        if i == 2:
                            tA = tt_
                        if i % 2:
                            yield
                    for h in range(4):
                        b, ps, w = g.bank()
                        rhs = ART[0:64, h].rearrange("p i t -> p (i t)")
                        g.mm(ps[:, 0:256], [(BK[0:64, 0, h, :], rhs)], tt_, tA, *w, inc=False)
                        tp = g.mm(ps[:, 256:512], [(BK[0:64, 1, h, :], rhs)])
                        tk = g.tt(M4[:, h, :].rearrange("p (i c) -> p i c", i=2),
                                  ps[:, :].rearrange("p (i c) -> p i c", i=2), bc_mid(m64, 2), ALU.mult, tp)
                        g.free(b, tk)
                    for lv in range(6):
                        mask = self.c("level", lv)
                        tmb = g.tt(Mb, M4[:, :, 0:128], bc_mid(mask, 4), ALU.mult, tk, tv_[5])
                        idb = bc_mid(self.ident, 4)
                        b, ps, w = g.bank()
                        for h in range(4):
                            rhs = self.ident if lv == 0 else Tm[:, h, :]
                            tp = g.mm(ps[:, h * P:(h + 1) * P], [(Mb[:, h, :], rhs)], tmb, *w, inc=h == 3)
                        yield
                        if lv == 0:
                            g.tt(Tm, idb, p4(ps), ALU.subtract, tp)
                            tk = g.tt(Tt, idb, Mb, ALU.subtract, tmb)
                            g.free(b, tk)
                            continue
                        tw_ = g.cp(Wm, p4(ps), tp, e="act")
                        g.free(b, tw_)
                        if lv < 5:
                            bm, pm, w = g.bank()
                            for h in range(4):
                                tpm = g.mm(pm[:, h * P:(h + 1) * P], [(Tt[:, h, :], Wm[:, h, :])], tw_, tk, *w,
                                           inc=h == 3)
                        b, ps, w = g.bank()
                        for h in range(4):
                            tp = g.mm(ps[:, h * P:(h + 1) * P], [(Wm[:, h, :], Tt[:, h, :])], tw_, tk, *w, inc=h == 3)
                        yield
                        if lv < 5:
                            g.free(bm, g.tt(Tm, Tm, p4(pm), ALU.subtract, tpm))
                        tk = g.tt(Tt, Tt, p4(ps), ALU.subtract, tp)
                        g.free(b, tk)
                    b, ps, w = g.bank()
                    for h in range(4):
                        tp = g.mm(ps[:, 64 * h:64 * h + 64], [(M4[:, h, 256:384], v[:, m, hs[h]])], *w)
                    yield
                    t = g.cp(MV, ps[:, 0:256], tp, e="act")
                    g.free(b, t)
                    b, ps, w = g.bank()
                    for h in range(4):
                        tp = g.mm(ps[:, 64 * h:64 * h + 64], [(Tt[:, h, :], MV[:, 64 * h:64 * h + 64])], t, tk, *w)
                    bt, pt, w = g.bank()
                    for h in range(4):
                        tpt = g.mm(pt[0:64, h * P:(h + 1) * P], [(vec[:, 0, 64 * h:64 * h + 64], Tt[:, h, :])], *w)
                    yield
                    tmv = g.cp(TMV, ps[:, 0:256], tp, e="act")
                    g.free(b, tmv)
                    tat = g.cp(TAT, p4(pt[0:64, :]), tpt)
                    g.free(bt, tat)
                    by, py, wy = g.bank()
                    for c in range(2):
                        o = 64 * c
                        b, ps, w = g.bank()
                        for h in range(4):
                            st = ST[:, hg * 4 + h, :]
                            tp = g.mm(ps[o:o + 64, 64 * h:64 * h + 64], [(TAT[:, h, o:o + 64], st)], tst, tat, *w)
                        for h in range(4):
                            st = ST[:, hg * 4 + h, :]
                            ty = g.mm(py[o:o + 64, 64 * h:64 * h + 64], [(ART[0:64, h, 1, o:o + 64], st)], *wy)
                        yield
                        tu = g.stt(U[o:o + 64, :], ps[o:o + 64, 0:256], -1.0, TMV[o:o + 64, :], ALU.mult,
                                   ALU.subtract, tp, tmv)
                        g.free(b, tu)
                        b, ps, w = g.bank()
                        for h in range(4):
                            hh = slice(64 * h, 64 * h + 64)
                            tp = g.mm(ps[0:64, hh], [(vec[o:o + 64, 4, hh], U[o:o + 64, hh]),
                                                     (vec[o:o + 64, 5, hh], v[o:o + 64, m, hs[h]])], tu, tv_[5], *w)
                        yield
                        sg = ST[:, hg * 4:hg * 4 + 4, :]
                        t = g.tt(sg, sg, bc(pc[:, :, c], 64), ALU.mult, ty, tc)
                        tst = g.tt(sg, sg, ps[0:64, 0:256].rearrange("p (h i) -> p h i", h=4), ALU.add, t, tp)
                        g.free(b, tst)
                    t = g.cp(Y1, py[:, 0:256], ty, e="act")
                    g.free(by, t)
                    b, ps, w = g.bank()
                    for h in range(4):
                        hh = slice(64 * h, 64 * h + 64)
                        tp = g.mm(ps[:, hh], [(M4[:, h, 128:256], U[:, hh]), (M4[:, h, 384:512], v[:, m, hs[h]])],
                                  tu, *w)
                    yield
                    y, vb = r[:, m, cs], v[:, m, cs]
                    t = g.tt(y, Y1, ps[:, 0:256], ALU.add, tp, t)
                    g.free(b, t)
                    b, ps, w = g.bank()
                    tgt = g.mm(ps[:, 0:256], [(lT[:, 2, m * P:(m + 1) * P], g2[:, cs])], tg2, tlo[2], *w)
                    tvb = g.tt(h3(vb), h3(vb), bc(bonus[:, m, 4 * hg:4 * hg + 4], 64), ALU.mult, tp, e="pool")
                    t = g.red(mu, h3(y), ALU.add, t)
                    t = g.ts(mu, mu, 1.0 / 64, None, ALU.mult, None, t)
                    t = g.tt(h3(y), h3(y), bc(mu, 64), ALU.subtract, t)
                    t = g.act(sqs, y, ACT.Square, t)
                    yield
                    t = g.red(var, h3(sqs), ALU.add, t)
                    t = g.ts(var, var, 1.0 / 64, 64e-5, ALU.mult, ALU.add, t)
                    t = g.tt(var, var, half, ALU.pow, t, e="pool")
                    yield
                    t = g.tt(h3(y), h3(y), bc(var, 64), ALU.mult, t)
                    t = g.tt(y, y, lng[:, cs], ALU.mult, t, tln)
                    t = g.tt(y, y, lnb[:, cs], ALU.add, t)
                    t = g.tt(y, y, vb, ALU.add, t, tvb)
                    ty = g.tt(y, y, ps[:, 0:256], ALU.mult, t, tgt)
                    g.free(b, ty)
                    done.append(ty)

        done = []
        self.together(heads(0, (0, 1)), heads(1, (2, 3)), lead=3)
        g.fence()
        g.free_unit(i2, done[-1])
        g.free_unit(ig, done[-1])
        toks = self.turn_back(r, [done[-1]] * 2, self.hp)
        banks = self.down("l1_w_o", self.hp, toks, T1, 8)
        self.postnorm(banks, "l1_mix_post_g", 0, False)

    def turn_back(self, y, ty, dst):
        g = self.g
        toks = []
        for q in range(8):
            b, ps, w = g.bank()
            for m in range(2):
                tp = g.tr(ps[:, m * P:(m + 1) * P], y[:, m, q * P:(q + 1) * P], self.ident, ty[m], *w)
            tk = g.split(dst[0][:, q, 0:T1], dst[1][:, q, 0:T1], ps[:, 0:T1], tp)
            g.free(b, tk)
            toks.append(tk)
        return toks
    def carve(self, start, limit=None):
        limit = limit or self.NA
        pos = self.pos = [start]

        def buf(n, *shape):
            v = self.A[:, pos[0]:pos[0] + n]
            pos[0] += n
            assert pos[0] <= limit, pos[0]
            if shape:
                names = "abcd"[:len(shape)]
                v = v.rearrange("p (%s) -> p %s" % (" ".join(names), " ".join(names)), **dict(zip(names, shape)))
            return v

        return buf

    def softplus(self, x, t1, t2, *toks):
        g = self.g
        t = g.act(t1, x, ACT.Abs, *toks)
        t = g.act(t1, t1, ACT.Exp, t, scale=-1.0)
        t = g.act(t1, t1, ACT.Ln, t, bias=1.0)
        t = g.stt(x, x, 0.0, t1, ALU.max, ALU.add, t)
        return t

    def hybrid(self):
        g, nc = self.g, self.g.nc
        xT, xt = self.xT, self.splitx()
        X = self.hp
        mem = self.carve(0)
        merged = mem(2048, 8, T1)
        fl = lambda v: v.rearrange("p k t -> p (k t)")
        buf = self.carve(2048)
        u = buf(4 * 260, 4, 260)
        xo = self.pos[0]
        xs = buf(2048, 8, T1)
        BC = buf(2048, 8, T1)
        xdt = buf(2048, 2, 1024)
        Bt = buf(512)
        xds = buf(1024)
        S0 = buf(1024)
        GL = buf(1024, 2, 4, P)
        CS = buf(1024, 2, 4, P)
        Gm = buf(256, 2, P)
        iw, (tw, kw), tt_ = g.unit((0, 256, 0, P, self.d["tokw"]), (256, 512, 0, P, self.d["kidx"]))
        tw = tw.rearrange("p (k n) -> p k n", k=8)
        kw = kw.rearrange("p (k n) -> p k n", k=8)
        s = self.small
        dt = s[:, 0:32].rearrange("p (m h) -> p m h", m=2)
        widx = s[:, 32:64].rearrange("p (m h) -> p m h", m=2)
        scr = s[:, 64:96].rearrange("p (m h) -> p m h", m=2)
        av = s[:, 96:128].rearrange("p (m h) -> p m h", m=2)
        acs = s[:, 128:160].rearrange("p (m h) -> p m h", m=2)
        dec = s[:, 160:176]
        ah = s[:, 176:192]
        rw = lambda n: self.rows[:, ROWS[n][0]:ROWS[n][0] + 16]
        ki = self.rstd[:, 2, 0:T1]
        yss = buf(2048, 8, T1)
        yp = [self.over("yss" + "hl"[i], xo + 2048 * i, 8, T1) for i in range(2)]
        b, ps, w = g.bank()
        for m in range(2):
            tp = g.mm(ps[:, 32 * m:32 * m + 32], [(xT[:, k, m * P:(m + 1) * P], tw[:, k, :]) for k in range(8)], tt_,
                      *w, *xt)
        ps2 = ps[:, 0:64].rearrange("p (m n) -> p m n", m=2)
        t = g.tt(dt, ps2[:, :, 0:16], bc_mid(rw("dt_bias_2"), 2), ALU.add, tp)
        tw_ = g.ts(widx, ps2[:, :, 16:32], 0.25, None, ALU.mult, None, tp)
        g.free(b, tw_)
        b, ps, w = g.bank()
        tp = g.mm(ps[0:64, 0:T1], [(kw[:, k, :], xT[:, k, 0:T1]) for k in range(8)], *w)
        g.free_unit(iw, tp)
        g.cp(ki[0:64, :], ps[0:64, 0:T1], tp, e="act")
        tki = g.cp(ki[64:128, :], ps[0:64, 0:T1], tp, e="act")
        g.free(b, tki)
        t = self.softplus(dt, scr, None, t)
        ta = g.act(ah, rw("a_log_2"), ACT.Exp)
        ta = g.ts(ah, ah, -1.0, None, ALU.mult, None, ta)
        ta = g.tt(av, dt, bc_mid(ah, 2), ALU.mult, ta, t)
        b, ps, w = g.bank()
        for m in range(2):
            tp = g.mm(ps[:, 16 * m:16 * m + 16], [(self.c("tri128"), av[:, m, :])], ta, *w)
        tp = g.mm(ps[:, 32:48], [(self.c("suf128"), av[:, 0, :])])
        tacs = g.cp(acs, ps[:, 0:32].rearrange("p (m h) -> p m h", m=2), tp)
        tdec = g.act(dec, ps[:, 32:48], ACT.Exp, tp, tacs)
        g.free(b, tdec)
        tz = g.op("dve", lambda: nc.vector.memset(u[:, :, 0:3], 0.0))
        ufree = [None] * 4
        txb = [None] * 16
        for j, b, ps, tp in self.linear("xbc", 16, X, xt, T1):
            uu = u[:, j % 4, :]
            t = g.cp(uu[:, 3:259], ps[:, 0:T1], tp, ufree[j % 4], e="act")
            g.free(b, t)
            i, v, tf = self.gettmp()
            v = v[:, 0:T1]
            wc = [self.col("conv_w_2", r * 16 + j) for r in range(4)]
            t = g.ts(v, uu[:, 3:259], wc[3], self.col("conv_b_2", j), ALU.mult, ALU.add, t, tf)
            for r in (2, 1, 0):
                t = g.stt(v, uu[:, r:r + T1], wc[r], v, ALU.mult, ALU.add, t, tz)
            ufree[j % 4] = t
            dst = xs[:, j, :] if j < 8 else BC[:, j - 8, :]
            txb[j] = g.act(dst, v, ACT.Silu, t)
            self.tmp_free[i] = txb[j]
        BT, CT = BC[:, 0:4, :], BC[:, 4:8, :]
        for m in range(2):
            for hf in range(2):
                b, ps, w = g.bank()
                for q in range(4):
                    tp = g.tr(ps[:, q * P:(q + 1) * P], xs[:, 4 * hf + q, m * P:(m + 1) * P], self.ident,
                              txb[4 * hf + q], *w)
                txd = g.tt(xdt[:, m, hf * 512:(hf + 1) * 512].rearrange("p (h j) -> p h j", h=8),
                           ps[:, :].rearrange("p (h j) -> p h j", h=8), bc(dt[:, m, 8 * hf:8 * hf + 8], 64),
                           ALU.mult, tp)
                g.free(b, txd)
        b, ps, w = g.bank()
        for q in range(4):
            tp = g.tr(ps[:, q * P:(q + 1) * P], BT[:, q, 0:P], self.ident, txb[8 + q], *w)
        tbt = g.cp(Bt, ps[:, :], tp, e="act")
        g.free(b, tbt)
        txs = g.tt(xds.rearrange("p (h j) -> p h j", h=16), xdt[:, 0, :].rearrange("p (h j) -> p h j", h=16),
                   bc(dec, 64), ALU.mult, tdec, txd)
        for hf in range(2):
            b, ps, w = g.bank()
            for q in range(2):
                gr = 2 * hf + q
                tp = g.mm(ps[:, q * 256:(q + 1) * 256], [(Bt[:, gr * P:(gr + 1) * P], xds[:, gr * 256:(gr + 1) * 256])],
                          tbt, txs, *w)
            ts0 = g.cp(S0[:, hf * 512:(hf + 1) * 512], ps[:, :], tp, e="act")
            g.free(b, ts0)
        ty = [None] * 8

        def groups(i):
            gfree = None
            for m in range(2):
                tc = slice(m * P, (m + 1) * P)
                for gr in (2 * i, 2 * i + 1):
                    b, ps, w = g.bank()
                    tp = g.mm(ps[:, 0:P], [(BT[:, gr, tc], CT[:, gr, tc])], txb[8 + gr], txb[12 + gr], *w)
                    tg = g.tt(Gm[:, i, :], ps[:, 0:P], self.c("tri128"), ALU.mult, tp, gfree)
                    g.free(b, tg)
                    b, ps, w = g.bank()
                    for r in range(4):
                        h = 4 * gr + r
                        tp = g.mm(ps[:, r * P:(r + 1) * P],
                                  [(av[:, m, h:h + 1].broadcast_to([P, P]), self.c("tri128"))], *w)
                    yield
                    for r in range(4):
                        h = 4 * gr + r
                        t = g.ts(GL[:, i, r, :], ps[:, r * P:(r + 1) * P], acs[:, m, h:h + 1], 0.0, ALU.subtract,
                                 ALU.min, tp, tacs, gfree)
                    if m:
                        tcs = g.act(CS[:, i], ps[:, :].rearrange("p (r t) -> p r t", r=4), ACT.Exp, tp, t, gfree)
                        g.free(b, tcs)
                    else:
                        g.free(b, t)
                    t = g.act(GL[:, i], GL[:, i], ACT.Exp, t)
                    yield
                    if m:
                        tcs = g.tt(CS[:, i], CS[:, i], bc_mid(CT[:, gr, tc], 4), ALU.mult, tcs, e="pool")
                    else:
                        tcs = None
                    tgl = g.tt(GL[:, i], GL[:, i], bc_mid(Gm[:, i, :], 4), ALU.mult, t, tg)
                    for r in range(0, 4, 2):
                        b, ps, w = g.bank()
                        for h in (4 * gr + r, 4 * gr + r + 1):
                            o = 64 * (h % 2)
                            pairs = [(xdt[:, m, h * 64:h * 64 + 64], GL[:, i, h % 4, :])]
                            if m:
                                pairs.append((S0[:, h * 64:h * 64 + 64], CS[:, i, h % 4, :]))
                            tp = g.mm(ps[o:o + 64, 0:P], pairs, tgl, tcs, ts0, txd, *w)
                        q = 2 * gr + r // 2
                        ty[q] = g.stt(yss[:, q, tc], xs[:, q, tc], self.col("d_skip_2c", q), ps[:, 0:P], ALU.mult,
                                      ALU.add, tp)
                        g.free(b, ty[q])
                    gfree = tp
                    yield

        self.together(groups(0), groups(1))
        for j, b, ps, tp in self.linear("z_2", 8, X, xt, T1):
            i, v, tf = self.gettmp()
            t = g.act(v[:, 0:T1], ps[:, 0:T1], ACT.Silu, tp, tf)
            g.free(b, t)
            ty[j] = g.tt(yss[:, j, 0:T1], yss[:, j, 0:T1], v[:, 0:T1], ALU.mult, t, ty[j])
            self.tmp_free[i] = ty[j]
            ts_ = g.act(self.sq[:, j, 0:T1], yss[:, j, 0:T1], ACT.Square, ty[j])
            if j % 2:
                b, ps, w = g.bank()
                tp = g.mm(ps[:, 0:T1], [(self.ones, self.sq[:, q, 0:T1]) for q in (j - 1, j)], ts_, *w)
                r_ = self.rstd[:, (j // 2) % 2, 0:T1]
                t = self.rsqrt(r_, ps[:, 0:T1], tp, 1.0 / 256, 1e-6, T1, b)
                for q in (j - 1, j):
                    t2 = g.stt(yss[:, q, 0:T1], yss[:, q, 0:T1], self.col("ssd_norm_w_2", q), r_, ALU.mult,
                               ALU.mult, t)
                    ty[q] = g.split(yp[0][:, q, :], yp[1][:, q, :], yss[:, q, :], t2)
        yt = self.evac8(self.down("w_proj_ssd_2", yp, ty, T1, 8), T1)
        tm = [None] * 8
        for j, b, ps, tp in self.linear("g_ssd", 8, X, xt, T1):
            t = g.act(merged[:, j, :], ps[:, 0:T1], ACT.Sigmoid, tp)
            g.free(b, t)
            tm[j] = g.tt(merged[:, j, :], merged[:, j, :], self.yT[:, j, 0:T1], ALU.mult, t, yt[j])
        g.fence()
        buf = self.carve(2048)
        qo = self.pos[0]
        qT = buf(2048, 8, T1)
        kT = buf(2048, 8, T1)
        V = buf(2048, 2, 1024)
        qio = self.pos[0]
        qi = buf(2048, 8, T1)
        S = buf(2048, 2, 4, T1)
        PT = buf(1024, 4, 2, P)
        sc = buf(512, 2, T1)
        wk = buf(1024, 2, 2, T1)
        sel = buf(512, 2, T1)
        cT = buf(512, 2, T1)
        cR = [self.over(f"cR{i}", self.pos[0] + 512 * i, 2, T1) for i in range(2)]
        buf(1024)
        m8 = s[:, 448:464].rearrange("p (m h) -> p m h", m=2)
        tck = [None] * 2
        for j, b, ps, tp in self.linear("ckv", 2, X, xt, T1):
            tck[j] = g.cp(cT[:, j, :], ps[:, 0:T1], tp)
            g.free(b, tck[j])
        for j in range(2):
            t = g.act(self.sq[:, j, 0:T1], cT[:, j, :], ACT.Square, tck[j])
        b, ps, w = g.bank()
        tp = g.mm(ps[:, 0:T1], [(self.ones, self.sq[:, q, 0:T1]) for q in range(2)], t, *w)
        r_ = self.rstd[:, 0, 0:T1]
        t = self.rsqrt(r_, ps[:, 0:T1], tp, 1.0 / 256, 1e-6, T1, b)
        for q in range(2):
            t2 = g.stt(cT[:, q, :], cT[:, q, :], self.col("kv_norm_w_2", q), r_, ALU.mult, ALU.mult, t)
            tck[q] = g.split(cR[0][:, q, :], cR[1][:, q, :], cT[:, q, :], t2)
        tq = []
        for j, b, ps, tp in self.linear("qidx", 8, X, xt, T1):
            tq.append(g.cp(qi[:, j, :], ps[:, 0:T1], tp, e="act"))
            g.free(b, tq[j])
        def choose():
            for m in range(2):
                nk = P * (m + 1)
                for h in range(16):
                    o = 64 * (h % 2)
                    b, ps, w = g.bank()
                    tp = g.mm(ps[:, 0:nk], [(qi[o:o + 64, h // 2, m * P:(m + 1) * P], ki[o:o + 64, 0:nk])], tq[h // 2],
                              tki, *w)
                    i, v, tf = self.gettmp()
                    t = g.act(v[:, 0:nk], ps[:, 0:nk], ACT.Relu, tp, tf)
                    g.free(b, t)
                    if h == 0:
                        ta = g.ts(sc[:, m, 0:nk], v[:, 0:nk], widx[:, m, h:h + 1], None, ALU.mult, None, t)
                    else:
                        ta = g.stt(sc[:, m, 0:nk], v[:, 0:nk], widx[:, m, h:h + 1], sc[:, m, 0:nk], ALU.mult, ALU.add,
                                   t)
                    self.tmp_free[i] = ta
                    yield
                al = self.c("alibi")[:, m * 256:m * 256 + nk]
                t = g.ts(sel[:, m, 0:nk], al, -1e29, BIG, ALU.is_lt, ALU.mult)
                cur = sc[:, m, 0:nk]
                t = g.tt(cur, cur, sel[:, m, 0:nk], ALU.add, t)
                for r in range(8):
                    nx = wk[:, m, r % 2, 0:nk]
                    t = g.op("dve", lambda o=m8[:, m, :], c=cur: nc.vector.max(o, c), t)
                    t = g.op("dve", lambda o=nx, v=m8[:, m, :], c=cur: nc.vector.match_replace(o, v, c, -3e38), t)
                    cur = nx
                    yield
                t = g.ts(sel[:, m, 0:nk], cur, -2e38, BIG, ALU.is_gt, ALU.mult, t)
                tsel[m] = g.tt(sel[:, m, 0:nk], sel[:, m, 0:nk], al, ALU.add, t)

        tsel = [None, None]
        pick = choose()
        tqq, tkk = [], []
        for j, b, ps, tp in self.linear("q_2", 8, X, xt, T1):
            tqq.append(g.act(qT[:, j, :], ps[:, 0:T1], ACT.Copy, tp, scale=0.125))
            g.free(b, tqq[j])
            for _ in range(4):
                next(pick, None)
        us = [self.rowunit("w_uk", r) for r in range(2)]
        for j in range(8):
            b, ps, w = g.bank()
            c = slice(j * P, (j + 1) * P)
            for r, (i, wk_, t) in enumerate(us):
                tp = g.mm3(ps[:, 0:T1], [x[:, c] for x in wk_], [x[:, r, :] for x in cR], t, *tck, *w,
                           first=r == 0, final=r == 1, inc=r == 1)
            tkk.append(g.cp(kT[:, j, :], ps[:, 0:T1], tp, e="act"))
            g.free(b, tkk[j])
            for _ in range(2):
                next(pick, None)
        for i, _, _ in us:
            g.free_weight(i, tp)
        us = [self.rowunit("w_uv", r) for r in range(2)]
        for m in range(2):
            for h in range(2):
                b, ps, w = g.bank()
                for r, (i, wv_, t) in enumerate(us):
                    tp = g.mm3(ps[:, :], [x[:, r, m * P:(m + 1) * P] for x in cR],
                               [x[:, h * 512:(h + 1) * 512] for x in wv_], t, *w,
                               first=r == 0, final=r == 1, inc=r == 1)
                tvv = g.cp(V[:, m, h * 512:(h + 1) * 512], ps[:, :], tp, e="act")
                g.free(b, tvv)
        for i, _, _ in us:
            g.free_weight(i, tp)
        for _ in pick:
            pass
        oT = (self.over("oTh", qio, 8, T1), self.sqR)
        to = [None] * 8

        def heads(n):
            ptf, sfree = [None, None], None
            SS = S[:, n]
            for m in range(2):
                nk = P * (m + 1)
                for h0 in (8 * n, 8 * n + 4):
                    for r in range(4):
                        h = h0 + r
                        o = 64 * (h % 2)
                        b, ps, w = g.bank()
                        tp = g.mm(ps[:, 0:nk],
                                  [(qT[o:o + 64, h // 2, m * P:(m + 1) * P], kT[o:o + 64, h // 2, 0:nk])],
                                  tqq[h // 2], tkk[h // 2], *w)
                        t = g.stt(SS[:, r, 0:nk], sel[:, m, 0:nk],
                                  float(np.float32(2.0) ** np.float32(-0.5 * (h + 1))), ps[:, 0:nk], ALU.mult, ALU.add,
                                  tp, tsel[m], sfree)
                        g.free(b, t)
                    yield
                    t = yield from self.softmax(SS[:, :, 0:nk], 4, nk, P, [t], n)
                    for r in range(4):
                        h = h0 + r
                        o = 64 * (h % 2)
                        pt = PT[:, 2 * n + h % 2]
                        tx = self.turn(pt, SS[:, r, :], P, [(c * P, P) for c in range(m + 1)], [t], (ptf[h % 2],))
                        sfree = ("pe", g.n["pe"])
                        yield
                        if h % 2 == 0:
                            bo, po, wo = g.bank()
                        ptf[h % 2] = g.mm(po[o:o + 64, 0:P], [(V[:, c, h * 64:h * 64 + 64], pt[:, c, :])
                                                              for c in range(m + 1)], tvv, *tx, *wo)
                        if h % 2:
                            to[h // 2] = g.split(oT[0][:, h // 2, m * P:(m + 1) * P],
                                                 oT[1][:, h // 2, m * P:(m + 1) * P], po[:, 0:P], ptf[h % 2])
                            g.free(bo, to[h // 2])

        self.together(heads(0), heads(1), lead=3)
        yt = self.evac8(self.down("w_proj_att_2", oT, to, T1, 8), T1)
        mp = [self.over("mp" + "hl"[i], qo + 2048 * i, 8, T1) for i in range(2)]
        for j, b, ps, tp in self.linear("g_att", 8, X, xt, T1):
            i, v, tf = self.gettmp()
            t = g.act(v[:, 0:T1], ps[:, 0:T1], ACT.Sigmoid, tp, tf)
            g.free(b, t)
            t = g.tt(v[:, 0:T1], v[:, 0:T1], self.yT[:, j, 0:T1], ALU.mult, t, yt[j])
            t = g.tt(merged[:, j, :], merged[:, j, :], v[:, 0:T1], ALU.add, t)
            self.tmp_free[i] = t
            tm[j] = g.split(mp[0][:, j, :], mp[1][:, j, :], merged[:, j, :], t)
        self.layernorm(self.down("w_out_2", mp, tm, T1, 8), 2, False)

    def mem(self):
        g = self.g
        buf = self.carve(0)
        xt = self.splitx()
        mT = [self.over("mT" + "hl"[i], 2048 * i, 8, T1) for i in range(2)]
        buf(4096)
        qT = buf(2048, 8, T1)
        kT = buf(2048, 8, T1)
        V = buf(2048, 2, 1024)
        S = buf(1024, 4, T1)
        PT = buf(1024, 4, 2, P)
        i, (mm,), t = g.unit((0, SLOT, 0, P, self.d["mem_2"]))
        tm = self.turn_back(mm.rearrange("p (m c) -> p m c", m=2), [t, t], mT)
        g.free_unit(i, ("pe", g.n["pe"]))
        tk, tq = [], []
        for j, b, ps, tp in self.linear("mk", 8, mT, tm, T1):
            tk.append(g.cp(kT[:, j, :], ps[:, 0:T1], tp, e="act"))
            g.free(b, tk[j])
        banks = self.tokmajor("mv", mT, tm)
        for m in range(2):
            for h in range(2):
                b, ps, tp = banks[m][h]
                tv = g.cp(V[:, m, h * 512:(h + 1) * 512], ps[:, :], tp)
                g.free(b, tv)
        for j, b, ps, tp in self.linear("mq", 8, self.hp, xt, T1):
            tq.append(g.act(qT[:, j, :], ps[:, 0:T1], ACT.Copy, tp, scale=1.0 / 16))
            g.free(b, tq[j])
        oT = self.hp
        to = [None] * 8

        def heads(n):
            ptf, sf = [None, None], None
            for m in range(2):
                for h in (2 * n, 2 * n + 1):
                    b, ps, w = g.bank()
                    tp = g.mm(ps[:, 0:T1],
                              [(qT[:, 2 * h + i, m * P:(m + 1) * P], kT[:, 2 * h + i, :]) for i in range(2)],
                              *tk, *tq, *w)
                    t = g.cp(S[:, h, :], ps[:, 0:T1], tp, sf)
                    g.free(b, t)
                yield
                t = yield from self.softmax(S[:, 2 * n:2 * n + 2, :], 2, T1, P, [t], n)
                for h in (2 * n, 2 * n + 1):
                    pt = PT[:, h]
                    tx = self.turn(pt, S[:, h, :], P, [(0, P), (P, P)], [t], (ptf[h % 2],))
                    sf = ("pe", g.n["pe"])
                    yield
                    b, ps, w = g.bank()
                    for i in range(2):
                        tp = g.mm(ps[:, i * P:(i + 1) * P],
                                  [(V[:, c, (2 * h + i) * P:(2 * h + i + 1) * P], pt[:, c, :]) for c in range(2)],
                                  tv, *tx, *w)
                    ptf[h % 2] = tp
                    t2 = g.split(oT[0][:, 2 * h:2 * h + 2, m * P:(m + 1) * P],
                                 oT[1][:, 2 * h:2 * h + 2, m * P:(m + 1) * P],
                                 ps[:, 0:256].rearrange("p (i t) -> p i t", i=2), tp)
                    g.free(b, t2)
                    to[2 * h] = to[2 * h + 1] = t2

        self.together(heads(0), heads(1), lead=2)
        self.layernorm(self.down("w_mo", oT, to, T1, 8), 3, False)

    TILES = ((0, 0, P), (1, P, P), (2, T1, 16))

    def tokmajor3(self, name, src, toks, scr):
        g = self.g
        banks = {(m, h): g.bank() for m in range(2) for h in range(2)}
        b2, p2, w2 = g.bank()
        out = []
        for k in range(8):
            i, w, t = self.rowunit(name, k)
            for m in range(2):
                for h in range(2):
                    b, ps, wt = banks[m, h]
                    tk = g.mm3(ps[:, :], [x[:, k, m * P:(m + 1) * P] for x in src],
                               [x[:, h * 512:(h + 1) * 512] for x in w], t, toks[k], *wt,
                               first=k == 0, final=k == 7, inc=k == 7)
                    if k == 7:
                        out.append((m, h, P, b, ps, tk))
            for n in range(8):
                tk = g.mm3(p2[:, n * 16:(n + 1) * 16], [x[:, n * P:(n + 1) * P] for x in w],
                           [x[:, k, T1:T3] for x in src], *w2, first=k == 0 and n == 0, final=k == 7,
                           inc=n == 7, loose=True)
            g.free_weight(i, tk)
        t = g.cp(scr, p2[:, 0:P], tk)
        g.free(b2, t)
        for h in range(2):
            b, ps, wt = g.bank()
            for n in range(4):
                q = 4 * h + n
                tp = g.tr(ps[0:16, n * P:(n + 1) * P], scr[:, q * 16:q * 16 + 16], self.ident, t, *wt)
            out.append((2, h, 16, b, ps, tp))
        return out

    def gla(self):
        g, nc, T = self.g, self.g.nc, T3
        buf = self.carve(0)
        q, k, gk, eb, en = [buf(4 * T, 4, T) for _ in range(5)]
        v = buf(3072, 3, 1024)
        sr = buf(8 * T, 8, T)
        ke = buf(1536, 3, 512)
        S = buf(1024, 4, 256)
        att = buf(512, 4, P)
        ot = buf(1024, 4, 256)
        lr = buf(T)
        scr = buf(P)
        lo_at = self.pos[0]
        buf(8 * T)
        ht = self.prenorm("norm_gains_3", 2)
        src = self.hp
        il, (wl, wg), tl = g.unit((0, 128, 0, P, self.d["gla_lr"]), (128, 512, 0, 16, self.d["gla_gate"]))
        wl = wl.rearrange("p (k n) -> p k n", k=8)
        b, ps, w = g.bank()
        tp = g.mm(ps[0:16, 0:T], [(wl[:, kk, :], self.sq[:, kk, 0:T]) for kk in range(8)], tl, *ht, *w)
        t = g.cp(lr[0:16, :], ps[0:16, 0:T], tp)
        g.free(b, t)
        for j in range(4):
            b, ps, w = g.bank()
            tp = g.mm(ps[:, 0:T], [(wg[0:16, j * P:(j + 1) * P], lr[0:16, :])], t, *w)
            tg = g.ts(gk[:, j, :], ps[:, 0:T], self.col("gla_b_gate_3", j), None, ALU.add, None, tp)
            g.free(b, tg)
        g.free_unit(il, tp)
        t = g.act(eb, gk, ACT.Abs, tg)
        t = g.act(eb, eb, ACT.Exp, t, scale=-1.0)
        t = g.act(eb, eb, ACT.Ln, t, bias=1.0)
        t = g.stt(gk, gk, 0.0, eb, ALU.min, ALU.subtract, t)
        t = g.ts(gk, gk, 1.0 / 16, None, ALU.mult, None, t)
        for j in range(4):
            tb = g.op("dve", lambda j=j: nc.vector.tensor_tensor_scan(en[:, j, :], self.c("reset"), gk[:, j, :], 0.0,
                                                                      ALU.mult, ALU.add), t)
        tbe = g.act(eb, en, ACT.Exp, tb)
        bl = en[:, :, 0:T1].rearrange("p j (c t) -> p j c t", c=4)
        for j in range(4):
            g.tt(gk[:, j, 0:T1].rearrange("p (c t) -> p c t", c=4), bc(bl[:, j, :, 63], 64), bl[:, j], ALU.subtract, tb)
        t = g.tt(gk[:, :, T1:T], bc(en[:, :, T - 1], 16), en[:, :, T1:T], ALU.subtract)
        tge = g.act(gk, gk, ACT.Exp, t)
        ten = g.act(en, en, ACT.Exp, tge, t, scale=-1.0)
        tq = []
        for j, b, ps, tp in self.linear("gla_qk", 8, src, ht, T):
            if j < 4:
                tq.append(g.stt(q[:, j, :], ps[:, 0:T], float(P ** -0.5), eb[:, j, :], ALU.mult, ALU.mult, tp, tbe))
            else:
                c = j - 4
                g.tt(k[:, c, :], ps[:, 0:T], en[:, c, :], ALU.mult, tp, ten)
                tq.append(g.tt(gk[:, c, :], gk[:, c, :], ps[:, 0:T], ALU.mult, tp, tge))
            g.free(b, tq[j])
        tv = [None] * 3
        for m, h, n, b, ps, tp in self.tokmajor3("gla_v", src, ht, scr):
            tv[m] = g.cp(v[0:n, m, h * 512:(h + 1) * 512], ps[0:n, :], tp, e="act")
            g.free(b, tv[m])
        tr_ = []
        for j, b, ps, tp in self.linear("gla_r", 8, src, ht, T):
            tr_.append(g.act(sr[:, j, :], ps[:, 0:T], ACT.Silu, tp))
            g.free(b, tr_[j])
        tke = []
        for m, c, n in self.TILES:
            b, ps, w = g.bank()
            for j in range(4):
                tp = g.tr(ps[0:n, j * P:(j + 1) * P], gk[:, j, c:c + n], self.ident, *tq, *w)
            tke.append(g.cp(ke[0:n, m, :], ps[0:n, :], tp))
            g.free(b, tke[m])
        mi = self.c("m64")[:, 128:256].bitcast(mybir.dt.uint32)
        t0 = g.op("dve", lambda: nc.vector.memset(att, 0.0))
        t0 = g.op("dve", lambda: nc.vector.memset(S, 0.0))
        mix = (self.sqR, self.over("glal", lo_at, 8, T))
        g.wait("act", [("pe", g.n["pe"])])
        tS = [t0] * 4
        of = [None] * 4
        s = self.small
        toks = [None] * 8
        for m, c, n in (self.TILES[2], self.TILES[0], self.TILES[1]):
            for h in range(4):
                hv = slice(h * 256, (h + 1) * 256)
                b, ps, w = g.bank()
                tp = g.mm(ps[0:n, 0:n], [(k[:, h, c:c + n], q[:, h, c:c + n])], *tq, *w)
                ta = g.op("dve", lambda o=att[0:n, h, 0:n], mk=mi[0:n, 0:n], dt=ps[0:n, 0:n]:
                          nc.vector.copy_predicated(o, mk, dt), tp, t0, of[h])
                g.free(b, ta)
                bo, po, wo = g.bank()
                to = g.mm(po[0:n, 0:256], [(att[0:n, h, 0:n], v[0:n, m, hv])], ta, tv[m], *wo, final=m == 2)
                for cc in range(1 if m == 2 else 2):
                    o = 64 * cc
                    w_ = min(n, 64)
                    if m < 2:
                        to = g.mm(po[o:o + 64, 0:256], [(q[:, h, c + o:c + o + 64], S[:, h, :])], tS[h],
                                  first=False)
                    if m == 1 and cc == 1:
                        break
                    b, ps, w = g.bank()
                    tp = g.mm(ps[:, 0:256], [(ke[o:o + w_, m, h * P:(h + 1) * P], v[o:o + w_, m, hv])], tke[m], *w)
                    tS[h] = g.stt(S[:, h, :], S[:, h, :], eb[:, h, c + o + w_ - 1:c + o + w_], ps[:, 0:256], ALU.mult,
                                  ALU.add, tp, to)
                    g.free(b, tS[h])
                ss = s[0:n, 16 * m + h:16 * m + h + 1]
                t = g.act(ot[0:n, h, :], po[0:n, 0:256], ACT.Square, to, of[h], accum_out=ss)
                t = g.ts(ss, ss, 1.0 / 256, 1e-6, ALU.mult, ALU.add, t)
                t = g.recip(ss, ss, t)
                t = g.act(ss, ss, ACT.Sqrt, t)
                t = g.ts(ot[0:n, h, :], po[0:n, 0:256], ss, None, ALU.mult, None, t)
                g.free(bo, t)
                b, ps, w = g.bank()
                for i in range(2):
                    tp = g.tr(ps[:, i * P:i * P + n], ot[0:n, h, i * P:(i + 1) * P], self.ident[0:n, 0:n], t, *w)
                of[h] = tp
                for i in range(2):
                    x, v_, tf = self.gettmp()
                    t = g.stt(v_[:, 0:n], ps[:, i * P:i * P + n], self.col("gla_norm_3", i),
                              sr[:, 2 * h + i, c:c + n], ALU.mult, ALU.mult, tp, tr_[2 * h + i], tf)
                    toks[2 * h + i] = g.split(mix[0][:, 2 * h + i, c:c + n], mix[1][:, 2 * h + i, c:c + n],
                                              v_[:, 0:n], t)
                    self.tmp_free[x] = toks[2 * h + i]
                g.free(b, t)
        self.postnorm(self.down("gla_out", mix, toks, T, 8), "norm_gains_3", 3, False)

    def rope(self, x, H, m, n, tok):
        g = self.g
        x3 = x.rearrange("p (h j) -> p h j", h=H)
        at = CSTS["rope"][0] + 16 * m
        c = bc_mid(self.cst[0:n, at:at + 8], H)
        s = bc_mid(self.cst[0:n, at + 8:at + 16], H)
        r = self.rstd.rearrange("p k t -> p (k t)")
        a, b2, d, e = [r[0:n, i * 128:i * 128 + 8 * H].rearrange("p (h j) -> p h j", h=H) for i in range(4)]
        x1, x2 = x3[:, :, 0:8], x3[:, :, 8:16]
        g.tt(a, x1, c, ALU.mult, tok)
        g.tt(b2, x2, s, ALU.mult)
        g.tt(d, x2, c, ALU.mult)
        g.tt(e, x1, s, ALU.mult)
        g.tt(x1, a, b2, ALU.subtract)
        return g.tt(x2, d, e, ALU.add)

    def shared(self):
        g, T = self.g, T3
        buf = self.carve(self.NA - 1856)
        kD, V = self.kD3, self.V3 = buf(4 * T, 4, T), buf(768, 3, 256)
        kt = self.A[:, 0:768].rearrange("p (m c) -> p m c", m=3)
        ht = self.prenorm("kv_norm_3")
        fm = self.A[:, 768:768 + 4 * T].rearrange("p (j t) -> p j t", j=4)
        tf = []
        for j, b, ps, tp in self.linear("w_kv", 4, self.hp, ht, T):
            tf.append(g.cp(fm[:, j, :], ps[:, 0:T], tp, e="act"))
            g.free(b, tf[j])
        for u in range(2):
            for m, c, n in self.TILES:
                b, ps, wt = g.bank()
                for j in range(2):
                    tp = g.tr(ps[0:n, j * P:(j + 1) * P], fm[:, 2 * u + j, c:c + n], self.ident, tf[2 * u + j], *wt)
                tk = g.cp((kt, V)[u][0:n, m, :], ps[0:n, 0:256], tp)
                g.free(b, tk)
                if u == 0:
                    tk = self.rope(kt[0:n, m, :], 4, m, n, tk)
                    b, ps, wt = g.bank()
                    for h in range(4):
                        tp2 = g.tr(ps[0:64, h * P:h * P + n], kt[0:n, m, h * 64:h * 64 + 64], self.ident[0:n, 0:n],
                                   tk, *wt)
                    p4 = ps[0:64, :].rearrange("p (h t) -> p h t", h=4)[:, :, 0:n]
                    g.cp(kD[0:64, :, c:c + n], p4, tp2)
                    tk = g.cp(kD[64:128, :, c:c + n], p4, tp2)
                    g.free(b, tk)
        self.tkv = tk
        g.fence()

    def swa(self):
        g, T = self.g, T3
        buf = self.carve(0, self.NA - 1856)
        qt = buf(3072, 3, 1024)
        qT = buf(8 * T, 8, T)
        S = buf(8 * T, 2, 4, T)
        PT = buf(1536, 4, 3, P)
        scr = buf(P)
        lo_at = self.pos[0]
        buf(8 * T)
        kD, V = self.kD3, self.V3
        ht = self.prenorm("norm_gains_3", 8)
        tm = [None] * 3
        for m, h, n, b, ps, tp in self.tokmajor3("swa_q", self.hp, ht, scr):
            tm[m] = g.act(qt[0:n, m, h * 512:(h + 1) * 512], ps[0:n, :], ACT.Copy, tp, scale=0.125)
            g.free(b, tm[m])
        tq = []
        for m, c, n in self.TILES:
            t = self.rope(qt[0:n, m, :], 16, m, n, tm[m])
            for hf in range(2):
                b, ps, w = g.bank()
                for i in range(4):
                    tp = g.tr(ps[:, i * P:i * P + n], qt[0:n, m, (4 * hf + i) * P:(4 * hf + i + 1) * P],
                              self.ident[0:n, 0:n], t, *w)
                tx = g.cp(qT[:, 4 * hf:4 * hf + 4, c:c + n],
                          ps[:, :].rearrange("p (h t) -> p h t", h=4)[:, :, 0:n], tp)
                g.free(b, tx)
            tq.append(tx)
        mix = (self.sqR, self.over("swal", lo_at, 8, T))
        g.wait("act", [("pe", g.n["pe"])])
        to = [None] * 8
        sinks = self.rows[:, ROWS["swa_sinks_3"][0]:ROWS["swa_sinks_3"][0] + 16]

        def heads(u):
            ptf, sfree = [None, None], None
            for m, c, n in self.TILES:
                keys = ((0, 2), (0, 1, 2), (2,))[m]
                SS = S[0:n, u]
                for kv in (2 * u, 2 * u + 1):
                    for r in range(4):
                        h = 4 * kv + r
                        o = 64 * (h % 2)
                        b, ps, w = g.bank()
                        tp = g.mm(ps[0:n, 0:T], [(qT[o:o + 64, h // 2, c:c + n], kD[o:o + 64, kv, :])], tq[m], self.tkv,
                                  *w)
                        at = CSTS["swa"][0] + m * T
                        t = g.tt(SS[:, r, :], ps[0:n, 0:T], self.cst[0:n, at:at + T], ALU.add, tp, sfree)
                        g.free(b, t)
                    yield
                    t = yield from self.softmax(SS, 4, T, n, [t], u, sink=sinks[0:n, 4 * kv:4 * kv + 4])
                    for r in range(4):
                        h = 4 * kv + r
                        o = 64 * (h % 2)
                        pt = PT[:, 2 * u + h % 2]
                        tx = self.turn(pt, SS[:, r, :], n, [(kk * P, (P, P, 16)[kk]) for kk in keys], [t], (ptf[h % 2],))
                        sfree = ("pe", g.n["pe"])
                        yield
                        if h % 2 == 0:
                            bo, po, wo = g.bank()
                        pairs = [(V[0:(P, P, 16)[kk], kk, kv * 64:kv * 64 + 64], pt[0:(P, P, 16)[kk], i, 0:n])
                                 for i, kk in enumerate(keys)]
                        ptf[h % 2] = g.mm(po[o:o + 64, 0:n], pairs, *tx, *wo)
                        if h % 2:
                            to[h // 2] = g.split(mix[0][:, h // 2, c:c + n], mix[1][:, h // 2, c:c + n], po[:, 0:n],
                                                 ptf[h % 2])
                            g.free(bo, to[h // 2])

        self.together(heads(0), heads(1), lead=3)
        self.postnorm(self.down("swa_out", mix, to, T, 8), "norm_gains_3", 9, False)


def colunits(w):
    k, n = w.shape
    return w.reshape(k // P, P, n // P, P).transpose(2, 1, 0, 3).reshape(n // P, P, k)


def rowunits(w):
    k, n = w.shape
    return w.reshape(k // P, P, n)


def layout(v):
    d = {"x": v["x"][0].reshape(2, P, D).transpose(1, 0, 2).reshape(P, SLOT), "cst": constants(), "meta_tokens_3": v["meta_tokens_3"]}
    cols = np.zeros((P, NCOL + P), np.float32)
    cols[:, NCOL:] = np.concatenate([v["l0_cmp_w2_k"], v["l0_cmp_w2_v"]], 1)
    for name, (at, n) in COLS.items():
        a = np.repeat(v["d_skip_2"].reshape(-1), 64) if name == "d_skip_2c" else v[name]
        cols[:, at:at + n] = np.asarray(a).reshape(n, P).T
    d["cols"] = cols
    d["rows"] = np.concatenate([np.asarray(v[n]).reshape(1, 16) for n in ROWS], 1)
    for f in FFNS:
        d[f + "_w_gate"] = colunits(v[f + "_w_gate"])
        d[f + "_w_up"] = colunits(v[f + "_w_up"])
        d[f + "_w_down"] = rowunits(v[f + "_w_down"])
    for f in ("ffn1", "ffn2"):
        w = v[f + "_w_in_2"][0]
        d[f + "_w_gate_2"] = colunits(w[:, :FF])
        d[f + "_w_up_2"] = colunits(w[:, FF:])
        d[f + "_w_out_2"] = rowunits(v[f + "_w_out_2"][0])
    for a in range(2):
        for b in range(2):
            w = v["w_ffn_in_3"][a, b]
            d[f"g3_{a}{b}"] = colunits(w[:, :FF])
            d[f"u3_{a}{b}"] = colunits(w[:, FF:])
            d[f"d3_{a}{b}"] = rowunits(v["w_ffn_out_3"][a, b])
    w = v["l0_w_in"]
    c = np.cumsum([0, 512, 24, 128, 128, 128, 128, 128, 128, 512, 512, 512])
    part = lambda i: w[:, c[i]:c[i + 1]]
    d["nsa_in"] = colunits(np.concatenate([part(i) for i in (0, 2, 3, 4, 6, 8, 9, 10)], 1))
    d["nsa_v"] = colunits(np.concatenate([part(5), part(7)], 1))
    d["nsa_g"] = part(1).reshape(8, P, 24).transpose(1, 0, 2).reshape(P, 192)
    for s in "kv":
        d["cmp_w1_" + s] = v["l0_cmp_w1_" + s].reshape(16, P, P).transpose(1, 0, 2).reshape(P, SLOT)
    d["nsa_out"] = rowunits(v["l0_w_out"])
    d["lora1"] = np.concatenate([v["l1_w_dec1"], v["l1_w_a1"], v["l1_w_g1"]], 1).reshape(8, P, 256).transpose(
        1, 0, 2).reshape(P, SLOT)
    d["lora2"] = np.concatenate([np.concatenate([v["l1_w_dec2"], v["l1_w_a2"]], 1),
                                 np.concatenate([v["l1_w0"], v["l1_a0"]])[None]], 0)
    d["l1_w_g2"] = v["l1_w_g2"]
    for n in ("l1_w_r", "l1_w_k", "l1_w_v", "l1_w_o"):
        d[n] = rowunits(v[n])
    for n in ("l1_k_k", "l1_k_a", "l1_r_k", "l1_lnx_g", "l1_lnx_b"):
        d[n] = v[n].reshape(1, D)
    w = v["w_in_2"][0]
    c = np.cumsum([0, 1024, 1024, 1024, 2048, 16, 1024, 256, 1024, 64, 16])
    part = lambda i: w[:, c[i]:c[i + 1]]
    for i, n in ((0, "g_ssd"), (1, "g_att"), (2, "z_2"), (3, "xbc"), (5, "q_2"), (6, "ckv"), (7, "qidx")):
        d[n] = colunits(part(i))
    d["tokw"] = np.concatenate([part(4), part(9)], 1).reshape(8, P, 32).transpose(1, 0, 2).reshape(P, 256)
    d["kidx"] = part(8).reshape(8, P, 64).transpose(1, 0, 2).reshape(P, 512)
    d["w_uk"] = v["w_uk_2"][0].transpose(2, 0, 1).reshape(2, P, D)
    d["w_uv"] = v["w_uv_2"][0].transpose(1, 0, 2).reshape(2, P, D)
    for n in ("w_proj_ssd_2", "w_proj_att_2", "w_out_2"):
        d[n] = rowunits(v[n][0])
    d["mem_2"] = v["mem_2"][0].reshape(2, P, D).transpose(1, 0, 2).reshape(P, SLOT)
    d["mq"] = colunits(v["w_mq_2"][0])
    d["mk"] = colunits(v["w_mkv_2"][0][:, :D])
    d["mv"] = rowunits(v["w_mkv_2"][0][:, D:])
    d["w_mo"] = rowunits(v["w_mo_2"][0])
    w = v["gla_w_in_3"][0]
    d["gla_qk"] = colunits(w[:, :1024])
    d["gla_v"] = rowunits(w[:, 1024:2048])
    d["gla_r"] = colunits(w[:, 2048:3072])
    d["gla_lr"] = w[:, 3072:].reshape(8, P, 16).transpose(1, 0, 2).reshape(P, 128)
    d["gla_gate"] = v["gla_w_gate_3"][0]
    d["gla_out"] = rowunits(v["gla_w_out_3"][0])
    d["w_kv"] = colunits(v["w_kv_3"])
    d["swa_q"] = rowunits(v["swa_w_q_3"][0])
    d["swa_out"] = rowunits(v["swa_w_out_3"][0])
    return {n: np.ascontiguousarray(a) for n, a in d.items()}


def program(nc, arrays, stages):
    d = {n: nc.dram_tensor("in_" + n, a.shape, F32, kind="ExternalInput").ap() for n, a in arrays.items()}
    out = nc.dram_tensor("out_0", (T1, D), F32, kind="ExternalOutput").ap()
    with ExitStack() as ctx:
        Model(nc, ctx, d, out, stages)


def kernel(**inputs):
    import concourse.bacc as _bacc
    from concourse.bass_utils import run_bass_kernel_spmd as _run

    arrays = layout({n: np.asarray(a) for n, a in inputs.items()})
    nc = _bacc.Bacc("TRN2", target_bir_lowering=False, num_devices=1)
    program(nc, arrays, range(18))
    r = _run(nc, [{"in_" + n: a for n, a in arrays.items()}], core_ids=[0])
    return r.results[0]["out_0"].reshape(1, T1, D)
```

```python
from contextlib import ExitStack

import numpy as np

import concourse.bass as bass
from concourse import mybir

P = 128
D = 1024
FF = 2816
NF = FF // P
T1 = 256
T3 = 272
NPAR = 2
SLOT = 2048
NRAW = 8
NHI = 5
UNIT = 1024
BIG = -1.0e30
ALPHA = 2.0 ** 0.25

ALU = mybir.AluOpType
ACT = mybir.ActivationFunctionType
F32 = mybir.dt.float32
F32R = mybir.dt.float32r
AX_X = mybir.AxisListType.X

FFNS = ("l0_ffn1", "l0_ffn2", "l1_ffn1", "l1_ffn2")


def table(sizes):
    at, out = 0, {}
    for name, n in sizes:
        out[name] = (at, n)
        at += n
    return out, at


COLS, NCOL = table(
    [(f + s, 8) for f in FFNS for s in ("_pre_g", "_post_g")]
    + [(f"l{i}_mix_{s}_g", 8) for i in range(2) for s in ("pre", "post")]
    + [("l0_conv_w", 12), ("l0_conv_b", 4), ("l0_cmp_pe_k", 16), ("l0_cmp_pe_v", 16), ("l1_mu", 48)]
    + [(f"ln{i}_{s}_2", 8) for i in range(1, 5) for s in "gb"]
    + [("conv_w_2", 64), ("conv_b_2", 16), ("d_skip_2c", 8), ("ssd_norm_w_2", 8), ("kv_norm_w_2", 2)]
    + [("norm_gains_3", 96), ("kv_norm_3", 8), ("gla_b_gate_3", 4), ("gla_norm_3", 2)])

ROWS, NROW = table([("dt_bias_2", 16), ("a_log_2", 16), ("d_skip_2", 16), ("swa_sinks_3", 16)])

CSTS, NCST = table([
    ("ident", 128), ("ones", 128), ("half", 1), ("alibi", 512), ("alibi_cmp", 32), ("m64", 256), ("suf64", 128),
    ("chunk", 2), ("level", 768), ("tri128", 128), ("suf128", 128), ("swa", 816), ("rope", 48),
    ("reset", 272)])


def constants():
    c = np.zeros((P, NCST), np.float32)

    def put(name, a):
        at, n = CSTS[name]
        a = np.asarray(a, np.float32)
        c[:a.shape[0], at:at + n] = a.reshape(a.shape[0], -1)

    i = np.arange(P)[:, None]
    j = np.arange(P)[None, :]
    put("ident", np.eye(P))
    put("ones", np.ones((P, P)))
    s = np.arange(T1)[None, :]
    put("alibi", np.concatenate([np.where(s <= i + P * m, s - (i + P * m), BIG) for m in range(2)], 1))
    n = np.arange(16)[None, :]
    e = 16 * n + 31
    put("alibi_cmp", np.concatenate([np.where((e <= i + P * m) & (n < 15), e - (i + P * m), BIG)
                                     for m in range(2)], 1))
    same = i // 64 == j // 64
    put("m64", np.concatenate([same & (i < j), same & (i <= j)], 1))
    put("suf64", same & (i > j))
    put("chunk", i // 64 == np.arange(2)[None, :])
    put("level", np.concatenate([(i // (2 * b) == j // (2 * b)) & (i % (2 * b) < b) & (j % (2 * b) >= b)
                                 for b in (1, 2, 4, 8, 16, 32)], 1))
    put("tri128", i <= j)
    put("suf128", i > j)
    put("half", np.full((P, 1), -0.5))
    keep = [np.concatenate([j <= i, np.zeros((P, P), bool), np.ones((P, 16), bool)], 1),
            np.concatenate([j > i, j <= i, np.ones((P, 16), bool)], 1),
            np.concatenate([np.zeros((P, T1), bool), np.arange(16)[None, :] <= i], 1)]
    put("swa", np.concatenate([np.where(k, 0.0, BIG) for k in keep], 1))
    freq = np.float32(500000.0) ** (-np.arange(0, 16, 2, dtype=np.float32) / np.float32(16))
    rope = []
    for base in (16, 16 + P, 0):
        ang = (np.arange(P, dtype=np.float32)[:, None] + np.float32(base)) * freq[None, :].astype(np.float32)
        rope += [np.cos(ang), np.sin(ang)]
    put("rope", np.concatenate(rope, 1))
    put("reset", np.broadcast_to((np.arange(T3) % 64 != 0)[None, :], (P, T3)))
    return c


class Prog:

    def __init__(self, nc, ctx):
        self.nc = nc
        self.ctx = ctx
        self.q = {e: [] for e in ("pe", "act", "dve", "pool", "sp")}
        self.h = {"pe": nc.tensor, "act": nc.scalar, "dve": nc.vector, "pool": nc.gpsimd, "sp": nc.sync}
        self.sem = {e: ctx.enter_context(nc.semaphore("s_" + e)) for e in ("pe", "act", "dve", "pool")}
        self.n = {e: 0 for e in self.sem}
        self.seen = {e: {} for e in self.q}
        self.at = (nc.sbuf_base + 63) // 64 * 64
        self.raw, self.raw_at = self.place("raw", NRAW * UNIT)
        self.lo = self.alias("lo", self.raw_at, NRAW * UNIT)
        self.hi, _ = self.place("hi", NHI * UNIT, F32R)
        self.par, _ = self.place("par", NPAR * SLOT)
        for i in range(NPAR):
            self.new_sem(f"par{i}")
        for i in range(NRAW):
            self.new_sem(f"raw{i}")
        self.new_sem("cvh")
        self.new_sem("cvl")
        self.new_sem("cvp")
        self.par_free = [None] * NPAR
        self.npar = 0
        self.weights = []
        self.w_free = []
        self.ps = [ctx.enter_context(nc.psum_tensor(f"ps{i}", [P, 512], F32)) for i in range(8)]
        self.ps_free = [[] for _ in range(8)]
        self.nps = 0
        for w in range(NHI):
            self.split_later(w)

    def new_sem(self, name):
        self.sem[name] = self.ctx.enter_context(self.nc.semaphore("s_" + name))
        self.n[name] = 0

    def place(self, name, n, dt=F32):
        at = self.at
        self.at += (4 * n + 63) // 64 * 64
        return self.nc.alloc_sbuf_tensor_at(name, [P, n], dt, offset=at), at

    def alias(self, name, at, n, dt=F32R):
        return self.nc.alloc_sbuf_tensor_at(name, [P, n], dt, offset=at)

    def sb(self, name, n):
        return self.place(name, n)[0]

    def wait(self, e, toks):
        for t in toks:
            if t is None:
                continue
            s, v = t
            if self.seen[e].get(s, 0) >= v:
                continue
            self.seen[e][s] = v
            self.q[e].append(lambda h=self.h[e], s=self.sem[s], v=v: h.wait_ge(s, v))

    def op(self, e, fn, *toks):
        if e != "pe" and self.n[e]:
            toks = toks + ((e, self.n[e]),)
        self.wait(e, toks)
        self.n[e] += 1
        self.q[e].append(lambda s=self.sem[e]: fn().then_inc(s, 1))
        return e, self.n[e]

    def last(self):
        return [(e, self.n[e]) for e in ("pe", "act", "dve", "pool") if self.n[e]]

    def fence(self):
        toks = self.last()
        for e in ("pe", "act", "dve", "pool"):
            self.wait(e, [t for t in toks if t[0] != e])
        for b in range(8):
            if self.ps_free[b] is not None:
                self.ps_free[b] = []

    def dma_group(self, name):
        self.new_sem(name)

    def dma(self, e, group, out, in_, *toks):
        self.wait(e, toks)
        self.n[group] += 16
        self.q[e].append(lambda h=self.h[e], s=self.sem[group]: h.dma_start(out, in_).then_inc(s, 16))
        return group, self.n[group]

    def unit(self, *loads):
        i = self.npar % NPAR
        self.npar += 1
        assert self.npar <= NPAR or self.par_free[i], "slot reused before it was freed"
        self.wait("pool", [self.par_free[i]])
        self.par_free[i] = None
        at = i * SLOT
        out = []
        for off, w, p0, p1, src in loads:
            dst = self.par[p0:p1, at + off:at + off + w]
            tok = self.dma("pool", f"par{i}", dst, src)
            out.append(dst)
        return i, out, tok

    def free_unit(self, i, tok):
        self.par_free[i] = tok

    def weight(self, src):
        w = len(self.weights)
        if w >= NRAW:
            self.wait("sp", [self.w_free[w - NRAW]])
        tok = self.dma("sp", f"raw{w % NRAW}", self.raw[:, w % NRAW * UNIT:(w % NRAW + 1) * UNIT], src)
        self.weights.append(tok)
        self.w_free.append(None)
        hi = self.hi[:, w % NHI * UNIT:(w % NHI + 1) * UNIT]
        lo = self.lo[:, w % NRAW * UNIT:(w % NRAW + 1) * UNIT]
        return w, hi, lo, self.parted(w)

    def parted(self, w):
        return ("cvp", w // 3 + 1) if w % 3 == 2 else ("cvl", w - w // 3 + 1 - (w % 3 == 2))

    def free_weight(self, w, tok):
        self.w_free[w] = tok
        self.split_later(w + NHI)

    def split_later(self, w):
        nc = self.nc
        raw = self.raw[:, w % NRAW * UNIT:(w % NRAW + 1) * UNIT]
        lo = self.lo[:, w % NRAW * UNIT:(w % NRAW + 1) * UNIT]
        hi = self.hi[:, w % NHI * UNIT:(w % NHI + 1) * UNIT]

        def first():
            if w >= len(self.weights):
                return
            s, v = self.weights[w]
            nc.scalar.wait_ge(self.sem[s], v)
            if w >= NHI:
                s, v = self.w_free[w - NHI]
                nc.scalar.wait_ge(self.sem[s], v)
            nc.scalar.activation(hi, raw, ACT.Copy).then_inc(self.sem["cvh"], 1)

        def second():
            if w >= len(self.weights):
                return
            h.wait_ge(self.sem["cvh"], w + 1)
            h.tensor_tensor(lo, raw, hi.bitcast(F32), ALU.subtract).then_inc(self.sem[self.parted(w)[0]], 1)

        e = "pool" if w % 3 == 2 else "dve"
        h = self.h[e]
        self.q["act"].append(first)
        self.q[e].append(second)

    def bank(self):
        while self.ps_free[self.nps % 8] is None:
            assert any(w is not None for w in self.ps_free), "every bank is held"
            self.nps += 1
        b = self.nps % 8
        self.nps += 1
        w, self.ps_free[b] = self.ps_free[b], None
        return b, self.ps[b], w

    def free(self, b, *toks):
        self.ps_free[b] = list(toks)

    def mm(self, out, pairs, *toks, first=True, final=True, inc=True, loose=False):
        self.wait("pe", toks)
        n = len(pairs)
        for i, (a, b) in enumerate(pairs):
            def f(a=a, b=b, st=first and i == 0, sp=final and i == n - 1):
                return self.nc.tensor.matmul(out, a, b, start=st, stop=sp, skip_group_check=loose)
            if i == n - 1 and inc:
                self.n["pe"] += 1
                self.q["pe"].append(lambda f=f: f().then_inc(self.sem["pe"], 1))
            else:
                self.q["pe"].append(f)
        return ("pe", self.n["pe"]) if inc else None

    def mm3(self, out, a, b, *toks, **kw):
        return self.mm(out, [(a[0], b[0]), (a[0], b[1]), (a[1], b[0])], *toks, **kw)

    def split(self, hi, lo, src, *toks):
        t = self.act(hi, src, ACT.Copy, *toks)
        return self.op("dve", lambda: self.nc.vector.tensor_tensor(lo, src, hi.bitcast(F32), ALU.subtract), t, *toks)

    def tr(self, out, in_, ident, *toks, inc=True):
        self.wait("pe", toks)
        f = lambda: self.nc.tensor.transpose(out, in_, ident)
        if inc:
            self.n["pe"] += 1
            self.q["pe"].append(lambda: f().then_inc(self.sem["pe"], 1))
            return "pe", self.n["pe"]
        self.q["pe"].append(f)

    def act(self, out, in_, func, *toks, **kw):
        return self.op("act", lambda: self.nc.scalar.activation(out, in_, func, **kw), *toks)

    def tt(self, out, a, b, op, *toks, e="dve"):
        return self.op(e, lambda: self.h[e].tensor_tensor(out, a, b, op), *toks)

    def ts(self, out, a, s1, s2, op0, op1, *toks, e="dve"):
        if s2 is None:
            return self.op(e, lambda: self.h[e].tensor_scalar(out, a, s1, None, op0), *toks)
        return self.op(e, lambda: self.h[e].tensor_scalar(out, a, s1, s2, op0, op1), *toks)

    def stt(self, out, a, s, b, op0, op1, *toks, **kw):
        return self.op("dve", lambda: self.nc.vector.scalar_tensor_tensor(out, a, s, b, op0, op1, **kw), *toks)

    def cp(self, out, in_, *toks, e="dve"):
        if e == "act":
            return self.act(out, in_, ACT.Copy, *toks)
        return self.op(e, lambda: self.h[e].tensor_copy(out, in_), *toks)

    def red(self, out, in_, op, *toks):
        return self.op("dve", lambda: self.nc.vector.tensor_reduce(out, in_, AX_X, op), *toks)

    def recip(self, out, in_, *toks):
        return self.op("dve", lambda: self.nc.vector.reciprocal(out, in_), *toks)

    def run(self):
        block = self.ctx.enter_context(self.nc.Block())

        def play(name):
            def body(_):
                for f in self.q[name]:
                    f()
            return body

        block.sync(play("sp"))
        block.scalar(play("act"))
        block.vector(play("dve"))
        block.gpsimd(play("pool"))
        block.tensor(play("pe"))


def bc(ap, *shape):
    full = list(ap.shape) + list(shape)
    for _ in shape:
        ap = ap.unsqueeze(len(ap.shape))
    return ap.broadcast_to(full)


def bc_mid(ap, n):
    return ap.unsqueeze(1).broadcast_to([ap.shape[0], n] + list(ap.shape[1:]))


class Model:
    def __init__(self, nc, ctx, d, out, stages):
        self.d = d
        g = self.g = Prog(nc, ctx)
        self.stages = stages
        self.cst = g.sb("cst", NCST)
        self.cols = g.sb("cols", NCOL + P)
        self.rows = g.sb("rows", NROW)
        self.xT = g.sb("xT", 8 * T3)[:, :].rearrange("p (k t) -> p k t", k=8)
        _, at = g.place("hT_hi", 8 * T3, F32R)
        self.H = self.view("hh", at, 8)
        self.Hf = self.view("hf32", at, 8, F32)
        _, at = g.place("hT_lo", 8 * T3, F32R)
        self.L = self.view("hl", at, 8)
        self.Lf = self.view("lf32", at, 8, F32)
        self.hp = (self.H, self.L)
        self.yT = g.sb("yT", 8 * T3)[:, :].rearrange("p (k t) -> p k t", k=8)
        self.sq_, at = g.place("sq", 8 * T3)
        self.sqR = self.view("sqr", at, 8)
        self.sq = self.sq_[:, :].rearrange("p (k t) -> p k t", k=8)
        self.rstd = g.sb("rstd", 3 * T3)[:, :].rearrange("p (k t) -> p k t", k=3)
        self.tmp = g.sb("tmp", 4 * T3)[:, :].rearrange("p (k t) -> p k t", k=4)
        self.tmp_free = [None] * 4
        self.ntmp = 0
        self.small = g.sb("small", 512)
        self.NA = (nc.sbuf_usable_end - g.at) // 4 // 16 * 16
        self.A, self.Aat = g.place("arena", self.NA)
        self.hf = (self.over("hfh", 0, NF, T3), self.over("hfl", NF * T3, NF, T3))
        self.ident = self.c("ident")
        self.ones = self.c("ones")
        g.dma_group("cst")
        t = g.dma("sp", "cst", self.cst[:, 0:257], d["cst"][:, 0:257])
        for e in ("pe", "act", "dve", "pool"):
            g.wait(e, [t])
        self.T = T1
        self.xtok = [None] * 8
        self.todo = [None] * 8
        self.spent = []
        self.load_x(d["x"], 0)
        g.dma_group("cols")
        t = g.dma("sp", "cols", self.cols[:, :], d["cols"])
        for e in ("pe", "act", "dve", "pool"):
            g.wait(e, [t])
        g.dma_group("cst2")
        self.cst2 = None
        plan = [
            lambda: self.ffn1("l0_ffn1"), self.nsa, lambda: self.ffn1("l0_ffn2"),
            lambda: self.ffn1("l1_ffn1"), self.rwkv, lambda: self.ffn1("l1_ffn2"),
            lambda: self.ffn2("ffn1", 1), self.hybrid, self.mem, lambda: self.ffn2("ffn2", 4),
            self.enter3, lambda: self.ffn3(0, 0), self.gla, lambda: self.ffn3(0, 1), self.shared, lambda: self.ffn3(1, 0),
            self.swa, lambda: self.ffn3(1, 1)]
        for i in stages:
            if plan[i] in (self.nsa, self.rwkv, self.hybrid, self.mem, self.gla, self.shared, self.swa):
                self.settle()
                g.fence()
                self.tables()
                for e in ("pe", "act", "dve", "pool"):
                    g.wait(e, [self.cst2])
            plan[i]()
        self.store(out)
        g.run()

    def view(self, name, at, k, dt=F32R, T=T3):
        return self.g.alias(name, at, k * T, dt)[:, :].rearrange("p (k t) -> p k t", k=k)

    def over(self, name, start, k, T):
        return self.view(name, self.Aat + 4 * start, k, F32R, T)

    def c(self, name, j=None, w=128):
        at, n = CSTS[name]
        if j is None:
            return self.cst[:, at:at + n]
        return self.cst[:, at + j * w:at + (j + 1) * w]

    def col(self, name, j):
        at = COLS[name][0] + j
        return self.cols[:, at:at + 1]

    def load_x(self, x, at):
        g = self.g
        if at == 0:
            g.dma_group("x")
            i, stage = 0, g.par[:, 0:SLOT]
            t = g.dma("sp", "x", stage, x)
            tiles = [(0, P, 0), (1, P, P)]
        else:
            i, (stage,), t = g.unit((0, D, 0, T3 - at, x))
            tiles = [(0, T3 - at, at)]
        stage = stage.rearrange("p (m c) -> p m c", c=D)
        for k in range(8):
            b, ps, w = g.bank()
            for m, p, c in tiles:
                tk = g.tr(ps[:, c - at:c - at + p], stage[0:p, m, k * P:(k + 1) * P], self.ident[0:p, 0:p], t, *w)
            wide = sum(p for _, p, _ in tiles)
            tk = g.cp(self.xT[:, k, at:at + wide], ps[:, 0:wide], tk)
            g.free(b, tk)
            self.xtok[k] = tk
        g.free_unit(i, ("pe", g.n["pe"]))
        g.fence()

    def store(self, out):
        g = self.g
        self.settle()
        g.fence()
        g.dma_group("out")
        stage = self.A[:, 0:2048].rearrange("p (m c) -> p m c", m=2)
        for m in range(2):
            for h in range(2):
                b, ps, w = g.bank()
                for k in range(4):
                    tk = g.tr(ps[:, k * P:(k + 1) * P], self.xT[:, 4 * h + k, m * P:(m + 1) * P], self.ident, *w)
                tk = g.cp(stage[:, m, h * 512:(h + 1) * 512], ps[:, :], tk, e=("dve", "act")[h])
                g.free(b, tk)
                t = g.dma("sp", "out", out[m * P:(m + 1) * P, h * 512:(h + 1) * 512],
                          stage[:, m, h * 512:(h + 1) * 512], tk)
        g.wait("sp", [t])

    def tiles(self):
        return ((0, 0, P), (1, P, P)) + (((2, T1, T3 - T1),) if self.T == T3 else ())

    def tables(self, *toks):
        if self.cst2 is None:
            g = self.g
            g.dma("pool", "cst2", self.cst[:, 257:NCST], self.d["cst"][:, 257:NCST], *toks)
            self.cst2 = g.dma("pool", "cst2", self.rows[:, :], self.d["rows"].broadcast_to([P, NROW]))

    def need(self, k):
        f, self.todo[k] = self.todo[k], None
        if f:
            f()

    def settle(self):
        for k in range(8):
            self.need(k)

    def squares(self, src, toks, k, e):
        if src is self.xT:
            self.need(k)
        s = self.sq[:, k, 0:self.T]
        x = src[:, k, 0:self.T]
        if e == "act":
            return self.g.act(s, x, ACT.Square, toks[k], self.sqtok)
        return self.g.tt(s, x, x, ALU.mult, toks[k], self.sqtok, e=e)

    def pair(self, k, *toks):
        s = self.sq
        return self.g.tt(s[:, k, 0:self.T], s[:, k, 0:self.T], s[:, k + 1, 0:self.T], ALU.add, *toks)

    def sums(self, mult, add, pairs):
        g, T = self.g, self.T
        b, ps, w = g.bank()
        for k in range(0, 8, 2):
            tk = pairs(k) if callable(pairs) else pairs[k // 2]
            for m, c, n in self.tiles():
                fin = m == self.tiles()[-1][0]
                tp = g.mm(ps[0:n, m:m + 1], [(self.sq[:, k, c:c + n], self.ones[:, 0:1])], tk, *w,
                          first=k == 0 and m == 0, final=k == 6, inc=k == 6 and fin, loose=True)
        self.sqtok = None
        r = self.small[:, 300:303]
        parts = [(P, 0, 2)] + ([(16, 2, 3)] if T == T3 else [])
        for n, x, y in parts:
            tk = g.ts(r[0:n, x:y], ps[0:n, x:y], mult, add, ALU.mult, ALU.add, tp)
        g.free(b, tk)
        half = self.c("half")
        for n, x, y in parts:
            tk = g.tt(r[0:n, x:y], r[0:n, x:y], half[0:n, :].broadcast_to([n, y - x]), ALU.pow, tk, e="pool")
        self.release()
        return tk

    def spread(self, tk):
        g = self.g
        r = self.small[:, 300:303]
        b, ps, w = g.bank()
        for m, c, n in self.tiles():
            tp = g.mm(ps[:, c:c + n], [(r[0:n, m:m + 1].broadcast_to([n, P]), self.ident[0:n, 0:n])], tk, *w)
        return b, ps, tp

    def rms(self, src, toks, mult, add, pairs=None):
        self.sqtok = self.sqtok or ("pe", self.g.n["pe"])

        def made(k):
            return self.pair(k, *[self.squares(src, toks, k + i, ("act", "dve")[i]) for i in range(2)])

        return self.spread(self.sums(mult, add, pairs or made))

    def rsqrt(self, out, ps, tp, mult, add, T, b=None):
        g = self.g
        tk = g.ts(out, ps, mult, add, ALU.mult, ALU.add, tp)
        if b is not None:
            g.free(b, tk)
        tk = g.recip(out, out, tk)
        return g.act(out, out, ACT.Sqrt, tk)

    def prenorm(self, gain, j=0):
        g, T = self.g, self.T
        b, ps, tp = self.rms(self.xT, self.xtok, 1.0 / D, 1e-6)
        whole, toks = [], []
        for k in range(9):
            if k < 8:
                whole.append(g.stt(self.sq[:, k, 0:T], self.xT[:, k, 0:T], self.col(gain, j * 8 + k), ps[:, 0:T],
                                   ALU.mult, ALU.mult, tp))
            if k:
                toks.append(g.split(self.H[:, k - 1, 0:T], self.L[:, k - 1, 0:T], self.sq[:, k - 1, 0:T],
                                    whole[k - 1]))
        g.free(b, whole[7])
        return toks

    def lazynorm(self, gain, j=0):
        g, T = self.g, self.T
        toks, sq = [], []
        self.sqtok = ("pe", g.n["pe"])
        self.need(0)
        for k in range(8):
            if k < 7:
                self.need(k + 1)
            c = self.col(gain, j * 8 + k)
            t = g.act(self.H[:, k, 0:T], self.xT[:, k, 0:T], ACT.Copy, self.xtok[k], scale=c)
            sq.append(self.squares(self.xT, self.xtok, k, "act"))
            toks.append(g.stt(self.L[:, k, 0:T], self.xT[:, k, 0:T], c, self.H[:, k, 0:T].bitcast(F32),
                              ALU.mult, ALU.subtract, t))

        def first():
            pairs = [self.pair(k, sq[k], sq[k + 1]) for k in range(0, 8, 2)]
            return self.sums(1.0 / D, 1e-6, pairs)

        def second(t):
            b, ps, tp = self.spread(t)
            t = g.cp(self.rstd[:, 2, 0:T], ps[:, 0:T], tp, e="act")
            g.free(b, t)
            return t

        return toks, (first, second)

    def evac8(self, banks, T):
        g = self.g
        toks = []
        for k, (b, ps, tp) in enumerate(banks):
            tk = g.cp(self.yT[:, k, 0:T], ps[:, 0:T], tp, e=("dve", "act")[k % 2])
            g.free(b, tk)
            toks.append(tk)
        return toks

    def postnorm(self, banks, gain, j, half, scaled=False, early=False):
        g, T = self.g, self.T
        pairs, toks = None, []
        if early:
            pairs = []
            self.sqtok = ("pe", g.n["pe"])
            for k, (b, ps, tp) in enumerate(banks):
                y = self.yT[:, k, 0:T]
                if scaled:
                    t = g.tt(y, ps[:, 0:T], self.rstd[:, 2, 0:T], ALU.mult, tp)
                else:
                    t = g.cp(y, ps[:, 0:T], tp)
                g.free(b, t)
                t = g.act(self.sq[:, k, 0:T], y, ACT.Square, t, self.sqtok)
                if k % 2:
                    pairs.append(self.pair(k - 1, t))
        else:
            toks = self.evac8(banks, T)
        f = 4.0 if half else 1.0
        b, ps, tp = self.rms(self.yT, toks, f / D, f * 1e-6, pairs)

        def update(k):
            tk = g.stt(self.yT[:, k, 0:T], self.yT[:, k, 0:T], self.col(gain, j * 8 + k), ps[:, 0:T],
                       ALU.mult, ALU.mult, tp)
            if k == 7:
                g.free(b, tk)
            self.xtok[k] = g.tt(self.xT[:, k, 0:T], self.xT[:, k, 0:T], self.yT[:, k, 0:T], ALU.add, tk,
                                e=("dve", "pool")[k % 2])

        self.todo = [lambda k=k: update(k) for k in range(8)]

    def layernorm(self, banks, n, half):
        g, T = self.g, self.T
        f = 2.0 if half else 1.0
        yt = []
        for k, (b, ps, tp) in enumerate(banks):
            tk = g.stt(self.yT[:, k, 0:T], self.xT[:, k, 0:T], ALPHA * f, ps[:, 0:T], ALU.mult, ALU.add, tp)
            g.free(b, tk)
            yt.append(tk)
        b, ps, w = g.bank()
        for k in range(8):
            tp = g.mm(ps[:, 0:T], [(self.ones, self.yT[:, k, 0:T])], yt[k], *w, first=k == 0, final=k == 7,
                      inc=k == 7)
        yt = [g.stt(self.yT[:, k, 0:T], ps[:, 0:T], -1.0 / D, self.yT[:, k, 0:T], ALU.mult, ALU.add, tp)
              for k in range(8)]
        g.free(b, yt[7])
        b, ps, tp = self.rms(self.yT, yt, 1.0 / D, f * f * 1e-5)

        def update(k):
            tk = g.stt(self.yT[:, k, 0:T], self.yT[:, k, 0:T], self.col(f"ln{n}_g_2", k), ps[:, 0:T],
                       ALU.mult, ALU.mult, tp)
            if k == 7:
                g.free(b, tk)
            self.xtok[k] = g.act(self.xT[:, k, 0:T], self.yT[:, k, 0:T], ACT.Identity, tk,
                                 bias=self.col(f"ln{n}_b_2", k))

        self.todo = [lambda k=k: update(k) for k in range(8)]

    def splitx(self):
        T = self.T
        toks = []
        self.need(0)
        for k in range(8):
            if k < 7:
                self.need(k + 1)
            toks.append(self.g.split(self.H[:, k, 0:T], self.L[:, k, 0:T], self.xT[:, k, 0:T], self.xtok[k]))
        return toks

    def release(self):
        while self.spent:
            self.g.free_weight(*self.spent.pop(0))

    def colunit(self, name, j):
        self.release()
        w, hi, lo, t = self.g.weight(self.d[name][j])
        return w, [x.rearrange("p (k n) -> p k n", k=8) for x in (hi, lo)], t

    def rowunit(self, name, j):
        self.release()
        w, hi, lo, t = self.g.weight(self.d[name][j])
        return w, (hi, lo), t

    def gettmp(self):
        i = self.ntmp % 4
        self.ntmp += 1
        return i, self.tmp[:, i, :], self.tmp_free[i]

    def down(self, name, src, toks, T, nk):
        g = self.g
        banks = [g.bank() for _ in range(8)]
        self.release()
        ends = nk > 8
        groups = [range(3)] * ends + [(k,) for k in range(3 * ends, nk - 3)] + [range(nk - 3, nk)]
        for ks in groups:
            us = [self.rowunit(name, k) for k in ks]
            fin = ks[-1] == nk - 1
            for n, (b, ps, wt) in enumerate(banks):
                c = slice(n * P, (n + 1) * P)
                for k, (i, w, t) in zip(ks, us):
                    end = k == nk - 1
                    tk = g.mm3(ps[:, 0:T], [x[:, c] for x in w], [x[:, k, 0:T] for x in src], t, toks[k], *wt,
                               first=k == 0, final=end, inc=end or n == 7)
                if n == 7:
                    last = g.n["pe"]
                if fin:
                    yield b, ps, tk
            for n, (i, w, t) in enumerate(us):
                done = i, ("pe", last - len(us) + 1 + n)
                if fin:
                    self.spent.append(done)
                else:
                    g.free_weight(*done)

    def ffn(self, ht, wg, wu, wd, later=None):
        g, T = self.g, self.T
        src = self.hp
        hf = []
        tr = None
        held = []
        for js in ((0, 1),) + tuple((j,) for j in range(2, NF)):
            us = [[self.colunit(name, j), g.bank()] for j in js for name in (wg, wu)]
            tps = []
            if js[0] == 0:
                for k in range(8):
                    if k == 7 and later:
                        tr = later[0]()
                    for (i, w, t), (b, ps, wt) in us:
                        tps.append(g.mm3(ps[:, 0:T], [x[:, k, :] for x in w], [x[:, k, 0:T] for x in src], t, ht[k],
                                         *wt, first=k == 0, final=k == 7, inc=k == 7))
                tps = tps[-4:]
            else:
                for (i, w, t), (b, ps, wt) in us:
                    for k in range(8):
                        tp = g.mm3(ps[:, 0:T], [x[:, k, :] for x in w], [x[:, k, 0:T] for x in src], t, ht[k], *wt,
                                   first=k == 0, final=k == 7, inc=k == 7)
                    tps.append(tp)
                    if later and js[0] == 2 and len(tps) == 1:
                        tr = later[1](tr)
            for n, ((i, w, t), _) in enumerate(us):
                g.free_weight(i, tps[n])
            held += [(j, us[2 * n][1], us[2 * n + 1][1], tps[2 * n], tps[2 * n + 1]) for n, j in enumerate(js)]
            if later and js[0] == 0:
                continue
            r = self.rstd[:, 2, 0:T]
            tmps = [self.gettmp() for _ in held]
            ts = []
            for (i, tmp, tf), (j, (bg, pg, _), _, tg, tu) in zip(tmps, held):
                if later:
                    t = g.tt(tmp[:, 0:T], pg[:, 0:T], r, ALU.mult, tg, tr, tf)
                    g.free(bg, t)
                    ts.append(g.act(tmp[:, 0:T], tmp[:, 0:T], ACT.Silu, t))
                else:
                    ts.append(g.act(tmp[:, 0:T], pg[:, 0:T], ACT.Silu, tg, tf))
                    g.free(bg, ts[-1])
            for t, (i, tmp, tf), (j, _, (bu, pu, _), tg, tu) in zip(ts, tmps, held):
                tmp = tmp[:, 0:T]
                t = g.tt(tmp, tmp, pu[:, 0:T], ALU.mult, t, tu)
                g.free(bu, t)
                t = g.split(self.hf[0][:, j, 0:T], self.hf[1][:, j, 0:T], tmp, t)
                self.tmp_free[i] = t
                hf.append(t)
            held = []
            if js[0] == 2:
                self.tables(tps[0])
        return self.down(wd, self.hf, hf, T, NF)

    def ffn1(self, n):
        ht, later = self.lazynorm(n + "_pre_g")
        banks = self.ffn(ht, n + "_w_gate", n + "_w_up", n + "_w_down", later)
        self.postnorm(banks, n + "_post_g", 0, True, scaled=True, early=True)

    def ffn2(self, n, ln):
        banks = self.ffn(self.splitx(), n + "_w_gate_2", n + "_w_up_2", n + "_w_out_2")
        self.layernorm(banks, ln, True)

    def ffn3(self, layer, i):
        ht, later = self.lazynorm("norm_gains_3", layer * 6 + 4 * i)
        banks = self.ffn(ht, f"g3_{layer}{i}", f"u3_{layer}{i}", f"d3_{layer}{i}", later)
        self.postnorm(banks, "norm_gains_3", layer * 6 + 4 * i + 1, True, scaled=True, early=True)

    def enter3(self):
        self.settle()
        self.g.fence()
        self.load_x(self.d["meta_tokens_3"], T1)
        self.T = T3


    def together(self, *work, lead=1):
        for i, w in enumerate(work):
            for _ in range(lead * (len(work) - 1 - i)):
                next(w)
        work = list(work)
        while work:
            work = [w for w in work if next(w, self) is not self]

    def softmax(self, S, H, nk, rows, toks, n, sink=None, gate=None, floor=False):
        g = self.g
        sm = self.small[0:rows, 64 * n:64 * n + 64]
        mx, den, e = sm[:, 0:H], sm[:, 16:16 + H], sm[:, 32:32 + H]
        tk = g.red(mx, S, ALU.max, *toks)
        if sink is not None:
            tk = g.tt(mx, mx, sink, ALU.max, tk)
        if floor:
            tk = g.ts(mx, mx, -1e20, None, ALU.max, None, tk)
        tk = g.ts(mx, mx, -1.0, None, ALU.mult, None, tk)
        if sink is not None:
            ts = g.tt(e, sink, mx, ALU.add, tk)
            te = g.act(e, e, ACT.Exp, ts)
        for h in range(H):
            ta = g.act(S[:, h, :], S[:, h, :], ACT.Exp, tk, bias=mx[:, h:h + 1], accum_out=den[:, h:h + 1])
        if sink is not None:
            ta = g.tt(den, den, e, ALU.add, ta)
        yield
        if floor:
            ta = g.ts(den, den, 1e-30, None, ALU.max, None, ta)
        ta = g.recip(den, den, ta)
        if gate is not None:
            ta = g.tt(den, den, gate, ALU.mult, ta)
        for h in range(H):
            tk = g.ts(S[:, h, :], S[:, h, :], den[:, h:h + 1], None, ALU.mult, None, ta)
        return tk

    def turn(self, dst, src, rows, widths, toks, wfree=()):
        g = self.g
        b, ps, w = g.bank()
        out = []
        for i, (c, wd) in enumerate(widths):
            tp = g.tr(ps[0:wd, i * P:i * P + rows], src[:, c:c + wd], self.ident[0:rows, 0:rows], *toks, *w)
        e = ("dve", "act")[self.nturn % 2]
        self.nturn += 1
        full = [i for i, (c, wd) in enumerate(widths) if wd == P]
        if full:
            n = len(full)
            tk = g.cp(dst[:, 0:n, 0:rows], ps[:, 0:n * P].rearrange("p (n r) -> p n r", n=n)[:, :, 0:rows], tp,
                      *wfree, e=e)
            out.append(tk)
        for i, (c, wd) in enumerate(widths):
            if wd != P:
                tk = g.cp(dst[0:wd, i, 0:rows], ps[0:wd, i * P:i * P + rows], tp, *wfree, e=e)
                out.append(tk)
        g.free(b, *out)
        return out

    sqtok = None
    nturn = 0

    def linear(self, name, n, src, toks, T, fresh=False):
        g = self.g
        if fresh:
            us = [(self.colunit(name, j), g.bank()) for j in range(2)]
            for kk in range(8):
                for (i, w, t), (b, ps, wt) in us:
                    tp = g.mm3(ps[:, 0:T], [x[:, kk, :] for x in w], [x[:, kk, 0:T] for x in src], t, toks[kk], *wt,
                               first=kk == 0, final=kk == 7, inc=kk == 7)
            done = [(tp[0], tp[1] - 1), tp]
            for j in range(2):
                g.free_weight(us[j][0][0], done[j])
            for j in range(2):
                yield j, us[j][1][0], us[j][1][1], done[j]
        for j in range(2 * fresh, n):
            i, w, t = self.colunit(name, j)
            b, ps, wt = g.bank()
            for kk in range(8):
                tp = g.mm3(ps[:, 0:T], [x[:, kk, :] for x in w], [x[:, kk, 0:T] for x in src], t, toks[kk], *wt,
                           first=kk == 0, final=kk == 7, inc=kk == 7)
            g.free_weight(i, tp)
            yield j, b, ps, tp

    def nsa(self):
        g, A = self.g, self.A
        at = [0]

        def buf(n, *shape):
            v = A[:, at[0]:at[0] + n]
            at[0] += n
            if shape:
                names = "abcd"[:len(shape)]
                v = v.rearrange("p (%s) -> p %s" % (" ".join(names), " ".join(names)), **dict(zip(names, shape)))
            return v

        qT = buf(4 * T1, 4, T1)
        kD = {s: buf(2 * T1, 2, T1) for s in ("ks", "kw")}
        kp = {s: buf(2 * T1, 2, T1) for s in ("kc", "vc")}
        V = buf(2 * T1, 2, T1)
        gate = buf(2 * 24, 2, 8, 3)
        z = buf(4 * 258, 4, 258)
        cb = buf(4 * T1, 4, T1)
        hid = buf(64, 2, 2, 16)
        kcT = buf(16 * 2, 2, 16)
        vc2 = buf(2 * 64, 2, 64)
        S1 = buf(8 * T1, 8, T1)
        S2 = buf(8 * T1, 8, T1)
        S3 = buf(8 * 16, 8, 16)
        E = S1.rearrange("p h t -> p (h t)")[:, 0:960].rearrange("p (s j g n) -> p s j g n", s=2, j=16, g=2)
        PT = buf(8 * 5 * P, 8, 5, P)
        buf(2048)
        mix = (self.sqR, self.over("nsal", at[0] - 2048, 8, T1))
        ig, (wg,), twg = g.unit((0, 192, 0, P, self.d["nsa_g"]))
        wg = wg.rearrange("p (k n) -> p k n", k=8)
        w1s = []

        def cmp_load(s):
            i2, (w1,), t1 = g.unit((0, SLOT, 0, P, self.d["cmp_w1_" + s]))
            w1s.append((i2, w1, t1))

        cmp_load("k")
        ht = self.prenorm("l0_mix_pre_g")
        src = self.hp
        w2 = self.cols[:, NCOL:NCOL + P]
        tkc = [None, None]

        def compressed():
            for s, name in enumerate(("kc", "vc")):
                i2, w1, t1 = w1s[s]
                w1 = w1.rearrange("p (j n) -> p j n", j=16)
                b, ps, wt = g.bank()
                pe_at = COLS["l0_cmp_pe_" + "kv"[s]][0]
                kv4 = kp[name].rearrange("p g (n t) -> p t g n", t=16)
                for x in range(2):
                    te = g.tt(E[:, s, 8 * x:8 * x + 8], kv4[:, 0:16:2, :, x:x + 15],
                              bc(self.cols[:, pe_at + 8 * x:pe_at + 8 * x + 8], 2, 15), ALU.add, tkp)
                tp = g.mm(ps[:, 0:30], [(w1[:, j, :], E[:, s, j]) for j in range(16)], t1, te, *wt)
                g.free_unit(i2, tp)
                th = g.act(hid[:, s, :, 0:15], ps[:, 0:30].rearrange("p (g n) -> p g n", g=2), ACT.Gelu_apprx_tanh, tp)
                g.free(b, th)
                yield
                b, ps, wt = g.bank()
                if s == 0:
                    for gr in range(2):
                        tp = g.mm(ps[0:64, gr * 16:gr * 16 + 15], [(w2[:, 0:64], hid[:, s, gr, 0:15])], th, *wt)
                    p3 = ps[0:64, 0:32].rearrange("p (a b) -> p a b", a=2)[:, :, 0:15]
                    g.cp(kcT[0:64, :, 0:15], p3, tp)
                    tkc[s] = g.cp(kcT[64:128, :, 0:15], p3, tp)
                else:
                    for gr in range(2):
                        tp = g.mm(ps[0:15, gr * 64:gr * 64 + 64], [(hid[:, s, gr, 0:15], w2[:, 64:128])], th, *wt)
                    tkc[s] = g.cp(vc2[0:15, :, :], ps[0:15, 0:128].rearrange("p (a b) -> p a b", a=2), tp)
                g.free(b, tkc[s])
                yield

        cmp_ = compressed()
        tq = [None] * 4
        cu = {}
        for j, b, ps, tp in self.linear("nsa_in", 20, src, ht, T1, fresh=True):
            if j == 1:
                bg, pg, wt = g.bank()
                for m in range(2):
                    tpg = g.mm(pg[:, m * 24:m * 24 + 24],
                               [(self.sq[:, k, m * P:(m + 1) * P], wg[:, k, :]) for k in range(8)], twg, *ht, *wt)
                tg = g.act(gate.rearrange("p a b c -> p (a b c)"), pg[:, 0:48], ACT.Sigmoid, tpg)
                g.free(bg, tg)
                g.free_unit(ig, tpg)
                cmp_load("v")
                for e in ("act", "dve"):
                    g.wait(e, [tpg])
            if j < 4:
                tk = g.act(qT[:, j, :], ps[:, 0:T1], ACT.Copy, tp, scale=0.125)
                tq[j] = tk
            elif j < 6:
                s = ("kc", "vc")[j - 4]
                for i in range(2):
                    rows = ps[64 * i:64 * i + 64, :]
                    g.cp(kp[s][0:64, i, 0:T1], rows[:, 0:T1], tp)
                    tk = g.cp(kp[s][64:128, i, 0:T1 - 1], rows[:, 1:T1], tp)
                tkp = tk
            elif j < 8:
                s = ("ks", "kw")[j - 6]
                for i in range(2):
                    rows = ps[64 * i:64 * i + 64, 0:T1]
                    g.cp(kD[s][0:64, i, :], rows, tp, e="act")
                    tk = g.cp(kD[s][64:128, i, :], rows, tp, e="act")
                tkd = tk
            elif j < 12:
                if j > 8:
                    next(cmp_, None)
                tk = g.cp(cb[:, j - 8, :], ps[:, 0:T1], tp, e="act")
                cu[j - 8] = tk
            elif j < 16:
                if j == 12:
                    tz = g.op("dve", lambda: self.g.nc.vector.memset(z[:, :, 0:2], 0.0))
                tk = g.cp(z[:, j - 12, 2:258], ps[:, 0:T1], tp)
            else:
                c = j - 16
                next(cmp_, None)
                tk = g.tt(z[:, c, 2:258], z[:, c, 2:258], ps[:, 0:T1], ALU.mult, tp, tz)
                g.free(b, tk)
                i, t, tf = self.gettmp()
                t = t[:, 0:T1]
                w = [self.col("l0_conv_w", r * 4 + c) for r in range(3)]
                tk = g.ts(t, z[:, c, 2:258], w[2], self.col("l0_conv_b", c), ALU.mult, ALU.add, tk, tf)
                tk = g.stt(t, z[:, c, 1:257], w[1], t, ALU.mult, ALU.add, tk)
                tk = g.stt(t, z[:, c, 0:256], w[0], t, ALU.mult, ALU.add, tk)
                tk = g.tt(t, t, cb[:, c, :], ALU.mult, tk, cu[c])
                tconv = g.split(mix[0][:, 4 + c, 0:T1], mix[1][:, 4 + c, 0:T1], t, tk)
                self.tmp_free[i] = tconv
                continue
            g.free(b, tk)
        for x in range(2):
            i, w, t = self.colunit("nsa_v", x)
            b, ps, wt = g.bank()
            for m in range(2):
                for k in range(8):
                    tp = g.mm3(ps[:, m * P:(m + 1) * P], [y[:, k, m * P:(m + 1) * P] for y in src],
                               [y[:, k, :] for y in w], t, *wt, first=k == 0, final=k == 7, inc=k == 7)
            tv = g.cp(V[:, :, x * P:(x + 1) * P], ps[:, 0:256].rearrange("p (m c) -> p m c", m=2), tp)
            g.free(b, tv)
            g.free_weight(i, tp)
        def heads(u):
            ptf = [None, None]
            so = None
            gr = u // 2
            sl = slice(2 * u, 2 * u + 2)
            for m in range(2):
                nk = P * (m + 1)
                for h in (2 * u, 2 * u + 1):
                    o = 64 * (h % 2)
                    q = qT[o:o + 64, h // 2, m * P:(m + 1) * P]
                    b, ps, wt = g.bank()
                    for x, s in enumerate(("ks", "kw")):
                        tp = g.mm(ps[:, x * 256:x * 256 + nk], [(q, kD[s][o:o + 64, gr, 0:nk])], tkd, tq[h // 2], *wt)
                    for x, S in enumerate((S1, S2)):
                        tk = g.stt(S[:, h, 0:nk], self.c("alibi")[:, m * 256:m * 256 + nk], 0.5 ** (h + 1),
                                   ps[:, x * 256:x * 256 + nk], ALU.mult, ALU.add, tp, so)
                    g.free(b, tk)
                    b, ps, wt = g.bank()
                    tp = g.mm(ps[:, 0:15], [(q, kcT[o:o + 64, gr, 0:15])], tkc[0], *wt)
                    tk = g.stt(S3[:, h, 0:15], self.c("alibi_cmp")[:, m * 16:m * 16 + 15], 0.5 ** (h + 1),
                               ps[:, 0:15], ALU.mult, ALU.add, tp, so)
                    g.free(b, tk)
                    if h % 2:
                        yield
                t1 = yield from self.softmax(S1[:, sl, 0:nk], 2, nk, P, [tk], u, gate=gate[:, m, sl, 1])
                t2 = yield from self.softmax(S2[:, sl, 0:nk], 2, nk, P, [tk], u, gate=gate[:, m, sl, 2])
                t3 = yield from self.softmax(S3[:, sl, 0:15], 2, 15, P, [tk], u, gate=gate[:, m, sl, 0], floor=True)
                for h in (2 * u, 2 * u + 1):
                    o = 64 * (h % 2)
                    pt = PT[:, h]
                    wf = (ptf[h % 2],)
                    ta = self.turn(pt[:, 0:2], S1[:, h, :], P, [(c * P, P) for c in range(m + 1)], [t1, tg], wf)
                    tb = self.turn(pt[:, 2:4], S2[:, h, :], P, [(c * P, P) for c in range(m + 1)], [t2], wf)
                    tc = self.turn(pt[:, 4:5], S3[:, h, 0:15], P, [(0, 15)], [t3], wf)
                    yield
                    if h % 2 == 0:
                        bo, po, wt = g.bank()
                    pairs = []
                    for c in range(m + 1):
                        pairs.append((V[:, c, gr * 64:gr * 64 + 64], pt[:, c, :]))
                        pairs.append((V[:, c, P + gr * 64:P + gr * 64 + 64], pt[:, 2 + c, :]))
                    pairs.append((vc2[0:15, gr, :], pt[0:15, 4, :]))
                    so = g.mm(po[o:o + 64, 0:P], pairs, tv, tkc[1], *ta, *tb, *tc, *wt)
                    ptf[h % 2] = so
                    if h % 2:
                        ty[h // 2] = g.split(mix[0][:, h // 2, m * P:(m + 1) * P], mix[1][:, h // 2, m * P:(m + 1) * P],
                                             po[:, 0:P], so)
                        g.free(bo, ty[h // 2])

        ty = [None] * 4
        self.together(*[heads(u) for u in range(4)], lead=0)
        banks = self.down("nsa_out", mix, ty + [tconv] * 4, T1, 8)
        self.postnorm(banks, "l0_mix_post_g", 0, False)

    def tokmajor(self, name, src, toks):
        g = self.g
        banks = [[g.bank() for _ in range(2)] for _ in range(2)]
        for k in range(8):
            i, w, t = self.rowunit(name, k)
            for m in range(2):
                for h in range(2):
                    b, ps, wt = banks[m][h]
                    tk = g.mm3(ps[:, :], [x[:, k, m * P:(m + 1) * P] for x in src],
                               [x[:, h * 512:(h + 1) * 512] for x in w], t, toks[k], *wt,
                               first=k == 0, final=k == 7, inc=k == 7 or (m == 1 and h == 1))
                    if k == 7:
                        banks[m][h] = (b, ps, tk)
            g.free_weight(i, ("pe", g.n["pe"]))
        return banks

    def rwkv(self):
        g, A, nc = self.g, self.A, self.g.nc
        C0 = float(np.exp(np.float64(-0.5)))
        v3 = lambda o: A[:, o:o + 2048].rearrange("p (m c) -> p m c", m=2)
        r, k, v, a, lw, kk = [v3(2048 * i) for i in range(6)]
        W = 12288
        xx = self.yT
        xf = [A[:, W + 2048 * i:W + 2048 * i + 2048].rearrange("p (k t) -> p k t", k=8) for i in range(2)]
        xm = [self.hp, [self.over(f"xm{i}", W + 2048 * i, 8, T1) for i in range(2)]]
        ht = self.prenorm("l1_mix_pre_g")
        hT = self.sq
        g.ts(xx[:, :, 0:1], hT[:, :, 0:1], -1.0, None, ALU.mult, None, *ht)
        txx = g.tt(xx[:, :, 1:T1], hT[:, :, 0:T1 - 1], hT[:, :, 1:T1], ALU.subtract, *ht)
        xfree = [("pe", g.n["pe"]), None]
        count = [0]
        lf = self.Lf.rearrange("p k t -> p (k t)")

        def mixed(i, split=False):
            n = count[0] % 2
            count[0] += 1
            if not split:
                return n, xf[n], [g.stt(xf[n][:, q, 0:T1], xx[:, q, 0:T1], self.col("l1_mu", i * 8 + q),
                                        hT[:, q, 0:T1], ALU.mult, ALU.add, txx, xfree[n]) for q in range(8)]
            toks = []
            for q in range(8):
                x, v, tf = self.gettmp()
                t = g.stt(v[:, 0:T1], xx[:, q, 0:T1], self.col("l1_mu", i * 8 + q), hT[:, q, 0:T1],
                          ALU.mult, ALU.add, txx, tf)
                self.tmp_free[x] = g.split(xm[n][0][:, q, 0:T1], xm[n][1][:, q, 0:T1], v[:, 0:T1], t, xfree[n])
                toks.append(self.tmp_free[x])
            return n, xm[n], toks

        il, (lora,), tl = g.unit((0, SLOT, 0, P, self.d["lora1"]))
        lora = lora.rearrange("p (k n) -> p k n", k=8)
        lT = self.rstd.rearrange("p k t -> p (k t)")[:, 0:768].rearrange("p (j t) -> p j t", j=3)
        tlo = []
        for j, (i, c0, w, f) in enumerate(((1, 0, 64, ACT.Tanh), (4, 64, 64, ACT.Copy), (5, 128, 128, ACT.Sigmoid))):
            n, x, toks = mixed(i)
            b, ps, wt = g.bank()
            for q in range(8):
                tp = g.mm(ps[0:w, 0:T1], [(lora[:, q, c0:c0 + w], x[:, q, 0:T1])], tl, toks[q], *wt,
                          first=q == 0, final=q == 7, inc=q == 7)
            xfree[n] = tp
            tk = g.act(lT[0:w, j, :], ps[0:w, 0:T1], f, tp)
            g.free(b, tk)
            tlo.append(tk)
        g.free_unit(il, tp)
        ib, (wa,), tb = g.unit((0, 2048, 0, 65, self.d["lora2"]))
        tone = g.op("dve", lambda: nc.vector.memset(lT[64:65, 0:2, :], 1.0))
        for j, dst in ((0, lw), (1, a)):
            for m in range(2):
                for h in range(2):
                    b, ps, wt = g.bank()
                    x = lT[:, j, m * P:(m + 1) * P]
                    hs = slice(h * 512, (h + 1) * 512)
                    tp = g.mm(ps[:, :], [(x[0:65], wa[0:65, j * 1024 + h * 512:j * 1024 + h * 512 + 512])],
                              tb, tlo[j], tone, *wt)
                    tk = g.act(dst[:, m, hs], ps[:, :], ACT.Sigmoid, tp)
                    g.free(b, tk)
        ta_ = tk
        g.free_unit(ib, tp)
        xfree = [xfree[0], ("pe", g.n["pe"])]
        iv, (kkg, kag), tv = g.unit((0, 1024, 0, P, self.d["l1_k_k"].broadcast_to([P, 1024])),
                                    (1024, 1024, 0, P, self.d["l1_k_a"].broadcast_to([P, 1024])))
        iw, (rkg,), tw = g.unit((0, 1024, 0, P, self.d["l1_r_k"].broadcast_to([P, 1024])))
        s16 = self.small
        bonus = s16[:, 256:288].rearrange("p (m h) -> p m h", m=2)
        sc = A[:, W + 4096:W + 6144].rearrange("p (m c) -> p m c", m=2)
        h3 = lambda ap: ap.rearrange("p (h j) -> p h j", j=64)
        got = {}

        def keys(m):
            t = g.tt(kk[:, m, :], k[:, m, :], kkg, ALU.mult, tv, *got["l1_w_k"])
            t = g.act(sc[:, m, :], kk[:, m, :], ACT.Square, t)
            ss = s16[:, 16 * m:16 * m + 16]
            t = g.red(ss, h3(sc[:, m, :]), ALU.add, t)
            t = g.ts(ss, ss, 1e-12, None, ALU.max, None, t)
            t = g.recip(ss, ss, t)
            t = g.act(ss, ss, ACT.Sqrt, t)
            g.tt(h3(kk[:, m, :]), h3(kk[:, m, :]), bc(ss, 64), ALU.mult, t)
            t = g.stt(sc[:, m, :], a[:, m, :], -1.0, kag, ALU.add, ALU.mult, ta_)
            t = g.stt(k[:, m, :], sc[:, m, :], 1.0, k[:, m, :], ALU.add, ALU.mult, t)
            return g.tt(a[:, m, :], a[:, m, :], kk[:, m, :], ALU.mult)

        def extra(m):
            t = g.tt(sc[:, m, :], r[:, m, :], k[:, m, :], ALU.mult, *got["l1_w_r"])
            t = g.tt(sc[:, m, :], sc[:, m, :], rkg, ALU.mult, t, tw)
            return g.red(bonus[:, m, :], h3(sc[:, m, :]), ALU.add, t)

        for i, name, dst in ((2, "l1_w_k", k), (0, "l1_w_r", r), (3, "l1_w_v", v)):
            n, x, toks = mixed(i, True)
            if i == 0:
                keys(0)
            if i == 3:
                g.free_unit(iv, keys(1))
                extra(0)
            banks = self.tokmajor(name, x, toks)
            xfree[n] = ("pe", g.n["pe"])
            got[name] = []
            for m in range(2):
                for h in range(2):
                    b, ps, tp = banks[m][h]
                    tk = g.cp(dst[:, m, h * 512:(h + 1) * 512], ps[:, :], tp, e=("dve", "act")[h])
                    g.free(b, tk)
                    got[name].append(tk)
        g.free_unit(iw, extra(1))
        g.fence()
        ig, (lng, lnb), tln = g.unit((0, 1024, 0, P, self.d["l1_lnx_g"].broadcast_to([P, 1024])),
                                     (1024, 1024, 0, P, self.d["l1_lnx_b"].broadcast_to([P, 1024])))
        i2, (g2,), tg2 = g.unit((0, 1024, 0, P, self.d["l1_w_g2"]))
        fl = self.yT.rearrange("p k t -> p (k t)")
        ST = self.sq_[0:64, 0:1024].rearrange("p (h i) -> p h i", h=16)
        t0 = g.op("dve", lambda: nc.vector.memset(ST, 0.0))
        m64 = self.c("m64")
        p4 = lambda x: x[:, :].rearrange("p (h c) -> p h c", h=4)

        def heads(n, hgs):
            o = W + 4096 * n
            ART = A[:, o:o + 1024].rearrange("p (h i t) -> p h i t", h=4, i=2)
            bk = A[:, o + 1024:o + 2048]
            BK = bk.rearrange("p (i h t) -> p i h t", i=2, h=4)
            Tm, Tt = p4(bk[:, 0:512]), p4(bk[:, 512:1024])
            M4 = p4((A[:, W + 2048:W + 4096], self.Hf.rearrange("p k t -> p (k t)")[:, 0:2048])[n])
            vec = (lf, fl)[n][:, 0:1536].rearrange("p (i c) -> p i c", i=6)
            exf = (self.tmp.rearrange("p k t -> p (k t)")[:, 0:1024], self.sq_[:, 1024:2048])[n]
            ex = exf.rearrange("p (i c) -> p i c", i=4)
            Mb, Wm = p4(exf[:, 0:512]), p4(exf[:, 512:1024])
            MV, TMV, U = vec[:, 1, :], vec[:, 2, :], vec[:, 3, :]
            Y1 = exf[:, 0:256]
            TAT = p4(exf[0:64, 256:768])
            mu, var = s16[:, 64 * n:64 * n + 4], s16[:, 64 * n + 16:64 * n + 20]
            sqs = exf[:, 768:1024]
            half = self.c("half").broadcast_to([P, 4])
            pc = s16[0:64, 320 + 8 * n:328 + 8 * n].rearrange("p (h c) -> p h c", h=4)
            ty = None
            for hg in hgs:
                tst = t0
                for m in range(2):
                    cs = slice(hg * 256, hg * 256 + 256)
                    hs = [slice(hg * 256 + 64 * h, hg * 256 + 64 * h + 64) for h in range(4)]
                    l = lw[:, m, cs]
                    b1, p1, w1 = g.bank()
                    g.mm(p1[:, 0:256], [(m64[:, 0:128], l)], *w1, inc=False)
                    t1 = g.mm(p1[:, 256:512], [(m64[:, 128:256], l)])
                    b2, p2, w2 = g.bank()
                    g.mm(p2[:, 0:256], [(self.c("suf64"), l)], *w2, inc=False)
                    for h in range(4):
                        t2 = g.mm(p2[0:64, 256 + 2 * h:258 + 2 * h], [(lw[:, m, hs[h]], self.c("chunk"))])
                    yield
                    t = g.act(ex[:, 0:2, :], p1[:, :].rearrange("p (i c) -> p i c", i=2), ACT.Exp, t1, ty, scale=-C0)
                    ta = g.act(ex[:, 2, :], p1[:, 256:512], ACT.Exp, t1, scale=C0)
                    tb = g.act(ex[:, 3, :], p2[:, 0:256], ACT.Exp, t2, scale=-C0)
                    tc = g.act(pc, p2[0:64, 256:264].rearrange("p (h c) -> p h c", h=4), ACT.Exp, t2, scale=-C0)
                    g.free(b1, ta)
                    g.free(b2, tc)
                    tv_ = []
                    for i, (x, e, w) in enumerate(((kk, 0, t), (r, 1, t), (a, 2, ta), (k, 2, ta), (a, 3, tb), (k, 3, tb))):
                        tv_.append(g.tt(vec[:, i, :], x[:, m, cs], ex[:, e, :], ALU.mult, w, ty,
                                        e="pool" if i > 3 else "dve"))
                    for i in range(4):
                        b, ps, w = g.bank()
                        for h in range(4):
                            tp = g.tr(ps[0:64, h * P:(h + 1) * P], vec[:, i, 64 * h:64 * h + 64], self.ident, tv_[i],
                                      *w)
                        dst = ART[0:64, :, i, :] if i < 2 else BK[0:64, i - 2, :, :]
                        tt_ = g.cp(dst, p4(ps[0:64, :]), tp, e=("dve", "act")[i % 2])
                        g.free(b, tt_)
                        if i == 2:
                            tA = tt_
                        if i % 2:
                            yield
                    for h in range(4):
                        b, ps, w = g.bank()
                        rhs = ART[0:64, h].rearrange("p i t -> p (i t)")
                        g.mm(ps[:, 0:256], [(BK[0:64, 0, h, :], rhs)], tt_, tA, *w, inc=False)
                        tp = g.mm(ps[:, 256:512], [(BK[0:64, 1, h, :], rhs)])
                        tk = g.tt(M4[:, h, :].rearrange("p (i c) -> p i c", i=2),
                                  ps[:, :].rearrange("p (i c) -> p i c", i=2), bc_mid(m64, 2), ALU.mult, tp)
                        g.free(b, tk)
                    for lv in range(6):
                        mask = self.c("level", lv)
                        tmb = g.tt(Mb, M4[:, :, 0:128], bc_mid(mask, 4), ALU.mult, tk, tv_[5])
                        idb = bc_mid(self.ident, 4)
                        b, ps, w = g.bank()
                        for h in range(4):
                            rhs = self.ident if lv == 0 else Tm[:, h, :]
                            tp = g.mm(ps[:, h * P:(h + 1) * P], [(Mb[:, h, :], rhs)], tmb, *w, inc=h == 3)
                        yield
                        if lv == 0:
                            g.tt(Tm, idb, p4(ps), ALU.subtract, tp)
                            tk = g.tt(Tt, idb, Mb, ALU.subtract, tmb)
                            g.free(b, tk)
                            continue
                        tw_ = g.cp(Wm, p4(ps), tp, e="act")
                        g.free(b, tw_)
                        if lv < 5:
                            bm, pm, w = g.bank()
                            for h in range(4):
                                tpm = g.mm(pm[:, h * P:(h + 1) * P], [(Tt[:, h, :], Wm[:, h, :])], tw_, tk, *w,
                                           inc=h == 3)
                        b, ps, w = g.bank()
                        for h in range(4):
                            tp = g.mm(ps[:, h * P:(h + 1) * P], [(Wm[:, h, :], Tt[:, h, :])], tw_, tk, *w, inc=h == 3)
                        yield
                        if lv < 5:
                            g.free(bm, g.tt(Tm, Tm, p4(pm), ALU.subtract, tpm))
                        tk = g.tt(Tt, Tt, p4(ps), ALU.subtract, tp)
                        g.free(b, tk)
                    b, ps, w = g.bank()
                    for h in range(4):
                        tp = g.mm(ps[:, 64 * h:64 * h + 64], [(M4[:, h, 256:384], v[:, m, hs[h]])], *w)
                    yield
                    t = g.cp(MV, ps[:, 0:256], tp, e="act")
                    g.free(b, t)
                    b, ps, w = g.bank()
                    for h in range(4):
                        tp = g.mm(ps[:, 64 * h:64 * h + 64], [(Tt[:, h, :], MV[:, 64 * h:64 * h + 64])], t, tk, *w)
                    bt, pt, w = g.bank()
                    for h in range(4):
                        tpt = g.mm(pt[0:64, h * P:(h + 1) * P], [(vec[:, 0, 64 * h:64 * h + 64], Tt[:, h, :])], *w)
                    yield
                    tmv = g.cp(TMV, ps[:, 0:256], tp, e="act")
                    g.free(b, tmv)
                    tat = g.cp(TAT, p4(pt[0:64, :]), tpt)
                    g.free(bt, tat)
                    by, py, wy = g.bank()
                    for c in range(2):
                        o = 64 * c
                        b, ps, w = g.bank()
                        for h in range(4):
                            st = ST[:, hg * 4 + h, :]
                            tp = g.mm(ps[o:o + 64, 64 * h:64 * h + 64], [(TAT[:, h, o:o + 64], st)], tst, tat, *w)
                        for h in range(4):
                            st = ST[:, hg * 4 + h, :]
                            ty = g.mm(py[o:o + 64, 64 * h:64 * h + 64], [(ART[0:64, h, 1, o:o + 64], st)], *wy)
                        yield
                        tu = g.stt(U[o:o + 64, :], ps[o:o + 64, 0:256], -1.0, TMV[o:o + 64, :], ALU.mult,
                                   ALU.subtract, tp, tmv)
                        g.free(b, tu)
                        b, ps, w = g.bank()
                        for h in range(4):
                            hh = slice(64 * h, 64 * h + 64)
                            tp = g.mm(ps[0:64, hh], [(vec[o:o + 64, 4, hh], U[o:o + 64, hh]),
                                                     (vec[o:o + 64, 5, hh], v[o:o + 64, m, hs[h]])], tu, tv_[5], *w)
                        yield
                        sg = ST[:, hg * 4:hg * 4 + 4, :]
                        t = g.tt(sg, sg, bc(pc[:, :, c], 64), ALU.mult, ty, tc)
                        tst = g.tt(sg, sg, ps[0:64, 0:256].rearrange("p (h i) -> p h i", h=4), ALU.add, t, tp)
                        g.free(b, tst)
                    t = g.cp(Y1, py[:, 0:256], ty, e="act")
                    g.free(by, t)
                    b, ps, w = g.bank()
                    for h in range(4):
                        hh = slice(64 * h, 64 * h + 64)
                        tp = g.mm(ps[:, hh], [(M4[:, h, 128:256], U[:, hh]), (M4[:, h, 384:512], v[:, m, hs[h]])],
                                  tu, *w)
                    yield
                    y, vb = r[:, m, cs], v[:, m, cs]
                    t = g.tt(y, Y1, ps[:, 0:256], ALU.add, tp, t)
                    g.free(b, t)
                    b, ps, w = g.bank()
                    tgt = g.mm(ps[:, 0:256], [(lT[:, 2, m * P:(m + 1) * P], g2[:, cs])], tg2, tlo[2], *w)
                    tvb = g.tt(h3(vb), h3(vb), bc(bonus[:, m, 4 * hg:4 * hg + 4], 64), ALU.mult, tp, e="pool")
                    t = g.red(mu, h3(y), ALU.add, t)
                    t = g.ts(mu, mu, 1.0 / 64, None, ALU.mult, None, t)
                    t = g.tt(h3(y), h3(y), bc(mu, 64), ALU.subtract, t)
                    t = g.act(sqs, y, ACT.Square, t)
                    yield
                    t = g.red(var, h3(sqs), ALU.add, t)
                    t = g.ts(var, var, 1.0 / 64, 64e-5, ALU.mult, ALU.add, t)
                    t = g.tt(var, var, half, ALU.pow, t, e="pool")
                    yield
                    t = g.tt(h3(y), h3(y), bc(var, 64), ALU.mult, t)
                    t = g.tt(y, y, lng[:, cs], ALU.mult, t, tln)
                    t = g.tt(y, y, lnb[:, cs], ALU.add, t)
                    t = g.tt(y, y, vb, ALU.add, t, tvb)
                    ty = g.tt(y, y, ps[:, 0:256], ALU.mult, t, tgt)
                    g.free(b, ty)
                    done.append(ty)

        done = []
        self.together(heads(0, (0, 1)), heads(1, (2, 3)), lead=2)
        g.fence()
        g.free_unit(i2, done[-1])
        g.free_unit(ig, done[-1])
        toks = self.turn_back(r, [done[-1]] * 2, self.hp)
        banks = self.down("l1_w_o", self.hp, toks, T1, 8)
        self.postnorm(banks, "l1_mix_post_g", 0, False, early=True)

    def turn_back(self, y, ty, dst):
        g = self.g
        toks = []
        for q in range(8):
            b, ps, w = g.bank()
            for m in range(2):
                tp = g.tr(ps[:, m * P:(m + 1) * P], y[:, m, q * P:(q + 1) * P], self.ident, ty[m], *w)
            tk = g.split(dst[0][:, q, 0:T1], dst[1][:, q, 0:T1], ps[:, 0:T1], tp)
            g.free(b, tk)
            toks.append(tk)
        return toks
    def carve(self, start, limit=None):
        limit = limit or self.NA
        pos = self.pos = [start]

        def buf(n, *shape):
            v = self.A[:, pos[0]:pos[0] + n]
            pos[0] += n
            assert pos[0] <= limit, pos[0]
            if shape:
                names = "abcd"[:len(shape)]
                v = v.rearrange("p (%s) -> p %s" % (" ".join(names), " ".join(names)), **dict(zip(names, shape)))
            return v

        return buf

    def softplus(self, x, t1, t2, *toks):
        g = self.g
        t = g.act(t1, x, ACT.Abs, *toks)
        t = g.act(t1, t1, ACT.Exp, t, scale=-1.0)
        t = g.act(t1, t1, ACT.Ln, t, bias=1.0)
        t = g.stt(x, x, 0.0, t1, ALU.max, ALU.add, t)
        return t

    def hybrid(self):
        g, nc = self.g, self.g.nc
        xT, xt = self.xT, self.splitx()
        X = self.hp
        mem = self.carve(0)
        merged = mem(2048, 8, T1)
        fl = lambda v: v.rearrange("p k t -> p (k t)")
        buf = self.carve(2048)
        u = buf(4 * 260, 4, 260)
        xo = self.pos[0]
        xs = buf(2048, 8, T1)
        BC = buf(2048, 8, T1)
        xdt = buf(2048, 2, 1024)
        Bt = buf(512)
        xds = buf(1024)
        S0 = buf(1024)
        GL = buf(1024, 2, 4, P)
        CS = buf(1024, 2, 4, P)
        Gm = buf(256, 2, P)
        iw, (tw, kw), tt_ = g.unit((0, 256, 0, P, self.d["tokw"]), (256, 512, 0, P, self.d["kidx"]))
        tw = tw.rearrange("p (k n) -> p k n", k=8)
        kw = kw.rearrange("p (k n) -> p k n", k=8)
        s = self.small
        dt = s[:, 0:32].rearrange("p (m h) -> p m h", m=2)
        widx = s[:, 32:64].rearrange("p (m h) -> p m h", m=2)
        scr = s[:, 64:96].rearrange("p (m h) -> p m h", m=2)
        av = s[:, 96:128].rearrange("p (m h) -> p m h", m=2)
        acs = s[:, 128:160].rearrange("p (m h) -> p m h", m=2)
        dec = s[:, 160:176]
        ah = s[:, 176:192]
        rw = lambda n: self.rows[:, ROWS[n][0]:ROWS[n][0] + 16]
        ki = self.rstd[:, 2, 0:T1]
        yss = buf(2048, 8, T1)
        zb = buf(2048, 8, T1)
        yp = [self.over("yss" + "hl"[i], xo + 2048 * i, 8, T1) for i in range(2)]
        b, ps, w = g.bank()
        for m in range(2):
            tp = g.mm(ps[:, 32 * m:32 * m + 32], [(xT[:, k, m * P:(m + 1) * P], tw[:, k, :]) for k in range(8)], tt_,
                      *w, *xt)
        ps2 = ps[:, 0:64].rearrange("p (m n) -> p m n", m=2)
        t = g.tt(dt, ps2[:, :, 0:16], bc_mid(rw("dt_bias_2"), 2), ALU.add, tp)
        tw_ = g.ts(widx, ps2[:, :, 16:32], 0.25, None, ALU.mult, None, tp)
        g.free(b, tw_)
        b, ps, w = g.bank()
        tp = g.mm(ps[0:64, 0:T1], [(kw[:, k, :], xT[:, k, 0:T1]) for k in range(8)], *w)
        g.free_unit(iw, tp)
        g.cp(ki[0:64, :], ps[0:64, 0:T1], tp, e="act")
        tki = g.cp(ki[64:128, :], ps[0:64, 0:T1], tp, e="act")
        g.free(b, tki)
        t = self.softplus(dt, scr, None, t)
        ta = g.act(ah, rw("a_log_2"), ACT.Exp)
        ta = g.ts(ah, ah, -1.0, None, ALU.mult, None, ta)
        ta = g.tt(av, dt, bc_mid(ah, 2), ALU.mult, ta, t)
        b, ps, w = g.bank()
        for m in range(2):
            tp = g.mm(ps[:, 16 * m:16 * m + 16], [(self.c("tri128"), av[:, m, :])], ta, *w)
        tp = g.mm(ps[:, 32:48], [(self.c("suf128"), av[:, 0, :])])
        tacs = g.cp(acs, ps[:, 0:32].rearrange("p (m h) -> p m h", m=2), tp)
        tdec = g.act(dec, ps[:, 32:48], ACT.Exp, tp, tacs)
        g.free(b, tdec)
        tz = g.op("dve", lambda: nc.vector.memset(u[:, :, 0:3], 0.0))
        ufree = [None] * 4
        txb = [None] * 16
        for j, b, ps, tp in self.linear("xbc", 16, X, xt, T1):
            uu = u[:, j % 4, :]
            t = g.cp(uu[:, 3:259], ps[:, 0:T1], tp, ufree[j % 4], e="act")
            g.free(b, t)
            i, v, tf = self.gettmp()
            v = v[:, 0:T1]
            wc = [self.col("conv_w_2", r * 16 + j) for r in range(4)]
            t = g.ts(v, uu[:, 3:259], wc[3], self.col("conv_b_2", j), ALU.mult, ALU.add, t, tf)
            for r in (2, 1, 0):
                t = g.stt(v, uu[:, r:r + T1], wc[r], v, ALU.mult, ALU.add, t, tz)
            ufree[j % 4] = t
            dst = xs[:, j, :] if j < 8 else BC[:, j - 8, :]
            txb[j] = g.act(dst, v, ACT.Silu, t)
            self.tmp_free[i] = txb[j]
        BT, CT = BC[:, 0:4, :], BC[:, 4:8, :]
        ty = [None] * 8

        def groups(i):
            gfree = None
            for m in range(2):
                tc = slice(m * P, (m + 1) * P)
                for gr in (2 * i, 2 * i + 1):
                    b, ps, w = g.bank()
                    tp = g.mm(ps[:, 0:P], [(BT[:, gr, tc], CT[:, gr, tc])], txb[8 + gr], txb[12 + gr], *w)
                    tg = g.tt(Gm[:, i, :], ps[:, 0:P], self.c("tri128"), ALU.mult, tp, gfree)
                    g.free(b, tg)
                    b, ps, w = g.bank()
                    for r in range(4):
                        h = 4 * gr + r
                        tp = g.mm(ps[:, r * P:(r + 1) * P],
                                  [(av[:, m, h:h + 1].broadcast_to([P, P]), self.c("tri128"))], *w)
                    yield
                    for r in range(4):
                        h = 4 * gr + r
                        t = g.ts(GL[:, i, r, :], ps[:, r * P:(r + 1) * P], acs[:, m, h:h + 1], 0.0, ALU.subtract,
                                 ALU.min, tp, tacs, gfree)
                    if m:
                        tcs = g.act(CS[:, i], ps[:, :].rearrange("p (r t) -> p r t", r=4), ACT.Exp, tp, t, gfree)
                        g.free(b, tcs)
                    else:
                        g.free(b, t)
                    t = g.act(GL[:, i], GL[:, i], ACT.Exp, t)
                    yield
                    if m:
                        tcs = g.tt(CS[:, i], CS[:, i], bc_mid(CT[:, gr, tc], 4), ALU.mult, tcs, e="pool")
                    else:
                        tcs = None
                    tgl = g.tt(GL[:, i], GL[:, i], bc_mid(Gm[:, i, :], 4), ALU.mult, t, tg)
                    for r in range(0, 4, 2):
                        b, ps, w = g.bank()
                        for h in (4 * gr + r, 4 * gr + r + 1):
                            o = 64 * (h % 2)
                            pairs = [(xdt[:, m, h * 64:h * 64 + 64], GL[:, i, h % 4, :])]
                            if m:
                                pairs.append((S0[:, h * 64:h * 64 + 64], CS[:, i, h % 4, :]))
                            tp = g.mm(ps[o:o + 64, 0:P], pairs, tgl, tcs, ts0, txd, *w)
                        q = 2 * gr + r // 2
                        ty[q] = g.stt(yss[:, q, tc], xs[:, q, tc], self.col("d_skip_2c", q), ps[:, 0:P], ALU.mult,
                                      ALU.add, tp)
                        g.free(b, ty[q])
                    gfree = tp
                    yield

        def ssd():
            nonlocal ts0, txd
            for m in range(2):
                for hf in range(2):
                    b, ps, w = g.bank()
                    for q in range(4):
                        tp = g.tr(ps[:, q * P:(q + 1) * P], xs[:, 4 * hf + q, m * P:(m + 1) * P], self.ident,
                                  txb[4 * hf + q], *w)
                    txd = g.tt(xdt[:, m, hf * 512:(hf + 1) * 512].rearrange("p (h j) -> p h j", h=8),
                               ps[:, :].rearrange("p (h j) -> p h j", h=8), bc(dt[:, m, 8 * hf:8 * hf + 8], 64),
                               ALU.mult, tp)
                    g.free(b, txd)
                    yield
            b, ps, w = g.bank()
            for q in range(4):
                tp = g.tr(ps[:, q * P:(q + 1) * P], BT[:, q, 0:P], self.ident, txb[8 + q], *w)
            tbt = g.cp(Bt, ps[:, :], tp, e="act")
            g.free(b, tbt)
            txs = g.tt(xds.rearrange("p (h j) -> p h j", h=16), xdt[:, 0, :].rearrange("p (h j) -> p h j", h=16),
                       bc(dec, 64), ALU.mult, tdec, txd)
            yield
            for hf in range(2):
                b, ps, w = g.bank()
                for q in range(2):
                    gr = 2 * hf + q
                    tp = g.mm(ps[:, q * 256:(q + 1) * 256], [(Bt[:, gr * P:(gr + 1) * P], xds[:, gr * 256:(gr + 1) * 256])],
                              tbt, txs, *w)
                ts0 = g.cp(S0[:, hf * 512:(hf + 1) * 512], ps[:, :], tp, e="act")
                g.free(b, ts0)
                yield
            work = [groups(0), groups(1)]
            while work:
                work = [w for w in work if next(w, self) is not self]
                yield

        ts0 = txd = None
        state = ssd()
        tzz = []
        for j, b, ps, tp in self.linear("z_2", 8, X, xt, T1):
            tzz.append(g.act(zb[:, j, :], ps[:, 0:T1], ACT.Silu, tp))
            g.free(b, tzz[j])
            if j % 2:
                next(state, None)
                next(state, None)
        tm = [None] * 8
        for j, b, ps, tp in self.linear("g_ssd", 8, X, xt, T1):
            tm[j] = g.act(merged[:, j, :], ps[:, 0:T1], ACT.Sigmoid, tp)
            g.free(b, tm[j])
            if j % 2:
                next(state, None)
                next(state, None)
        for _ in state:
            pass
        for j in range(8):
            ty[j] = g.tt(yss[:, j, 0:T1], yss[:, j, 0:T1], zb[:, j, :], ALU.mult, tzz[j], ty[j])
            tq = self.squares(yss, ty, j, "act")
            if j == 0:
                b, ps, w = g.bank()
            for m in range(2):
                at = 2 * (j // 2) + m
                tp = g.mm(ps[:, at:at + 1], [(self.sq[:, j, m * P:(m + 1) * P], self.ones[:, 0:1])], tq, *w,
                          first=j == 0 and m == 0, final=j == 7, inc=j == 7 and m == 1, loose=True)
        nr = self.small[:, 304:312]
        t = g.ts(nr, ps[:, 0:8], 1.0 / 256, 1e-6, ALU.mult, ALU.add, tp)
        g.free(b, t)
        t = g.tt(nr, nr, self.c("half").broadcast_to([P, 8]), ALU.pow, t, e="pool")
        for gr in range(4):
            b, ps, w = g.bank()
            for m in range(2):
                at = 2 * gr + m
                tp = g.mm(ps[:, m * P:(m + 1) * P], [(nr[:, at:at + 1].broadcast_to([P, P]), self.ident)], t, *w)
            for q in (2 * gr, 2 * gr + 1):
                t2 = g.stt(yss[:, q, 0:T1], yss[:, q, 0:T1], self.col("ssd_norm_w_2", q), ps[:, 0:T1], ALU.mult,
                           ALU.mult, tp)
                ty[q] = g.split(yp[0][:, q, :], yp[1][:, q, :], yss[:, q, :], t2)
            g.free(b, t2)
        yt = self.evac8(self.down("w_proj_ssd_2", yp, ty, T1, 8), T1)
        for j in range(8):
            tm[j] = g.tt(merged[:, j, :], merged[:, j, :], self.yT[:, j, 0:T1], ALU.mult, tm[j], yt[j])
        g.fence()
        buf = self.carve(2048)
        qo = self.pos[0]
        qT = buf(2048, 8, T1)
        kT = buf(2048, 8, T1)
        V = buf(2048, 2, 1024)
        qio = self.pos[0]
        qi = buf(2048, 8, T1)
        S = buf(2048, 4, 2, T1)
        PT = buf(2048, 8, 2, P)
        sc = buf(512, 2, T1)
        wk = buf(1024, 2, 2, T1)
        sel = buf(512, 2, T1)
        cT = buf(512, 2, T1)
        cR = [self.over(f"cR{i}", self.pos[0] + 512 * i, 2, T1) for i in range(2)]
        buf(1024)
        m8 = s[:, 448:464].rearrange("p (m h) -> p m h", m=2)
        tck = [None] * 2
        for j, b, ps, tp in self.linear("ckv", 2, X, xt, T1):
            tck[j] = g.cp(cT[:, j, :], ps[:, 0:T1], tp)
            g.free(b, tck[j])
        for j in range(2):
            t = g.act(self.sq[:, j, 0:T1], cT[:, j, :], ACT.Square, tck[j])
        b, ps, w = g.bank()
        tp = g.mm(ps[:, 0:T1], [(self.ones, self.sq[:, q, 0:T1]) for q in range(2)], t, *w)
        r_ = self.rstd[:, 0, 0:T1]
        t = self.rsqrt(r_, ps[:, 0:T1], tp, 1.0 / 256, 1e-6, T1, b)
        for q in range(2):
            t2 = g.stt(cT[:, q, :], cT[:, q, :], self.col("kv_norm_w_2", q), r_, ALU.mult, ALU.mult, t)
            tck[q] = g.split(cR[0][:, q, :], cR[1][:, q, :], cT[:, q, :], t2)
        tq = []
        for j, b, ps, tp in self.linear("qidx", 8, X, xt, T1):
            tq.append(g.cp(qi[:, j, :], ps[:, 0:T1], tp, e="act"))
            g.free(b, tq[j])
        def choose():
            for m in range(2):
                nk = P * (m + 1)
                for h in range(16):
                    o = 64 * (h % 2)
                    b, ps, w = g.bank()
                    tp = g.mm(ps[:, 0:nk], [(qi[o:o + 64, h // 2, m * P:(m + 1) * P], ki[o:o + 64, 0:nk])], tq[h // 2],
                              tki, *w)
                    i, v, tf = self.gettmp()
                    t = g.act(v[:, 0:nk], ps[:, 0:nk], ACT.Relu, tp, tf)
                    g.free(b, t)
                    if h == 0:
                        ta = g.ts(sc[:, m, 0:nk], v[:, 0:nk], widx[:, m, h:h + 1], None, ALU.mult, None, t)
                    else:
                        ta = g.stt(sc[:, m, 0:nk], v[:, 0:nk], widx[:, m, h:h + 1], sc[:, m, 0:nk], ALU.mult, ALU.add,
                                   t)
                    self.tmp_free[i] = ta
                    yield
                al = self.c("alibi")[:, m * 256:m * 256 + nk]
                t = g.ts(sel[:, m, 0:nk], al, -1e29, BIG, ALU.is_lt, ALU.mult)
                cur = sc[:, m, 0:nk]
                t = g.tt(cur, cur, sel[:, m, 0:nk], ALU.add, t)
                for r in range(8):
                    nx = wk[:, m, r % 2, 0:nk]
                    t = g.op("dve", lambda o=m8[:, m, :], c=cur: nc.vector.max(o, c), t)
                    t = g.op("dve", lambda o=nx, v=m8[:, m, :], c=cur: nc.vector.match_replace(o, v, c, -3e38), t)
                    cur = nx
                    yield
                t = g.ts(sel[:, m, 0:nk], cur, -2e38, BIG, ALU.is_gt, ALU.mult, t)
                tsel[m] = g.tt(sel[:, m, 0:nk], sel[:, m, 0:nk], al, ALU.add, t)

        tsel = [None, None]
        pick = choose()
        tqq, tkk = [], []
        for j, b, ps, tp in self.linear("q_2", 8, X, xt, T1):
            tqq.append(g.act(qT[:, j, :], ps[:, 0:T1], ACT.Copy, tp, scale=0.125))
            g.free(b, tqq[j])
            for _ in range(4):
                next(pick, None)
        us = [self.rowunit("w_uk", r) for r in range(2)]
        for j in range(8):
            b, ps, w = g.bank()
            c = slice(j * P, (j + 1) * P)
            for r, (i, wk_, t) in enumerate(us):
                tp = g.mm3(ps[:, 0:T1], [x[:, c] for x in wk_], [x[:, r, :] for x in cR], t, *tck, *w,
                           first=r == 0, final=r == 1, inc=r == 1)
            tkk.append(g.cp(kT[:, j, :], ps[:, 0:T1], tp, e="act"))
            g.free(b, tkk[j])
            for _ in range(2):
                next(pick, None)
        for i, _, _ in us:
            g.free_weight(i, tp)
        us = [self.rowunit("w_uv", r) for r in range(2)]
        for m in range(2):
            for h in range(2):
                b, ps, w = g.bank()
                for r, (i, wv_, t) in enumerate(us):
                    tp = g.mm3(ps[:, :], [x[:, r, m * P:(m + 1) * P] for x in cR],
                               [x[:, h * 512:(h + 1) * 512] for x in wv_], t, *w,
                               first=r == 0, final=r == 1, inc=r == 1)
                tvv = g.cp(V[:, m, h * 512:(h + 1) * 512], ps[:, :], tp, e="act")
                g.free(b, tvv)
        for i, _, _ in us:
            g.free_weight(i, tp)
        for _ in pick:
            pass
        oT = (self.over("oTh", qio, 8, T1), self.sqR)
        to = [None] * 8

        def heads(n):
            ptf, sfree = [None, None], None
            SS = S[:, n]
            for m in range(2):
                nk = P * (m + 1)
                for h0 in (4 * n, 4 * n + 2):
                    for r in range(2):
                        h = h0 + r
                        o = 64 * (h % 2)
                        b, ps, w = g.bank()
                        tp = g.mm(ps[:, 0:nk],
                                  [(qT[o:o + 64, h // 2, m * P:(m + 1) * P], kT[o:o + 64, h // 2, 0:nk])],
                                  tqq[h // 2], tkk[h // 2], *w)
                        t = g.stt(SS[:, r, 0:nk], sel[:, m, 0:nk],
                                  float(np.float32(2.0) ** np.float32(-0.5 * (h + 1))), ps[:, 0:nk], ALU.mult, ALU.add,
                                  tp, tsel[m], sfree)
                        g.free(b, t)
                    yield
                    t = yield from self.softmax(SS[:, :, 0:nk], 2, nk, P, [t], n)
                    for r in range(2):
                        h = h0 + r
                        o = 64 * (h % 2)
                        pt = PT[:, 2 * n + h % 2]
                        tx = self.turn(pt, SS[:, r, :], P, [(c * P, P) for c in range(m + 1)], [t], (ptf[h % 2],))
                        sfree = ("pe", g.n["pe"])
                        yield
                        if h % 2 == 0:
                            bo, po, wo = g.bank()
                        ptf[h % 2] = g.mm(po[o:o + 64, 0:P], [(V[:, c, h * 64:h * 64 + 64], pt[:, c, :])
                                                              for c in range(m + 1)], tvv, *tx, *wo)
                        if h % 2:
                            to[h // 2] = g.split(oT[0][:, h // 2, m * P:(m + 1) * P],
                                                 oT[1][:, h // 2, m * P:(m + 1) * P], po[:, 0:P], ptf[h % 2])
                            g.free(bo, to[h // 2])

        self.together(*[heads(n) for n in range(4)])
        yt = self.evac8(self.down("w_proj_att_2", oT, to, T1, 8), T1)
        mp = [self.over("mp" + "hl"[i], qo + 2048 * i, 8, T1) for i in range(2)]
        for j, b, ps, tp in self.linear("g_att", 8, X, xt, T1):
            i, v, tf = self.gettmp()
            t = g.act(v[:, 0:T1], ps[:, 0:T1], ACT.Sigmoid, tp, tf)
            g.free(b, t)
            t = g.tt(v[:, 0:T1], v[:, 0:T1], self.yT[:, j, 0:T1], ALU.mult, t, yt[j])
            t = g.tt(merged[:, j, :], merged[:, j, :], v[:, 0:T1], ALU.add, t)
            self.tmp_free[i] = t
            tm[j] = g.split(mp[0][:, j, :], mp[1][:, j, :], merged[:, j, :], t)
        self.layernorm(self.down("w_out_2", mp, tm, T1, 8), 2, False)

    def mem(self):
        g = self.g
        buf = self.carve(0)
        xt = self.splitx()
        mT = [self.over("mT" + "hl"[i], 2048 * i, 8, T1) for i in range(2)]
        buf(4096)
        qT = buf(2048, 8, T1)
        kT = buf(2048, 8, T1)
        V = buf(2048, 2, 1024)
        S = buf(1024, 4, T1)
        PT = buf(1024, 4, 2, P)
        i, (mm,), t = g.unit((0, SLOT, 0, P, self.d["mem_2"]))
        tm = self.turn_back(mm.rearrange("p (m c) -> p m c", m=2), [t, t], mT)
        g.free_unit(i, ("pe", g.n["pe"]))
        tk, tq = [], []
        for j, b, ps, tp in self.linear("mk", 8, mT, tm, T1):
            tk.append(g.cp(kT[:, j, :], ps[:, 0:T1], tp, e="act"))
            g.free(b, tk[j])
        banks = self.tokmajor("mv", mT, tm)
        for m in range(2):
            for h in range(2):
                b, ps, tp = banks[m][h]
                tv = g.cp(V[:, m, h * 512:(h + 1) * 512], ps[:, :], tp)
                g.free(b, tv)
        for j, b, ps, tp in self.linear("mq", 8, self.hp, xt, T1):
            tq.append(g.act(qT[:, j, :], ps[:, 0:T1], ACT.Copy, tp, scale=1.0 / 16))
            g.free(b, tq[j])
        oT = self.hp
        to = [None] * 8

        def heads(n):
            ptf, sf = [None, None], None
            for m in range(2):
                for h in (n,):
                    b, ps, w = g.bank()
                    tp = g.mm(ps[:, 0:T1],
                              [(qT[:, 2 * h + i, m * P:(m + 1) * P], kT[:, 2 * h + i, :]) for i in range(2)],
                              *tk, *tq, *w)
                    t = g.cp(S[:, h, :], ps[:, 0:T1], tp, sf)
                    g.free(b, t)
                yield
                t = yield from self.softmax(S[:, n:n + 1, :], 1, T1, P, [t], n)
                for h in (n,):
                    pt = PT[:, h]
                    tx = self.turn(pt, S[:, h, :], P, [(0, P), (P, P)], [t], (ptf[h % 2],))
                    sf = ("pe", g.n["pe"])
                    yield
                    b, ps, w = g.bank()
                    for i in range(2):
                        tp = g.mm(ps[:, i * P:(i + 1) * P],
                                  [(V[:, c, (2 * h + i) * P:(2 * h + i + 1) * P], pt[:, c, :]) for c in range(2)],
                                  tv, *tx, *w)
                    ptf[h % 2] = tp
                    t2 = g.split(oT[0][:, 2 * h:2 * h + 2, m * P:(m + 1) * P],
                                 oT[1][:, 2 * h:2 * h + 2, m * P:(m + 1) * P],
                                 ps[:, 0:256].rearrange("p (i t) -> p i t", i=2), tp)
                    g.free(b, t2)
                    to[2 * h] = to[2 * h + 1] = t2

        self.together(*[heads(n) for n in range(4)], lead=0)
        self.layernorm(self.down("w_mo", oT, to, T1, 8), 3, False)

    TILES = ((0, 0, P), (1, P, P), (2, T1, 16))

    def tokmajor3(self, name, src, toks, scr):
        g = self.g
        banks = {(m, h): g.bank() for m in range(2) for h in range(2)}
        b2, p2, w2 = g.bank()
        out = []
        for k in range(8):
            i, w, t = self.rowunit(name, k)
            for m in range(2):
                for h in range(2):
                    b, ps, wt = banks[m, h]
                    tk = g.mm3(ps[:, :], [x[:, k, m * P:(m + 1) * P] for x in src],
                               [x[:, h * 512:(h + 1) * 512] for x in w], t, toks[k], *wt,
                               first=k == 0, final=k == 7, inc=k == 7)
                    if k == 7:
                        out.append((m, h, P, b, ps, tk))
            for n in range(8):
                tk = g.mm3(p2[:, n * 16:(n + 1) * 16], [x[:, n * P:(n + 1) * P] for x in w],
                           [x[:, k, T1:T3] for x in src], *w2, first=k == 0 and n == 0, final=k == 7,
                           inc=n == 7, loose=True)
            g.free_weight(i, tk)
        t = g.cp(scr, p2[:, 0:P], tk)
        g.free(b2, t)
        for h in range(2):
            b, ps, wt = g.bank()
            for n in range(4):
                q = 4 * h + n
                tp = g.tr(ps[0:16, n * P:(n + 1) * P], scr[:, q * 16:q * 16 + 16], self.ident, t, *wt)
            out.append((2, h, 16, b, ps, tp))
        return out

    def gla(self):
        g, nc, T = self.g, self.g.nc, T3
        buf = self.carve(0)
        q, k, gk, eb, en = [buf(4 * T, 4, T) for _ in range(5)]
        v = buf(3072, 3, 1024)
        sr = buf(8 * T, 8, T)
        ke = buf(1536, 3, 512)
        S = buf(1024, 4, 256)
        att = buf(512, 4, P)
        ot = buf(1024, 4, 256)
        lr = buf(T)
        scr = buf(P)
        lo_at = self.pos[0]
        buf(8 * T)
        il, (wl, wg), tl = g.unit((0, 128, 0, P, self.d["gla_lr"]), (128, 512, 0, 16, self.d["gla_gate"]))
        ht = self.prenorm("norm_gains_3", 2)
        src = self.hp
        wl = wl.rearrange("p (k n) -> p k n", k=8)
        def decay():
            nonlocal tbe, ten, tge
            b, ps, w = g.bank()
            tp = g.mm(ps[0:16, 0:T], [(wl[:, kk, :], self.sq[:, kk, 0:T]) for kk in range(8)], tl, *ht, *w)
            t = g.cp(lr[0:16, :], ps[0:16, 0:T], tp)
            g.free(b, t)
            yield
            for j in range(4):
                b, ps, w = g.bank()
                tp = g.mm(ps[:, 0:T], [(wg[0:16, j * P:(j + 1) * P], lr[0:16, :])], t, *w)
                tg = g.ts(gk[:, j, :], ps[:, 0:T], self.col("gla_b_gate_3", j), None, ALU.add, None, tp)
                g.free(b, tg)
            g.free_unit(il, tp)
            t = g.act(eb, gk, ACT.Abs, tg)
            t = g.act(eb, eb, ACT.Exp, t, scale=-1.0)
            yield
            t = g.act(eb, eb, ACT.Ln, t, bias=1.0)
            yield
            t = g.stt(gk, gk, 0.0, eb, ALU.min, ALU.subtract, t)
            t = g.ts(gk, gk, 1.0 / 16, None, ALU.mult, None, t)
            yield
            for j in range(4):
                tb = g.op("dve", lambda j=j: nc.vector.tensor_tensor_scan(en[:, j, :], self.c("reset"), gk[:, j, :], 0.0,
                                                                          ALU.mult, ALU.add), t)
            yield
            tbe = g.act(eb, en, ACT.Exp, tb)
            bl = en[:, :, 0:T1].rearrange("p j (c t) -> p j c t", c=4)
            for j in range(4):
                g.tt(gk[:, j, 0:T1].rearrange("p (c t) -> p c t", c=4), bc(bl[:, j, :, 63], 64), bl[:, j], ALU.subtract, tb)
            t = g.tt(gk[:, :, T1:T], bc(en[:, :, T - 1], 16), en[:, :, T1:T], ALU.subtract)
            yield
            tge = g.act(gk, gk, ACT.Exp, t)
            ten = g.act(en, en, ACT.Exp, tge, t, scale=-1.0)

        tbe = ten = tge = None
        chain = decay()
        tr_ = []
        for j, b, ps, tp in self.linear("gla_r", 8, src, ht, T, fresh=True):
            tr_.append(g.act(sr[:, j, :], ps[:, 0:T], ACT.Silu, tp))
            g.free(b, tr_[j])
            next(chain, None)
        for _ in chain:
            pass
        tv = [None] * 3
        for m, h, n, b, ps, tp in self.tokmajor3("gla_v", src, ht, scr):
            tv[m] = g.cp(v[0:n, m, h * 512:(h + 1) * 512], ps[0:n, :], tp, e="act")
            g.free(b, tv[m])
        tq = []
        for j, b, ps, tp in self.linear("gla_qk", 8, src, ht, T):
            if j < 4:
                tq.append(g.stt(q[:, j, :], ps[:, 0:T], float(P ** -0.5), eb[:, j, :], ALU.mult, ALU.mult, tp, tbe))
            else:
                c = j - 4
                g.tt(k[:, c, :], ps[:, 0:T], en[:, c, :], ALU.mult, tp, ten)
                tq.append(g.tt(gk[:, c, :], gk[:, c, :], ps[:, 0:T], ALU.mult, tp, tge))
            g.free(b, tq[j])
        tke = []
        for m, c, n in self.TILES:
            b, ps, w = g.bank()
            for j in range(4):
                tp = g.tr(ps[0:n, j * P:(j + 1) * P], gk[:, j, c:c + n], self.ident, *tq, *w)
            tke.append(g.cp(ke[0:n, m, :], ps[0:n, :], tp))
            g.free(b, tke[m])
        mi = self.c("m64")[:, 128:256].bitcast(mybir.dt.uint32)
        t0 = g.op("dve", lambda: nc.vector.memset(att, 0.0))
        t0 = g.op("dve", lambda: nc.vector.memset(S, 0.0))
        mix = (self.sqR, self.over("glal", lo_at, 8, T))
        g.wait("act", [("pe", g.n["pe"])])
        tS = [t0] * 4
        s = self.small
        toks = [None] * 8

        def heads(hs):
            of = {h: None for h in hs}
            for m, c, n in (self.TILES[2], self.TILES[0], self.TILES[1]):
                for h in hs:
                    hv = slice(h * 256, (h + 1) * 256)
                    b, ps, w = g.bank()
                    tp = g.mm(ps[0:n, 0:n], [(k[:, h, c:c + n], q[:, h, c:c + n])], *tq, *w)
                    yield
                    ta = g.op("dve", lambda o=att[0:n, h, 0:n], mk=mi[0:n, 0:n], dt=ps[0:n, 0:n]:
                              nc.vector.copy_predicated(o, mk, dt), tp, t0, of[h])
                    g.free(b, ta)
                    bo, po, wo = g.bank()
                    to = g.mm(po[0:n, 0:256], [(att[0:n, h, 0:n], v[0:n, m, hv])], ta, tv[m], *wo, final=m == 2)
                    for cc in range(1 if m == 2 else 2):
                        o = 64 * cc
                        w_ = min(n, 64)
                        if m < 2:
                            to = g.mm(po[o:o + 64, 0:256], [(q[:, h, c + o:c + o + 64], S[:, h, :])], tS[h],
                                      first=False)
                        if m == 1 and cc == 1:
                            break
                        b, ps, w = g.bank()
                        tp = g.mm(ps[:, 0:256], [(ke[o:o + w_, m, h * P:(h + 1) * P], v[o:o + w_, m, hv])], tke[m], *w)
                        yield
                        tS[h] = g.stt(S[:, h, :], S[:, h, :], eb[:, h, c + o + w_ - 1:c + o + w_], ps[:, 0:256],
                                      ALU.mult, ALU.add, tp, to)
                        g.free(b, tS[h])
                    ss = s[0:n, 16 * m + h:16 * m + h + 1]
                    t = g.act(ot[0:n, h, :], po[0:n, 0:256], ACT.Square, to, of[h], accum_out=ss)
                    t = g.ts(ss, ss, 1.0 / 256, 1e-6, ALU.mult, ALU.add, t)
                    t = g.tt(ss, ss, self.c("half")[0:n, :], ALU.pow, t, e="pool")
                    yield
                    t = g.ts(ot[0:n, h, :], po[0:n, 0:256], ss, None, ALU.mult, None, t)
                    g.free(bo, t)
                    b, ps, w = g.bank()
                    for i in range(2):
                        tp = g.tr(ps[:, i * P:i * P + n], ot[0:n, h, i * P:(i + 1) * P], self.ident[0:n, 0:n], t, *w)
                    of[h] = tp
                    yield
                    for i in range(2):
                        x, v_, tf = self.gettmp()
                        t = g.stt(v_[:, 0:n], ps[:, i * P:i * P + n], self.col("gla_norm_3", i),
                                  sr[:, 2 * h + i, c:c + n], ALU.mult, ALU.mult, tp, tr_[2 * h + i], tf)
                        toks[2 * h + i] = g.split(mix[0][:, 2 * h + i, c:c + n], mix[1][:, 2 * h + i, c:c + n],
                                                  v_[:, 0:n], t)
                        self.tmp_free[x] = toks[2 * h + i]
                    g.free(b, t)

        self.together(heads((0,)), heads((1,)), heads((2,)), heads((3,)))
        self.postnorm(self.down("gla_out", mix, toks, T, 8), "norm_gains_3", 3, False)

    def rope(self, x, H, m, n, tok):
        g = self.g
        x3 = x.rearrange("p (h j) -> p h j", h=H)
        at = CSTS["rope"][0] + 16 * m
        c = bc_mid(self.cst[0:n, at:at + 8], H)
        s = bc_mid(self.cst[0:n, at + 8:at + 16], H)
        r = self.rstd.rearrange("p k t -> p (k t)")
        a, b2, d, e = [r[0:n, i * 128:i * 128 + 8 * H].rearrange("p (h j) -> p h j", h=H) for i in range(4)]
        x1, x2 = x3[:, :, 0:8], x3[:, :, 8:16]
        g.tt(a, x1, c, ALU.mult, tok)
        g.tt(b2, x2, s, ALU.mult)
        g.tt(d, x2, c, ALU.mult)
        g.tt(e, x1, s, ALU.mult)
        g.tt(x1, a, b2, ALU.subtract)
        return g.tt(x2, d, e, ALU.add)

    def shared(self):
        g, T = self.g, T3
        buf = self.carve(self.NA - 1856)
        kD, V = self.kD3, self.V3 = buf(4 * T, 4, T), buf(768, 3, 256)
        kt = self.A[:, 0:768].rearrange("p (m c) -> p m c", m=3)
        ht = self.prenorm("kv_norm_3")
        fm = self.A[:, 768:768 + 4 * T].rearrange("p (j t) -> p j t", j=4)
        tf = []
        for j, b, ps, tp in self.linear("w_kv", 4, self.hp, ht, T, fresh=True):
            tf.append(g.cp(fm[:, j, :], ps[:, 0:T], tp, e="act"))
            g.free(b, tf[j])
        for u in range(2):
            for m, c, n in self.TILES:
                b, ps, wt = g.bank()
                for j in range(2):
                    tp = g.tr(ps[0:n, j * P:(j + 1) * P], fm[:, 2 * u + j, c:c + n], self.ident, tf[2 * u + j], *wt)
                tk = g.cp((kt, V)[u][0:n, m, :], ps[0:n, 0:256], tp)
                g.free(b, tk)
                if u == 0:
                    tk = self.rope(kt[0:n, m, :], 4, m, n, tk)
                    b, ps, wt = g.bank()
                    for h in range(4):
                        tp2 = g.tr(ps[0:64, h * P:h * P + n], kt[0:n, m, h * 64:h * 64 + 64], self.ident[0:n, 0:n],
                                   tk, *wt)
                    p4 = ps[0:64, :].rearrange("p (h t) -> p h t", h=4)[:, :, 0:n]
                    g.cp(kD[0:64, :, c:c + n], p4, tp2)
                    tk = g.cp(kD[64:128, :, c:c + n], p4, tp2)
                    g.free(b, tk)
        self.tkv = tk
        g.fence()

    def swa(self):
        g, T = self.g, T3
        buf = self.carve(0, self.NA - 1856)
        qt = buf(3072, 3, 1024)
        qT = buf(8 * T, 8, T)
        S = buf(8 * T, 4, 2, T)
        PT = buf(3072, 8, 3, P)
        scr = buf(P)
        lo_at = self.pos[0]
        buf(8 * T)
        kD, V = self.kD3, self.V3
        ht = self.prenorm("norm_gains_3", 8)
        tm = [None] * 3
        for m, h, n, b, ps, tp in self.tokmajor3("swa_q", self.hp, ht, scr):
            tm[m] = g.act(qt[0:n, m, h * 512:(h + 1) * 512], ps[0:n, :], ACT.Copy, tp, scale=0.125)
            g.free(b, tm[m])
        tq = []
        for m, c, n in self.TILES:
            t = self.rope(qt[0:n, m, :], 16, m, n, tm[m])
            for hf in range(2):
                b, ps, w = g.bank()
                for i in range(4):
                    tp = g.tr(ps[:, i * P:i * P + n], qt[0:n, m, (4 * hf + i) * P:(4 * hf + i + 1) * P],
                              self.ident[0:n, 0:n], t, *w)
                tx = g.cp(qT[:, 4 * hf:4 * hf + 4, c:c + n],
                          ps[:, :].rearrange("p (h t) -> p h t", h=4)[:, :, 0:n], tp)
                g.free(b, tx)
            tq.append(tx)
        mix = (self.sqR, self.over("swal", lo_at, 8, T))
        g.wait("act", [("pe", g.n["pe"])])
        to = [None] * 8
        sinks = self.rows[:, ROWS["swa_sinks_3"][0]:ROWS["swa_sinks_3"][0] + 16]

        def heads(u):
            ptf, sfree = [None, None], None
            for m, c, n in self.TILES:
                keys = ((0, 2), (0, 1, 2), (2,))[m]
                SS = S[0:n, u]
                for h0 in (4 * u, 4 * u + 2):
                    kv = u
                    for r in range(2):
                        h = h0 + r
                        o = 64 * (h % 2)
                        b, ps, w = g.bank()
                        tp = g.mm(ps[0:n, 0:T], [(qT[o:o + 64, h // 2, c:c + n], kD[o:o + 64, kv, :])], tq[m], self.tkv,
                                  *w)
                        at = CSTS["swa"][0] + m * T
                        t = g.tt(SS[:, r, :], ps[0:n, 0:T], self.cst[0:n, at:at + T], ALU.add, tp, sfree)
                        g.free(b, t)
                    yield
                    t = yield from self.softmax(SS, 2, T, n, [t], u, sink=sinks[0:n, h0:h0 + 2])
                    for r in range(2):
                        h = h0 + r
                        o = 64 * (h % 2)
                        pt = PT[:, 2 * u + h % 2]
                        tx = self.turn(pt, SS[:, r, :], n, [(kk * P, (P, P, 16)[kk]) for kk in keys], [t], (ptf[h % 2],))
                        sfree = ("pe", g.n["pe"])
                        yield
                        if h % 2 == 0:
                            bo, po, wo = g.bank()
                        pairs = [(V[0:(P, P, 16)[kk], kk, kv * 64:kv * 64 + 64], pt[0:(P, P, 16)[kk], i, 0:n])
                                 for i, kk in enumerate(keys)]
                        ptf[h % 2] = g.mm(po[o:o + 64, 0:n], pairs, *tx, *wo)
                        if h % 2:
                            to[h // 2] = g.split(mix[0][:, h // 2, c:c + n], mix[1][:, h // 2, c:c + n], po[:, 0:n],
                                                 ptf[h % 2])
                            g.free(bo, to[h // 2])

        self.together(*[heads(u) for u in range(4)])
        self.postnorm(self.down("swa_out", mix, to, T, 8), "norm_gains_3", 9, False)


def colunits(w):
    k, n = w.shape
    return w.reshape(k // P, P, n // P, P).transpose(2, 1, 0, 3).reshape(n // P, P, k)


def rowunits(w):
    k, n = w.shape
    return w.reshape(k // P, P, n)


def layout(v):
    d = {"x": v["x"][0].reshape(2, P, D).transpose(1, 0, 2).reshape(P, SLOT), "cst": constants(), "meta_tokens_3": v["meta_tokens_3"]}
    cols = np.zeros((P, NCOL + P), np.float32)
    cols[:, NCOL:] = np.concatenate([v["l0_cmp_w2_k"], v["l0_cmp_w2_v"]], 1)
    for name, (at, n) in COLS.items():
        a = np.repeat(v["d_skip_2"].reshape(-1), 64) if name == "d_skip_2c" else v[name]
        cols[:, at:at + n] = np.asarray(a).reshape(n, P).T
    d["cols"] = cols
    d["rows"] = np.concatenate([np.asarray(v[n]).reshape(1, 16) for n in ROWS], 1)
    for f in FFNS:
        d[f + "_w_gate"] = colunits(v[f + "_w_gate"])
        d[f + "_w_up"] = colunits(v[f + "_w_up"])
        d[f + "_w_down"] = rowunits(v[f + "_w_down"])
    for f in ("ffn1", "ffn2"):
        w = v[f + "_w_in_2"][0]
        d[f + "_w_gate_2"] = colunits(w[:, :FF])
        d[f + "_w_up_2"] = colunits(w[:, FF:])
        d[f + "_w_out_2"] = rowunits(v[f + "_w_out_2"][0])
    for a in range(2):
        for b in range(2):
            w = v["w_ffn_in_3"][a, b]
            d[f"g3_{a}{b}"] = colunits(w[:, :FF])
            d[f"u3_{a}{b}"] = colunits(w[:, FF:])
            d[f"d3_{a}{b}"] = rowunits(v["w_ffn_out_3"][a, b])
    w = v["l0_w_in"]
    c = np.cumsum([0, 512, 24, 128, 128, 128, 128, 128, 128, 512, 512, 512])
    part = lambda i: w[:, c[i]:c[i + 1]]
    d["nsa_in"] = colunits(np.concatenate([part(i) for i in (0, 2, 3, 4, 6, 8, 9, 10)], 1))
    d["nsa_v"] = colunits(np.concatenate([part(5), part(7)], 1))
    d["nsa_g"] = part(1).reshape(8, P, 24).transpose(1, 0, 2).reshape(P, 192)
    for s in "kv":
        d["cmp_w1_" + s] = v["l0_cmp_w1_" + s].reshape(16, P, P).transpose(1, 0, 2).reshape(P, SLOT)
    d["nsa_out"] = rowunits(v["l0_w_out"])
    d["lora1"] = np.concatenate([v["l1_w_dec1"], v["l1_w_a1"], v["l1_w_g1"]], 1).reshape(8, P, 256).transpose(
        1, 0, 2).reshape(P, SLOT)
    d["lora2"] = np.concatenate([np.concatenate([v["l1_w_dec2"], v["l1_w_a2"]], 1),
                                 np.concatenate([v["l1_w0"], v["l1_a0"]])[None]], 0)
    d["l1_w_g2"] = v["l1_w_g2"]
    for n in ("l1_w_r", "l1_w_k", "l1_w_v", "l1_w_o"):
        d[n] = rowunits(v[n])
    for n in ("l1_k_k", "l1_k_a", "l1_r_k", "l1_lnx_g", "l1_lnx_b"):
        d[n] = v[n].reshape(1, D)
    w = v["w_in_2"][0]
    c = np.cumsum([0, 1024, 1024, 1024, 2048, 16, 1024, 256, 1024, 64, 16])
    part = lambda i: w[:, c[i]:c[i + 1]]
    for i, n in ((0, "g_ssd"), (1, "g_att"), (2, "z_2"), (3, "xbc"), (5, "q_2"), (6, "ckv"), (7, "qidx")):
        d[n] = colunits(part(i))
    d["tokw"] = np.concatenate([part(4), part(9)], 1).reshape(8, P, 32).transpose(1, 0, 2).reshape(P, 256)
    d["kidx"] = part(8).reshape(8, P, 64).transpose(1, 0, 2).reshape(P, 512)
    d["w_uk"] = v["w_uk_2"][0].transpose(2, 0, 1).reshape(2, P, D)
    d["w_uv"] = v["w_uv_2"][0].transpose(1, 0, 2).reshape(2, P, D)
    for n in ("w_proj_ssd_2", "w_proj_att_2", "w_out_2"):
        d[n] = rowunits(v[n][0])
    d["mem_2"] = v["mem_2"][0].reshape(2, P, D).transpose(1, 0, 2).reshape(P, SLOT)
    d["mq"] = colunits(v["w_mq_2"][0])
    d["mk"] = colunits(v["w_mkv_2"][0][:, :D])
    d["mv"] = rowunits(v["w_mkv_2"][0][:, D:])
    d["w_mo"] = rowunits(v["w_mo_2"][0])
    w = v["gla_w_in_3"][0]
    d["gla_qk"] = colunits(w[:, :1024])
    d["gla_v"] = rowunits(w[:, 1024:2048])
    d["gla_r"] = colunits(w[:, 2048:3072])
    d["gla_lr"] = w[:, 3072:].reshape(8, P, 16).transpose(1, 0, 2).reshape(P, 128)
    d["gla_gate"] = v["gla_w_gate_3"][0]
    d["gla_out"] = rowunits(v["gla_w_out_3"][0])
    d["w_kv"] = colunits(v["w_kv_3"])
    d["swa_q"] = rowunits(v["swa_w_q_3"][0])
    d["swa_out"] = rowunits(v["swa_w_out_3"][0])
    return {n: np.ascontiguousarray(a) for n, a in d.items()}


def program(nc, arrays, stages):
    d = {n: nc.dram_tensor("in_" + n, a.shape, F32, kind="ExternalInput").ap() for n, a in arrays.items()}
    out = nc.dram_tensor("out_0", (T1, D), F32, kind="ExternalOutput").ap()
    with ExitStack() as ctx:
        Model(nc, ctx, d, out, stages)


def kernel(**inputs):
    import concourse.bacc as _bacc
    from concourse.bass_utils import run_bass_kernel_spmd as _run

    arrays = layout({n: np.asarray(a) for n, a in inputs.items()})
    nc = _bacc.Bacc("TRN2", target_bir_lowering=False, num_devices=1)
    program(nc, arrays, range(18))
    r = _run(nc, [{"in_" + n: a for n, a in arrays.items()}], core_ids=[0])
    return r.results[0]["out_0"].reshape(1, T1, D)
```
